# Optimizing a Trainium2 kernel written in Bass

```python
import math
import jax, jax.numpy as jnp
from jax import lax
import numpy as np

D_MODEL = 1024
BATCH = 1
SEQ = 1024
DEPTH = 1

GRID_W = 64
CTX_LEN = 256
N_BRANCH = 4
D_A = D_MODEL // 2
SC_K = 3
D_NA = D_MODEL // 2
NA_HEADS = 8
NA_HD = D_NA // NA_HEADS
NA_KH = 8
NA_KW = 16
D_HY = D_MODEL // 2
HY_EMB = 33
HY_FH = 64
HY_SHIFT = 0.05
HY_FAST = 0.3
HY_SLOW = 1.5
HY_TARGET = 1e-2
D_CF = D_MODEL // 2
CF_K = 31
D_FF = ((8 * D_MODEL + 3 * 256 - 1) // (3 * 256)) * 256
EPS = 1e-6
OFF_A = 0
OFF_Q = OFF_A + 3 * D_A
OFF_K = OFF_Q + D_NA
OFF_V = OFF_K + D_NA
OFF_HY = OFF_V + D_NA
OFF_CF = OFF_HY + 3 * D_HY
OFF_G = OFF_CF + 2 * D_CF
N_IN = OFF_G + N_BRANCH * D_MODEL

kernel_name = 'hybrid_conv_na_hyena_conformer_dit_block'

def rmsnorm(x, g):
    xf = x.astype(jnp.float32)
    y = xf * lax.rsqrt(jnp.mean(xf * xf, axis=-1, keepdims=True) + EPS)
    return y.astype(x.dtype) * g

def layernorm(x, g, b):
    xf = x.astype(jnp.float32)
    mu = jnp.mean(xf, axis=-1, keepdims=True)
    var = jnp.mean(jnp.square(xf - mu), axis=-1, keepdims=True)
    return ((xf - mu) * lax.rsqrt(var + EPS)).astype(x.dtype) * g + b

def modulate(h, shift, scale):
    return h * (1 + scale) + shift

def dwconv(x, w):
    k = w.shape[0]
    return lax.conv_general_dilated(x, w[:, None, :].astype(x.dtype), (1,), [((k - 1) // 2, k // 2)],
                                    dimension_numbers=('NWC', 'WIO', 'NWC'), feature_group_count=x.shape[-1])

def split_heads(t):
    return t.reshape(t.shape[:-1] + (NA_HEADS, NA_HD))

def na_context(qc, kc, vc):
    s = jnp.einsum('bqhd,bkhd->bhqk', qc, kc) * (NA_HD ** -0.5)
    p = jax.nn.softmax(s.astype(jnp.float32), axis=-1).astype(vc.dtype)
    return jnp.einsum('bhqk,bkhd->bqhd', p, vc)

def na_latent(q, k, v, kc, vc, rpb):
    b, s = q.shape[0], q.shape[1]
    rows = s // GRID_W
    kh = min(NA_KH, rows)
    qg = q.reshape(b, rows, GRID_W, NA_HEADS, NA_HD)
    kg = k.reshape(b, rows, GRID_W, NA_HEADS, NA_HD)
    vg = v.reshape(b, rows, GRID_W, NA_HEADS, NA_HD)
    cols = jnp.arange(GRID_W)
    cidx = jnp.clip(cols - NA_KW // 2, 0, GRID_W - NA_KW)[:, None] + jnp.arange(NA_KW)[None, :]
    dc = cidx - cols[:, None] + NA_KW - 1
    scale = NA_HD ** -0.5
    n_loc = kh * NA_KW

    def row_block(r):
        rs = jnp.clip(r - kh // 2, 0, rows - kh)
        dr = rs + jnp.arange(kh) - r + NA_KH - 1
        bias = rpb[:, dr][:, :, dc].transpose(0, 2, 1, 3)
        q_r = lax.dynamic_index_in_dim(qg, r, axis=1, keepdims=False)
        k_win = lax.dynamic_slice_in_dim(kg, rs, kh, axis=1)[:, :, cidx]
        v_win = lax.dynamic_slice_in_dim(vg, rs, kh, axis=1)[:, :, cidx]
        s_loc = jnp.einsum('bqhd,biqjhd->bhqij', q_r, k_win) * scale + bias[None]
        s_ctx = jnp.einsum('bqhd,bchd->bhqc', q_r, kc) * scale
        s_all = jnp.concatenate([s_loc.reshape(b, NA_HEADS, GRID_W, n_loc), s_ctx], axis=-1)
        p = jax.nn.softmax(s_all.astype(jnp.float32), axis=-1).astype(v.dtype)
        p_loc = p[..., :n_loc].reshape(b, NA_HEADS, GRID_W, kh, NA_KW)
        p_ctx = p[..., n_loc:]
        return (jnp.einsum('bhqij,biqjhd->bqhd', p_loc, v_win)
                + jnp.einsum('bhqc,bchd->bqhd', p_ctx, vc))

    out = lax.map(row_block, jnp.arange(rows))
    return out.transpose(1, 0, 2, 3, 4).reshape(b, s, D_NA)

def hyena_filter(length, w1, b1, w2, b2, w3, b3, w4, freq):
    f32 = jnp.float32
    t = jnp.linspace(0.0, 1.0, length, dtype=f32)[:, None]
    bands = (HY_EMB - 1) // 2
    w = 2.0 * math.pi * jnp.arange(length, dtype=f32)[:, None] / length
    f = jnp.linspace(1e-4, bands - 1, bands, dtype=f32)[None, :]
    z = jnp.concatenate([t, jnp.cos(f * w), -jnp.sin(f * w)], axis=-1)
    fr = freq.astype(f32)
    h = jnp.sin(fr * (z @ w1.astype(f32) + b1.astype(f32)))
    h = jnp.sin(fr * (h @ w2.astype(f32) + b2.astype(f32)))
    h = jnp.sin(fr * (h @ w3.astype(f32) + b3.astype(f32)))
    h = h @ w4.astype(f32)
    deltas = jnp.abs(jnp.linspace(math.log(HY_TARGET) / HY_SLOW, math.log(HY_TARGET) / HY_FAST, D_HY, dtype=f32))
    window = jnp.exp(-t * jnp.tile(deltas, 2)[None, :]) + HY_SHIFT
    return h * window

def bidir_fft_conv(u, filt):
    n_tok, ch = u.shape[1], u.shape[2]
    k_f, k_b = filt[:, :ch], filt[:, ch:]
    kern = jnp.concatenate([k_f, jnp.zeros((1, ch), filt.dtype), k_b[:0:-1]], axis=0)
    uf = jnp.fft.rfft(u.astype(jnp.float32), n=2 * n_tok, axis=1)
    kf = jnp.fft.rfft(kern, n=2 * n_tok, axis=0)
    y = jnp.fft.irfft(uf * kf[None], n=2 * n_tok, axis=1)[:, :n_tok]
    return y.astype(u.dtype)

def shortconv_branch(pa, conv_a, w_a_out):
    xin, bg, cg = jnp.split(pa, 3, axis=-1)
    return (bg * dwconv(cg * xin, conv_a)) @ w_a_out

def hyena_branch(ph, conv_h, filt, hy_skip, w_h_out):
    x0, x1, v = jnp.split(dwconv(ph, conv_h), 3, axis=-1)
    u = x1 * v
    return (x0 * (bidir_fft_conv(u, filt) + u * hy_skip)) @ w_h_out

def conformer_branch(pd, conv_d, conv_d_b, ln_g, ln_b, w_d_out):
    a, g = jnp.split(pd, 2, axis=-1)
    u = dwconv(a * jax.nn.sigmoid(g), conv_d) + conv_d_b
    return jax.nn.silu(layernorm(u, ln_g, ln_b)) @ w_d_out

def mixer(proj, attn, filt, conv_a, w_a_out, w_na_out, conv_h, hy_skip, w_h_out,
          conv_d, conv_d_b, ln_g, ln_b, w_d_out, w_o):
    y_a = shortconv_branch(proj[..., OFF_A:OFF_Q], conv_a, w_a_out)
    y_na = attn @ w_na_out
    y_hy = hyena_branch(proj[..., OFF_HY:OFF_CF], conv_h, filt, hy_skip, w_h_out)
    y_cf = conformer_branch(proj[..., OFF_CF:OFF_G], conv_d, conv_d_b, ln_g, ln_b, w_d_out)
    g = jax.nn.sigmoid(proj[..., OFF_G:])
    merged = (g[..., 0 * D_MODEL:1 * D_MODEL] * y_a + g[..., 1 * D_MODEL:2 * D_MODEL] * y_na
              + g[..., 2 * D_MODEL:3 * D_MODEL] * y_hy + g[..., 3 * D_MODEL:4 * D_MODEL] * y_cf)
    return merged @ w_o

def swiglu(h, w_ffn_in, w_ffn_out):
    a, up = jnp.split(h @ w_ffn_in, 2, axis=-1)
    return (jax.nn.silu(a) * up) @ w_ffn_out

def setup_inputs(seed: int = 0) -> dict:
    key = jax.random.key(seed)
    k = jax.random.split(key, 34)
    L = DEPTH

    def nrm(i, shape, scale):
        return jax.random.normal(k[i], shape, jnp.float32) * scale

    return {
        'x': nrm(0, (BATCH, SEQ, D_MODEL), 1.0),
        'c': nrm(1, (BATCH, D_MODEL), 1.0),
        'ctx': nrm(2, (BATCH, CTX_LEN, D_MODEL), 1.0),
        'c_ctx': nrm(3, (D_MODEL,), 1.0),
        'w_mod': nrm(4, (L, D_MODEL, 6 * D_MODEL), 0.5 * D_MODEL ** -0.5),
        'b_mod': nrm(5, (L, 6 * D_MODEL), 0.02),
        'g_norm1': 1.0 + nrm(6, (L, D_MODEL), 0.05),
        'g_norm2': 1.0 + nrm(7, (L, D_MODEL), 0.05),
        'w_in': nrm(8, (L, D_MODEL, N_IN), D_MODEL ** -0.5),
        'conv_a': nrm(9, (L, SC_K, D_A), SC_K ** -0.5),
        'w_a_out': nrm(10, (L, D_A, D_MODEL), D_A ** -0.5),
        'q_gain': 1.0 + nrm(11, (L, NA_HD), 0.05),
        'k_gain': 1.0 + nrm(12, (L, NA_HD), 0.05),
        'rpb': nrm(13, (L, NA_HEADS, 2 * NA_KH - 1, 2 * NA_KW - 1), 0.2),
        'w_na_out': nrm(14, (L, D_NA, D_MODEL), D_NA ** -0.5),
        'conv_h': nrm(15, (L, SC_K, 3 * D_HY), SC_K ** -0.5),
        'filt_w1': nrm(16, (L, HY_EMB, HY_FH), HY_EMB ** -0.5),
        'filt_b1': nrm(17, (L, HY_FH), 0.1),
        'filt_w2': nrm(18, (L, HY_FH, HY_FH), HY_FH ** -0.5),
        'filt_b2': nrm(19, (L, HY_FH), 0.1),
        'filt_w3': nrm(20, (L, HY_FH, HY_FH), HY_FH ** -0.5),
        'filt_b3': nrm(21, (L, HY_FH), 0.1),
        'filt_w4': nrm(22, (L, HY_FH, 2 * D_HY), 0.1 * HY_FH ** -0.5),
        'filt_freq': 1.0 + nrm(23, (L, HY_FH), 0.05),
        'hy_skip': nrm(24, (L, D_HY), 0.5),
        'w_h_out': nrm(25, (L, D_HY, D_MODEL), D_HY ** -0.5),
        'conv_d': nrm(26, (L, CF_K, D_CF), CF_K ** -0.5),
        'conv_d_b': nrm(27, (L, D_CF), 0.02),
        'ln_g': 1.0 + nrm(28, (L, D_CF), 0.05),
        'ln_b': nrm(29, (L, D_CF), 0.02),
        'w_d_out': nrm(30, (L, D_CF, D_MODEL), D_CF ** -0.5),
        'w_o': nrm(31, (L, D_MODEL, D_MODEL), D_MODEL ** -0.5),
        'w_ffn_in': nrm(32, (L, D_MODEL, 2 * D_FF), D_MODEL ** -0.5),
        'w_ffn_out': nrm(33, (L, D_FF, D_MODEL), D_FF ** -0.5),
    }

def reference(x, c, ctx, c_ctx, w_mod, b_mod, g_norm1, g_norm2, w_in, conv_a, w_a_out, q_gain, k_gain, rpb,
              w_na_out, conv_h, filt_w1, filt_b1, filt_w2, filt_b2, filt_w3, filt_b3, filt_w4, filt_freq,
              hy_skip, w_h_out, conv_d, conv_d_b, ln_g, ln_b, w_d_out, w_o, w_ffn_in, w_ffn_out):
    for l in range(DEPTH):
        last = l == DEPTH - 1

        def run_mixer(proj, attn, filt):
            return mixer(proj, attn, filt, conv_a[l], w_a_out[l], w_na_out[l], conv_h[l], hy_skip[l], w_h_out[l],
                         conv_d[l], conv_d_b[l], ln_g[l], ln_b[l], w_d_out[l], w_o[l])

        def make_filt(n_tok):
            return hyena_filter(n_tok, filt_w1[l], filt_b1[l], filt_w2[l], filt_b2[l], filt_w3[l], filt_b3[l],
                                filt_w4[l], filt_freq[l])

        mx = (jax.nn.silu(c) @ w_mod[l] + b_mod[l])[:, None, :]
        sh1, sc1, g1, sh2, sc2, g2 = jnp.split(mx, 6, axis=-1)
        mc = jax.nn.silu(c_ctx) @ w_mod[l] + b_mod[l]
        csh1, csc1, cg1, csh2, csc2, cg2 = jnp.split(mc, 6, axis=-1)

        hx = modulate(rmsnorm(x, g_norm1[l]), sh1, sc1)
        hc = modulate(rmsnorm(ctx, g_norm1[l]), csh1, csc1)
        px = hx @ w_in[l]
        q = rmsnorm(split_heads(px[..., OFF_Q:OFF_K]), q_gain[l])
        k = rmsnorm(split_heads(px[..., OFF_K:OFF_V]), k_gain[l])
        v = split_heads(px[..., OFF_V:OFF_HY])
        if last:
            kv_c = hc @ w_in[l][:, OFF_K:OFF_HY]
            kc_raw, vc_raw = kv_c[..., :D_NA], kv_c[..., D_NA:]
        else:
            pc = hc @ w_in[l]
            kc_raw, vc_raw = pc[..., OFF_K:OFF_V], pc[..., OFF_V:OFF_HY]
        kc = rmsnorm(split_heads(kc_raw), k_gain[l])
        vc = split_heads(vc_raw)

        attn_x = na_latent(q, k, v, kc, vc, rpb[l])
        x_mix = run_mixer(px, attn_x, make_filt(x.shape[1]))

        if not last:
            qc = rmsnorm(split_heads(pc[..., OFF_Q:OFF_K]), q_gain[l])
            attn_c = na_context(qc, kc, vc).reshape(ctx.shape[0], ctx.shape[1], D_NA)
            c_mix = run_mixer(pc, attn_c, make_filt(ctx.shape[1]))
            ctx = ctx + cg1 * c_mix
            ctx = ctx + cg2 * swiglu(modulate(rmsnorm(ctx, g_norm2[l]), csh2, csc2), w_ffn_in[l], w_ffn_out[l])

        x = x + g1 * x_mix
        x = x + g2 * swiglu(modulate(rmsnorm(x, g_norm2[l]), sh2, sc2), w_ffn_in[l], w_ffn_out[l])
    return x


_drawn_inputs = setup_inputs


def setup_inputs(seed=0):
    import zlib

    import numpy as np

    out = dict(_drawn_inputs(seed))
    spreads = {}
    factors = {'ctx': 4.807,
     'g_norm2': 3.706,
     'q_gain': 8.0,
     'k_gain': 8.0,
     'rpb': 25.032,
     'filt_freq': 7.241,
     'conv_d_b': 8.0,
     'ln_g': 8.0,
     'ln_b': 23.1}
    for name, (base, spread) in spreads.items():
        noise = np.random.default_rng([zlib.crc32(name.encode()), seed]).standard_normal(out[name].shape)
        drawn = base * np.exp(spread * noise) if base else spread * noise
        out[name] = __import__('jax').numpy.asarray(drawn.astype(out[name].dtype))
    for name, factor in factors.items():
        out[name] = (out[name] * factor).astype(out[name].dtype)
    return out
```

```python
from contextlib import ExitStack, contextmanager

import numpy as np
import concourse.bass as bass
from concourse import mybir

F32 = mybir.dt.float32
F32R = mybir.dt.float32r
ALU = mybir.AluOpType
ACT = mybir.ActivationFunctionType

P = 128
T = 1024
C = 256
TC = T + C
D = 1024
KT = D // P
DB = 512
NB = DB // P
HALF = 512
HD = 64
HEADS = 8
GRID = 64
ROWS = T // GRID
WIN_H, WIN_W = 8, 16
NROW = 10
LOC = NROW * GRID
KEYS = LOC + C
XR = 18
EPS = 1e-6
NEG = -1e30
FF = 2816
FFT = FF // P
FGROUPS = (8, 7, 7)
CFK = 31
NBR = 4
CH = 8 * P

CK_KDFT = 0
CK_IN = CK_KDFT + 2 * KT
N_CF, N_HY, N_A, N_QKV, N_G = 2 * NB, 3 * NB, 3 * NB, 3 * NB, NBR * KT
S_HY = N_CF
S_A = S_HY + N_HY
S_QKV = S_A + N_A
S_G = S_QKV + N_QKV
N_STRIP = S_G + N_G
CK_UDFT = CK_IN + N_STRIP
CK_IDFT = CK_UDFT + 2 * KT
CK_Y = CK_IDFT + 2 * KT
CK_WO = CK_Y + NBR * NB
CK_FFN = CK_WO + KT
N_CHUNK = CK_FFN + 2 * FFT + KT * len(FGROUPS)
assert N_CHUNK % 4 == 0 and CK_IN % 4 == 0

GATE_OF = (0, 3, 1, 2)
Z_A, Z_CF, Z_NA, Z_HY = range(4)

VEC = {}
_at = 0
for _name, _n in (("g1", KT), ("g2", KT), ("qg", 1), ("kg", 1), ("ca", 3 * NB), ("chy", 9 * NB),
                  ("skip", NB), ("cd", CFK * NB), ("cdb", NB), ("lng", NB), ("lnb", NB),
                  ("bmod", 6 * KT), ("c", 2 * KT), ("fb", 3), ("freq", 1), ("eps", 1)):
    VEC[_name] = _at
    _at += _n
NVEC = _at

M_ID, M_ONE, M_HEAD, M_ALT = range(4)


def window_start(rp):
    return min(max(2 * rp - WIN_H // 2, 0), ROWS - NROW)


MASKS = (0, 1, 2, ROWS // 2 - 2, ROWS // 2 - 1)


class Steps:

    def __init__(self, eng, sem):
        self.eng, self.sem, self.n = eng, sem, 0

    def done(self, ins):
        self.n += 1
        ins.then_inc(self.sem, 1)
        self.eng.wait_ge(self.sem, self.n)


def layer_program(nc, w, wmod, xc, vec, mats, filt, win, gat, masks, out):
    kspec = nc.dram_tensor("kspec", (KT, P, 2, DB), F32, kind="Internal").ap()
    x0_d = nc.dram_tensor("x0_d", (NB, P, T), F32, kind="Internal").ap()
    u_d = nc.dram_tensor("u_d", (NB, P, T), F32, kind="Internal").ap()
    qkv_d = nc.dram_tensor("qkv_d", (3 * NB, P, T), F32, kind="Internal").ap()
    kvc_d = nc.dram_tensor("kvc_d", (2 * NB, P, C), F32, kind="Internal").ap()
    gate_d = nc.dram_tensor("gate_d", (NBR * KT, P, T), F32, kind="Internal").ap()
    z_d = nc.dram_tensor("z_d", (NBR, NB, P, T), F32, kind="Internal").ap()

    with ExitStack() as ctx:
        def sb(name, shape, dt=F32):
            return ctx.enter_context(nc.sbuf_tensor(name, shape, dt))

        def sem(name):
            return ctx.enter_context(nc.semaphore(name))

        v_sb = sb("v_sb", [P, NVEC])
        m_sb = sb("m_sb", [P, 4, P])
        altr = sb("altr", [P, P], F32R)
        cs = sb("cs", [P, 2 * KT])
        csg = sb("csg", [P, 2 * KT])
        mod = sb("mod", [P, 6 * KT, 2])
        aff = sb("aff", [P, KT, 2])
        aff2 = sb("aff2", [P, KT])
        qg8 = sb("qg8", [P, 1])
        gate0 = sb("gate0", [P, 2])
        st_nm = sb("st_nm", [P, 2])
        st_m = sb("st_m", [P, 2])
        st_l = sb("st_l", [P, 2])
        st_r = sb("st_r", [P, 2])
        ident = m_sb[:, M_ID, :]
        ones = m_sb[:, M_ONE, :]
        heads = m_sb[:, M_HEAD, :]

        floor = (nc.sbuf_base + 63) // 64 * 64
        room = nc.sbuf_usable_end - floor
        KB = 1024

        def at(name, kb, shape, dt=F32):
            size = int(np.prod(shape[1:])) * 4
            off = int(kb * KB)
            assert off + size <= room, (name, off + size, room)
            return nc.alloc_sbuf_tensor_at(name, shape, dt, offset=floor + off)

        raw = at("raw", 0, [P, 4, CH])
        whi = at("whi", 16, [P, 2, CH], F32R)
        wlo = at("wlo", 24, [P, 2, CH], F32R)
        h_hi = at("h_hi", 32, [P, KT, T], F32R)
        h_lo = at("h_lo", 64, [P, KT, T], F32R)
        c_hi = at("c_hi", 96, [P, KT, C], F32R)
        c_lo = at("c_lo", 104, [P, KT, C], F32R)
        mraw = at("mraw", 112, [P, 2, CH])
        e_hi = at("e_hi", 120, [P, KT, DB], F32R)
        e_lo = at("e_lo", 136, [P, KT, DB], F32R)
        o_hi = at("o_hi", 152, [P, KT, DB], F32R)
        o_lo = at("o_lo", 168, [P, KT, DB], F32R)
        xs = at("xs", 184, [P, 2, TC])
        rstd = at("rstd", 194, [P, TC])
        ksp = at("ksp", 199, [P, 2, DB])
        f_sb = at("f_sb", 32, [64, 2 * T + 3 * 64])
        f_w4 = at("f_w4", 41, [64, 2, DB])
        f_a = at("f_a", 45, [64, T])
        f_k = at("f_k", 49, [64, T])
        f_h = at("f_h", 53, [64, T])
        eo = at("eo", 57, [P, 2, 2, DB])
        win_sb = at("win_sb", 65, [P, KT, DB])
        nv = at("nv", 82, [P, TC])
        nt = at("nt", 88, [P, TC])
        cfm = at("cfm", 120, [P, NB, T + CFK - 1])
        cfo = at("cfo", 137, [P, NB, T])
        st = at("st", 153, [P, 6, T + 8])
        cvo = at("cvo", 178, [P, 3, T])
        sqt = at("sqt", 190, [P, 2, T])
        cst = at("cst", 198, [P, 4, C])
        q_t = at("q_t", 137, [P, TC])
        q_r = at("q_r", 142, [P, TC])
        q_v = at("q_v", 147, [P, TC])
        l_r = at("l_r", 120, [P, T])
        l_v = at("l_v", 124, [P, T])
        l_t = at("l_t", 128, [P, T])
        u_f = at("u_f", 185, [P, NB, T])
        u_hi = at("u_hi", 153, [P, KT, DB], F32R)
        u_lo = at("u_lo", 169, [P, KT, DB], F32R)
        a_q = at("a_q", 32, [P, T])
        a_k = at("a_k", 36, [P, T])
        a_v = at("a_v", 40, [P, T])
        a_kc = at("a_kc", 44, [P, C])
        a_vc = at("a_vc", 45, [P, C])
        a_vt = at("a_vt", 46, [P, 10, P])
        a_g = at("a_g", 51, [P, 2, XR * GRID])
        a_m = at("a_m", 60, [P, len(MASKS), LOC])
        a_b = at("a_b", 73, [P, KEYS])
        a_s = at("a_s", 77, [P, 2, KEYS])
        a_p = at("a_p", 84, [P, 2, KEYS])
        a_pt = at("a_pt", 91, [P, 2, KEYS])
        a_o = at("a_o", 98, [P, ROWS // 2, P])
        a_z = at("a_z", 102, [P, T])
        pr_hi = at("pr_hi", 32, [P, KT, DB], F32R)
        pr_lo = at("pr_lo", 48, [P, KT, DB], F32R)
        ps_hi = at("ps_hi", 64, [P, KT, DB], F32R)
        ps_lo = at("ps_lo", 80, [P, KT, DB], F32R)
        k_sb = at("k_sb", 96, [P, 2, 2, DB])
        pw = at("pw", 136, [P, 2, 4, DB])
        x0_f = at("x0_f", 120, [P, NB, T])
        y_t = at("y_t", 112, [P, 2, DB])
        y_w = at("y_w", 116, [P, 2, NB, P])
        z_hi = [at("z_hi0", 153, [P, NB, T], F32R), at("z_hi1", 32, [P, NB, T], F32R)]
        z_lo = [at("z_lo0", 169, [P, NB, T], F32R), at("z_lo1", 48, [P, NB, T], F32R)]
        mrg = at("mrg", 64, [P, KT, T])
        gt = at("gt", 96, [P, 4, T])
        zraw = at("zraw", 136, [P, NB, T])
        yt = at("yt", 185, [P, T])
        m_hi = at("m_hi", 120, [P, KT, T], F32R)
        m_lo = at("m_lo", 152, [P, KT, T], F32R)
        x1 = at("x1", 32, [P, KT, T])
        sq2 = at("sq2", 96, [P, 2, T])
        r2 = at("r2", 185, [P, T])
        v2 = at("v2", 189, [P, T])
        t2 = at("t2", 193, [P, T])
        h2_hi = at("h2_hi", 64, [P, KT, T], F32R)
        h2_lo = at("h2_lo", 96, [P, KT, T], F32R)
        ht = at("ht", 160, [P, 2, T])
        g_hi = at("g_hi", 128, [P, 8, T], F32R)
        g_lo = at("g_lo", 160, [P, 8, T], F32R)
        sg = at("sg", 192, [P, T])
        gm = at("gm", 196, [P, T])

        ps = ctx.enter_context(nc.psum_tensor("ps", [P, 8 * HALF], F32))

        def bank(b, n=1, width=None):
            return ps[:, b * HALF:b * HALF + (width or n * HALF)]

        s_const = sem("s_const")
        s_filt = sem("s_filt")
        s_win = sem("s_win")
        s_raw = [sem(f"s_raw{i}") for i in range(4)]
        s_hi = sem("s_hi")
        s_split = sem("s_split")
        s_used = sem("s_used")
        s_gate = sem("s_gate")
        s_mraw = [sem(f"s_mraw{i}") for i in range(2)]
        s_mused = sem("s_mused")
        s_csg = sem("s_csg")
        s_cs = sem("s_cs")
        s_xs = [sem(f"s_xs{i}") for i in range(2)]
        s_sq = sem("s_sq")
        s_ss = sem("s_ss")
        s_fmm = sem("s_fmm")
        s_fred = sem("s_fred")
        s_fsin = sem("s_fsin")
        s_w4 = sem("s_w4")
        s_eomm = sem("s_eomm")
        s_eoev = sem("s_eoev")
        s_eo = sem("s_eo")
        s_eohi = sem("s_eohi")
        s_eolo = sem("s_eolo")
        s_alt = sem("s_alt")
        s_ny = sem("s_ny")
        s_r0 = sem("s_r0")
        s_nv = sem("s_nv")
        s_ht = sem("s_ht")
        s_hh = sem("s_hh")
        s_hlo = sem("s_hlo")
        s_ev = sem("s_ev")
        s_kst = sem("s_kst")
        s_pad = sem("s_pad")
        s_cfm = sem("s_cfm")
        s_grpout = sem("s_grpout")
        s_cvst = sem("s_cvst")
        s_cacc = sem("s_cacc")
        s_cev = sem("s_cev")
        s_qsq = sem("s_qsq")
        s_qones = sem("s_qones")
        s_qr = sem("s_qr")
        s_qfree = sem("s_qfree")
        s_qn = sem("s_qn")
        s_qst = [sem(f"s_qst{i}") for i in range(6)]
        s_cst = [sem(f"s_cst{i}") for i in range(4)]
        s_gst = [sem(f"s_gst{i}") for i in range(4)]
        s_modev = sem("s_modev")
        s_conv = sem("s_conv")
        s_l1 = sem("s_l1")
        s_lx = sem("s_lx")
        s_lsq = sem("s_lsq")
        s_l2 = sem("s_l2")
        s_lr = sem("s_lr")
        s_lf = sem("s_lf")
        s_ly = sem("s_ly")
        s_lz = sem("s_lz")
        s_zst = sem("s_zst")
        s_uld = sem("s_uld")
        s_ut = sem("s_ut")
        s_uhi = sem("s_uhi")
        s_ulo = sem("s_ulo")
        s_mask = sem("s_mask")
        s_ald = sem("s_ald")
        s_avt = sem("s_avt")
        s_avev = sem("s_avev")
        s_as = sem("s_as")
        s_attr = sem("s_attr")
        s_anm = sem("s_anm")
        s_aexp = sem("s_aexp")
        s_at = sem("s_at")
        s_aeva = sem("s_aeva")
        s_aevd = sem("s_aevd")
        s_apv = sem("s_apv")
        s_ao = sem("s_ao")
        s_azt = sem("s_azt")
        s_azev = sem("s_azev")
        s_azst = sem("s_azst")
        s_k = [sem(f"s_k{i}") for i in range(2)]
        s_ud = sem("s_ud")
        s_udev = sem("s_udev")
        s_pr = sem("s_pr")
        s_prhi = sem("s_prhi")
        s_prlo = sem("s_prlo")
        s_x0 = sem("s_x0")
        s_id = sem("s_id")
        s_idev = sem("s_idev")
        s_idt = sem("s_idt")
        s_idz = sem("s_idz")
        s_idst = [sem(f"s_idst{i}") for i in range(2)]
        s_zld = sem("s_zld")
        s_zhi = sem("s_zhi")
        s_zlo = sem("s_zlo")
        s_gld = [sem(f"s_gld{i}") for i in range(4)]
        s_y = sem("s_y")
        s_yev = sem("s_yev")
        s_mg = sem("s_mg")
        s_mhi = sem("s_mhi")
        s_mlo = sem("s_mlo")
        s_x1 = sem("s_x1")
        s_wo = sem("s_wo")
        s_woev = sem("s_woev")
        s_sq2 = sem("s_sq2")
        s_one2 = sem("s_one2")
        s_r2 = sem("s_r2")
        s_v2 = sem("s_v2")
        s_mod1 = sem("s_mod1")
        s_t2 = sem("s_t2")
        s_h2h = sem("s_h2h")
        s_h2 = sem("s_h2")
        s_fin = sem("s_fin")
        s_sil = sem("s_sil")
        s_up = sem("s_up")
        s_ghi = sem("s_ghi")
        s_glo = sem("s_glo")
        s_fo = sem("s_fo")
        s_foev = sem("s_foev")
        s_out = sem("s_out")
        s_dve = sem("s_dve")
        s_act = sem("s_act")

        def vcol(name, i=0, n=1):
            return v_sb[:, VEC[name] + i:VEC[name] + i + n]

        block = ctx.enter_context(nc.Block())

        @block.sync
        def _(sp):
            def mod_chunk(n, slot):
                sp.dma_start(mraw[:, slot, :], wmod[n]).then_inc(s_mraw[slot], 16)

            sp.dma_start(f_sb[:, :], filt).then_inc(s_filt, 16)
            for k in range(KT):
                if k >= 2:
                    sp.wait_ge(s_ss, k - 1)
                sp.dma_start(xs[:, k % 2, :], xc[k]).then_inc(s_xs[k % 2], 16)
                for j in range(2):
                    if k >= 1:
                        sp.wait_ge(s_mused, 2 * k + j - 1)
                    mod_chunk(2 * k + j, j)
            sp.dma_start(win_sb[:, :, :], win).then_inc(s_win, 16)

            def main_chunks(i, first=False):
                for j in range(4):
                    if not first:
                        sp.wait_ge(s_split, 4 * i + j - 3)
                    sp.dma_start(raw[:, j, :], w[4 * i + j]).then_inc(s_raw[j], 16)

            main_chunks(0, first=True)
            n_k = CK_IN // 4
            n_m = 32 // 4
            with sp.Fori(1, n_k) as i:
                main_chunks(i)
            with sp.Fori(n_k, n_k + n_m) as i:
                main_chunks(i)
                for j in range(4):
                    m = 16 + 4 * (i - n_k) + j
                    sp.wait_ge(s_mused, m - 1)
                    mod_chunk(m, j % 2)
            with sp.Fori(n_k + n_m, CK_UDFT // 4) as i:
                main_chunks(i)

            sp.wait_ge(s_l2, NB)
            for i in range(6):
                sp.wait_ge(s_qst[i], 32)
            for i in range(4):
                sp.wait_ge(s_cst[i], 32)
            sp.wait_ge(s_cvst, 16 * (2 * NB + NB))
            sp.dma_start(u_f[:, :, :], u_d.rearrange("c p t -> p c t")).then_inc(s_uld, 16)
            sp.dma_start(a_m[:, :, :], masks).then_inc(s_mask, 16)
            for hp in range(NB):
                if hp:
                    sp.wait_ge(s_apv, 16 * hp)
                    sp.wait_ge(s_attr, 16 * hp)
                sp.dma_start(a_q[:, :], qkv_d[hp]).then_inc(s_ald, 16)
                sp.dma_start(a_k[:, :], qkv_d[NB + hp]).then_inc(s_ald, 16)
                sp.dma_start(a_v[:, :], qkv_d[2 * NB + hp]).then_inc(s_ald, 16)
                sp.dma_start(a_kc[:, :], kvc_d[hp]).then_inc(s_ald, 16)
                sp.dma_start(a_vc[:, :], kvc_d[NB + hp]).then_inc(s_ald, 16)
                sp.dma_start(a_g[:, :, :], gat[2 * hp:2 * hp + 2].rearrange("e p x -> p e x")).then_inc(s_ald, 16)
            with sp.Fori(CK_UDFT // 4, N_CHUNK // 4) as i:
                main_chunks(i)
            for d in range(KT):
                sp.wait_ge(s_foev, 2 * KT + d + 1)
                sp.dma_start(out[d], x1[:, d, :]).then_inc(s_out, 16)
            sp.wait_ge(s_out, 16 * KT)

        @block.gpsimd
        def _(pool):
            def split(i, first=False):
                for j in range(4):
                    n = 4 * i + j
                    pool.wait_ge(s_raw[j], 16 * (i + 1))
                    if not (first and j < 2):
                        pool.wait_ge(s_used, n - 1)
                    nc.gpsimd.tensor_tensor(gate0[:, 1:2], gate0[:, 0:1], gate0[:, 0:1], ALU.add)
                    nc.gpsimd.tensor_scalar(whi[:, j % 2, :], raw[:, j, :], 1.0, 0.0, ALU.mult,
                                            ALU.add).then_inc(s_hi, 1)
                    pool.wait_ge(s_hi, n + 1)
                    nc.gpsimd.tensor_tensor(wlo[:, j % 2, :], raw[:, j, :], whi[:, j % 2, :].bitcast(F32),
                                            ALU.subtract).then_inc(s_split, 1)

            nc.gpsimd.memset(gate0[:, :], 0.0).then_inc(s_gate, 1)
            pool.wait_ge(s_gate, 1)
            split(0, first=True)
            with pool.Fori(1, N_CHUNK // 4) as i:
                split(i)

        @block.tensor
        def _(pe):
            def chunk_in(n):
                pe.wait_ge(s_split, n + 1)

            def mm3(o, slot, k, hi, lo, start, stop):
                a, b = whi[:, slot, k * P:(k + 1) * P], wlo[:, slot, k * P:(k + 1) * P]
                nc.tensor.matmul(o, a, hi, start=start, stop=False)
                nc.tensor.matmul(o, a, lo, start=False, stop=False)
                return nc.tensor.matmul(o, b, hi, start=False, stop=stop)

            def strip(slot, b0, hi, lo, ks=KT, k0=0, sk=0, last=None):
                for half in range(2):
                    for k in range(ks):
                        t = slice(half * HALF, (half + 1) * HALF)
                        mm = mm3(bank(b0 + half), slot, sk + k, hi[:, k0 + k, t], lo[:, k0 + k, t],
                                 k == 0, k == ks - 1)
                return mm

            def filter_layer(n, lhsT, rhs):
                for half in range(2):
                    t = slice(half * HALF, (half + 1) * HALF)
                    mm = nc.tensor.matmul(bank(4 + half)[0:64, :], lhsT, rhs[:, t], start=True, stop=True)
                mm.then_inc(s_fmm, 1)

            def mod_tile(n, slot):
                for k in range(KT):
                    mm = nc.tensor.matmul(ps[:, bass.ds(6 * HALF + 2 * n, 2)], mraw[:, slot, k * P:(k + 1) * P],
                                          cs[:, 2 * k:2 * k + 2], start=k == 0, stop=k == KT - 1)
                mm.then_inc(s_mused, 1)

            pe.wait_ge(s_filt, 16)
            filter_layer(0, f_sb[0:33, 2 * T:2 * T + 64], f_sb[0:33, 0:T])
            pe.wait_ge(s_const, 32)
            for k in range(KT):
                pe.wait_ge(s_sq, k + 1)
                for b, n in ((0, HALF), (1, HALF), (2, C)):
                    mm = nc.tensor.matmul(bank(b, width=n), ones, xs[:, k % 2, b * HALF:b * HALF + n],
                                          start=k == 0, stop=k == KT - 1)
                mm.then_inc(s_ss, 1)
                if k == 0:
                    pe.wait_ge(s_cs, 1)
                for j in range(2):
                    pe.wait_ge(s_mraw[j], 16 * (k + 1))
                    mod_tile(2 * k + j, j)
                if k == 3:
                    pe.wait_ge(s_fsin, 1)
                    filter_layer(1, f_sb[:, 2 * T + 64:2 * T + 128], f_h)
                if k == 7:
                    pe.wait_ge(s_fsin, 2)
                    filter_layer(2, f_sb[:, 2 * T + 128:2 * T + 192], f_h)
            pe.wait_ge(s_fsin, 3)
            pe.wait_ge(s_w4, 1)
            for t in range(KT):
                for part in range(2):
                    n = 2 * t + part
                    if n >= 2:
                        pe.wait_ge(s_eoev, n - 1)
                    nc.tensor.matmul(bank(4 + n % 2), f_h[:, t * P:(t + 1) * P], f_w4[:, part, :],
                                     start=True, stop=True).then_inc(s_eomm, 1)
            pe.wait_ge(s_eolo, KT)
            pe.wait_ge(s_alt, 1)
            pe.wait_ge(s_eoev, 2 * KT)
            for t in range(KT):
                nc.tensor.matmul(bank(4), altr[:, :], e_hi[:, t, :], start=t == 0, stop=False)
                mm = nc.tensor.matmul(bank(4), altr[:, :], e_lo[:, t, :], start=False, stop=t == KT - 1)
            mm.then_inc(s_ny, 1)
            pe.wait_ge(s_nv, 1)
            pe.wait_ge(s_r0, 1)

            def kdft(i, first=False):
                for j in range(2):
                    q = 2 * i + j
                    if not first:
                        pe.wait_ge(s_ev, q - 1)
                    for part, (hi, lo) in enumerate(((e_hi, e_lo), (o_hi, o_lo))):
                        chunk_in(CK_KDFT + 2 * q + part)
                        for k in range(KT):
                            mm = mm3(bank(2 * j + part), part, k, hi[:, k, :], lo[:, k, :], k == 0, k == KT - 1)
                        mm.then_inc(s_used, 1)

            kdft(0, first=True)
            with pe.Fori(1, KT // 2) as i:
                kdft(i)

            pe.wait_ge(s_hlo, KT)
            pe.wait_ge(s_mod1, 1)

            def in_strip(n, j):
                chunk_in(CK_IN + n)
                pe.wait_ge(s_ev, n + KT - 1)
                strip(j, 2 * j, h_hi, h_lo).then_inc(s_used, 1)

            with pe.Fori(0, S_QKV // 2) as i:
                for j in range(2):
                    in_strip(2 * i + j, j)
                    pe.wait_ge(s_mraw[j], 16 * (i + KT + 1))
                    mod_tile(16 + 2 * i + j, j)

            def q_ones(t):
                pe.wait_ge(s_qsq, t + 1)
                if t >= NB:
                    pe.wait_ge(s_cev, t - NB + 1)
                if t:
                    pe.wait_ge(s_qfree, t)
                    pe.wait_ge(s_qr, t)
                for half in range(2):
                    mm = nc.tensor.matmul(bank(6 + half), heads, q_t[:, half * HALF:(half + 1) * HALF],
                                          start=True, stop=True)
                if t >= NB:
                    mm = nc.tensor.matmul(bank(4 + t % 2)[:, C:2 * C], heads, q_t[:, T:TC], start=True, stop=True)
                mm.then_inc(s_qones, 1)

            for t in range(N_QKV):
                n, j = S_QKV + t, t % 2
                if t == 0:
                    pe.wait_ge(s_modev, 1)
                if t >= NB:
                    chunk_in(CK_IN + n)
                    if t >= NB + 2:
                        pe.wait_ge(s_cev, t - NB - 1)
                        if t - 2 < 2 * NB:
                            pe.wait_ge(s_qfree, t - 1)
                            pe.wait_ge(s_qr, t - 1)
                    for k in range(KT):
                        mm = mm3(bank(4 + j, width=C), j, k, c_hi[:, k, :], c_lo[:, k, :], k == 0, k == KT - 1)
                    mm.then_inc(s_cacc, 1)
                in_strip(n, j)
                if 1 <= t <= 2 * NB:
                    q_ones(t - 1)
            with pe.Fori(0, N_G // 2) as i:
                for j in range(2):
                    in_strip(S_G + 2 * i + j, j)

            pe.wait_ge(s_conv, NB)
            for half in range(2):
                for c in range(NB):
                    mm = nc.tensor.matmul(bank(4 + half), ones, cfo[:, c, half * HALF:(half + 1) * HALF],
                                          start=c == 0, stop=c == NB - 1)
            mm.then_inc(s_l1, 1)
            for c in range(NB):
                pe.wait_ge(s_lsq, c + 1)
                for half in range(2):
                    mm = nc.tensor.matmul(bank(6 + half), ones, sqt[:, c % 2, half * HALF:(half + 1) * HALF],
                                          start=c == 0, stop=c == NB - 1)
                mm.then_inc(s_l2, 1)
            pe.wait_ge(s_uld, 16)
            pe.wait_ge(s_ev, KT + N_STRIP)
            for t in range(KT):
                if t >= 4:
                    pe.wait_ge(s_ulo, t - 3)
                for c in range(NB):
                    mm = nc.tensor.transpose(bank(t % 4)[:, c * P:(c + 1) * P], u_f[:, c, t * P:(t + 1) * P], ident)
                mm.then_inc(s_ut, 1)
            pe.wait_ge(s_ulo, KT)
            pe.wait_ge(s_lf, 1)
            pe.wait_ge(s_lr, 1)

            def scores(g):
                hp, it = divmod(g, 16)
                e, rp = divmod(it, 8)
                if it == 0:
                    pe.wait_ge(s_ald, 96 * (hp + 1))
                    if hp:
                        pe.wait_ge(s_azev, hp)
                    for t in range(8):
                        nc.tensor.transpose(ps[:, 4 * HALF + t * P:4 * HALF + (t + 1) * P],
                                            a_v[:, t * P:(t + 1) * P], ident)
                    if hp:
                        pe.wait_ge(s_ao, 16 * hp)
                    for t in range(2):
                        mm = nc.tensor.transpose(ps[:, 6 * HALF + t * P:6 * HALF + (t + 1) * P],
                                                 a_vc[:, t * P:(t + 1) * P], ident)
                    mm.then_inc(s_avt, 1)
                if g >= 2:
                    pe.wait_ge(s_attr, g - 1)
                hs = slice(e * HD, (e + 1) * HD)
                b0 = 2 * (g % 2)
                q = a_q[hs, rp * P:(rp + 1) * P]
                k0 = window_start(rp) * GRID
                nc.tensor.matmul(bank(b0), q, a_k[hs, k0:k0 + HALF], start=True, stop=True)
                nc.tensor.matmul(bank(b0 + 1)[:, 0:P], q, a_k[hs, k0 + HALF:k0 + LOC], start=True, stop=True)
                nc.tensor.matmul(bank(b0 + 1)[:, P:P + C], q, a_kc[hs, :], start=True,
                                 stop=True).then_inc(s_as, 1)

            def turn(g):
                if g % 16 == 0:
                    pe.wait_ge(s_avev, g // 16 + 1)
                pe.wait_ge(s_aexp, g + 1)
                if g:
                    pe.wait_ge(s_aeva, g)
                    pe.wait_ge(s_aevd, g)
                for b in range(7):
                    mm = nc.tensor.transpose(ps[:, 4 * HALF + b * P:4 * HALF + (b + 1) * P],
                                             a_p[:, g % 2, b * P:(b + 1) * P], ident)
                mm.then_inc(s_at, 1)

            def values(g):
                e, rp = divmod(g % 16, 8)
                pe.wait_ge(s_aeva, g + 1)
                pe.wait_ge(s_aevd, g + 1)
                if g >= 2:
                    pe.wait_ge(s_ao, g - 1)
                v0 = window_start(rp) // 2
                for b in range(7):
                    tile = v0 + b if b < 5 else 8 + b - 5
                    mm = nc.tensor.matmul(bank(6 + g % 2)[:, 0:HD], a_pt[:, g % 2, b * P:(b + 1) * P],
                                          a_vt[:, tile, e * HD:(e + 1) * HD], start=b == 0, stop=b == 6)
                mm.then_inc(s_apv, 1)

            for hp in range(NB):
                g0 = 16 * hp
                scores(g0)
                for it in range(16):
                    if it < 15:
                        scores(g0 + it + 1)
                    turn(g0 + it)
                    if it:
                        values(g0 + it - 1)
                values(g0 + 15)
                pe.wait_ge(s_ao, g0 + 16)
                for rp in range(8):
                    mm = nc.tensor.transpose(ps[:, 4 * HALF + rp * P:4 * HALF + (rp + 1) * P], a_o[:, rp, :], ident)
                mm.then_inc(s_azt, 1)

            def udft(i, first=False):
                for j in range(2):
                    q = 2 * i + j
                    if not first:
                        pe.wait_ge(s_udev, q - 1)
                    for part in range(2):
                        chunk_in(CK_UDFT + 2 * q + part)
                        for k in range(KT):
                            mm = mm3(bank(2 * j + part), part, k, u_hi[:, k, :], u_lo[:, k, :], k == 0, k == KT - 1)
                        mm.then_inc(s_used, 1)

            pe.wait_ge(s_attr, 16 * NB)
            udft(0, first=True)
            with pe.Fori(1, KT // 2) as i:
                udft(i)
            pe.wait_ge(s_prlo, KT)
            pe.wait_ge(s_udev, KT)

            def inverse(t, slot, first=False):
                if not first:
                    pe.wait_ge(s_idev, t - 1)
                for part, (hi, lo) in enumerate(((pr_hi, pr_lo), (ps_hi, ps_lo))):
                    chunk_in(CK_IDFT + 2 * t + part)
                    for k in range(KT):
                        mm = mm3(bank(slot), part, k, hi[:, k, :], lo[:, k, :],
                                 part == 0 and k == 0, part == 1 and k == KT - 1)
                    mm.then_inc(s_used, 1)

            def back(t, slot, first=False):
                pe.wait_ge(s_idev, t + 1)
                if not first:
                    pe.wait_ge(s_idz, t - 1)
                for c in range(NB):
                    mm = nc.tensor.transpose(bank(4 + slot)[:, c * P:(c + 1) * P], y_t[:, slot, c * P:(c + 1) * P], ident)
                mm.then_inc(s_idt, 1)

            pe.wait_ge(s_azev, NB)
            inverse(0, 0, first=True)
            inverse(1, 1, first=True)
            back(0, 0, first=True)
            inverse(2, 0)
            back(1, 1, first=True)
            with pe.Fori(1, 3) as i:
                inverse(2 * i + 1, 1)
                back(2 * i, 0)
                inverse(2 * i + 2, 0)
                back(2 * i + 1, 1)
            inverse(7, 1)
            back(6, 0)
            back(7, 1)

            pe.wait_ge(s_idev, KT)
            for b in range(NBR):
                pe.wait_ge(s_zlo, b + 1)

                def y_pair(i, slot, first=False):
                    chunk_in(CK_Y + NB * b + 2 * i + slot)
                    for dd in range(2):
                        if not first:
                            pe.wait_ge(s_yev, 8 * b + 4 * i + 2 * slot + dd - 1)
                        mm = strip(slot, 2 * dd, z_hi[b % 2], z_lo[b % 2], ks=NB, sk=NB * dd)
                        if dd == 0:
                            mm.then_inc(s_y, 1)
                    mm.then_inc(s_used, 1)

                if b == 0:
                    y_pair(0, 0, first=True)
                    y_pair(0, 1)
                    with pe.Fori(1, 2) as i:
                        for slot in range(2):
                            y_pair(i, slot)
                else:
                    with pe.Fori(0, 2) as i:
                        for slot in range(2):
                            y_pair(i, slot)

            pe.wait_ge(s_mlo, KT)

            def wo(d, slot):
                chunk_in(CK_WO + d)
                strip(slot, 2 * slot, m_hi, m_lo).then_inc(s_used, 1)

            def wo_ones(d, slot, start=False, stop=False):
                pe.wait_ge(s_sq2, d + 1)
                for half in range(2):
                    mm = nc.tensor.matmul(bank(4 + half), ones, sq2[:, slot, half * HALF:(half + 1) * HALF],
                                          start=start, stop=stop)
                mm.then_inc(s_one2, 1)

            pe.wait_ge(s_yev, NBR * KT)
            wo(0, 0)
            wo(1, 1)
            wo_ones(0, 0, start=True)
            with pe.Fori(0, 3) as i:
                pe.wait_ge(s_woev, 2 * i + 1)
                wo(2 * i + 2, 0)
                wo_ones(2 * i + 1, 1)
                pe.wait_ge(s_woev, 2 * i + 2)
                wo(2 * i + 3, 1)
                wo_ones(2 * i + 2, 0)
            wo_ones(7, 1, stop=True)

            pe.wait_ge(s_h2, KT)
            base, done = CK_FFN, 0
            for g, gn in enumerate(FGROUPS):

                def hidden(i, first=False):
                    chunk_in(base + 2 * i)
                    if not first:
                        pe.wait_ge(s_sil, done + i)
                    strip(0, 0, h2_hi, h2_lo).then_inc(s_used, 1)
                    chunk_in(base + 2 * i + 1)
                    if not first:
                        pe.wait_ge(s_up, done + i)
                    strip(1, 2, h2_hi, h2_lo).then_inc(s_used, 1)

                if g == 0:
                    hidden(0, first=True)
                with pe.Fori(int(g == 0), gn) as i:
                    hidden(i)
                done += gn
                base += 2 * gn
                pe.wait_ge(s_glo, done)
                if g == 0:
                    pe.wait_ge(s_h2, KT)

                def ffn_out(i, first=False):
                    for j in range(2):
                        chunk_in(base + 2 * i + j)
                        if not first:
                            pe.wait_ge(s_foev, KT * g + 2 * i + j - 1)
                        strip(j, 4 + 2 * j, g_hi, g_lo, ks=gn).then_inc(s_used, 1)

                if g == 0:
                    ffn_out(0, first=True)
                    with pe.Fori(1, KT // 2) as i:
                        ffn_out(i)
                else:
                    with pe.Fori(0, KT // 2) as i:
                        ffn_out(i)
                base += KT

        @block.scalar
        def _(act):
            own = Steps(act, s_act)

            def func(o, i, f, **kw):
                return nc.scalar.activation(o, i, f, **kw)

            def copy(o, i):
                return func(o, i, ACT.Identity)

            def log_rsqrt(r, sums, n):
                own.done(func(r, sums, ACT.Ln, scale=1.0 / n, bias=vcol("eps")))
                return func(r, r, ACT.Exp, scale=-0.5)

            act.dma_start(v_sb[:, :], vec).then_inc(s_const, 16)
            act.dma_start(m_sb[:, :, :], mats).then_inc(s_const, 16)
            act.wait_ge(s_const, 32)
            func(csg[:, :], vcol("c", 0, 2 * KT), ACT.Sigmoid).then_inc(s_csg, 1)

            def sin(n):
                act.wait_ge(s_fred, n + 1)
                func(f_h[:, :], f_a[:, :], ACT.Sin).then_inc(s_fsin, 1)

            for k in range(KT):
                act.wait_ge(s_xs[k % 2], 16 * (k // 2 + 1))
                func(xs[:, k % 2, :], xs[:, k % 2, :], ACT.Square).then_inc(s_sq, 1)
                if k == 3:
                    sin(0)
                if k == 7:
                    sin(1)
            sin(2)
            act.wait_ge(s_ss, KT)
            act.wait_ge(s_nv, 1)
            log_rsqrt(rstd[:, :], bank(0, width=TC), D).then_inc(s_r0, 1)
            for t in range(KT):
                act.wait_ge(s_eo, t + 1)
                copy(e_hi[:, t, :], eo[:, t % 2, 0, :])
                copy(o_hi[:, t, :], eo[:, t % 2, 1, :]).then_inc(s_eohi, 1)

            def x_load(k):
                act.dma_start(xs[:, k % 2, :], xc[k]).then_inc(s_xs[k % 2], 16)

            x_load(0)
            x_load(1)
            for k in range(KT):
                act.wait_ge(s_ht, k + 1)
                own.done(func(xs[:, k % 2, 0:T], xs[:, k % 2, 0:T], ACT.Identity, bias=mod[:, k, 0:1]))
                own.done(func(xs[:, k % 2, T:TC], xs[:, k % 2, T:TC], ACT.Identity, bias=mod[:, k, 1:2]))
                copy(h_hi[:, k, :], xs[:, k % 2, 0:T])
                copy(c_hi[:, k, :], xs[:, k % 2, T:TC]).then_inc(s_hh, 1)
                if k + 2 < KT:
                    act.wait_ge(s_hlo, k + 1)
                    x_load(k + 2)
            for q in range(KT):
                act.wait_ge(s_used, 2 * q + 2)
                if q:
                    act.wait_ge(s_kst, 16 * q)
                copy(ksp[:, :, :], bank(2 * (q % 2), 2)).then_inc(s_ev, 1)
                act.wait_ge(s_ev, q + 1)
                if q == 0:
                    act.wait_ge(s_ny, 1)
                    own.done(copy(ksp[0:1, 1, :], bank(4)[0:1, :]))
                act.dma_start(kspec[q], ksp[:, :, :]).then_inc(s_kst, 16)

            def strip_out(n, dst, f=ACT.Identity):
                act.wait_ge(s_used, CK_IN + n + 1)
                func(dst, bank(2 * (n % 2), 2), f).then_inc(s_ev, 1)

            for c in range(NB):
                if c >= 2:
                    act.wait_ge(s_cfm, c - 1)
                strip_out(2 * c, st[:, 2 * c % 4, 1:T + 1])
                strip_out(2 * c + 1, st[:, (2 * c + 1) % 4, 1:T + 1], ACT.Sigmoid)
            for g in range(2 * NB):
                if g == 0:
                    act.wait_ge(s_cfm, NB)
                if g >= 2:
                    act.wait_ge(s_grpout, g - 1)
                for j in range(3):
                    strip_out(S_HY + 3 * g + j, st[:, 3 * (g % 2) + j, 1:T + 1])
                act.wait_ge(s_grpout, g + 1)
                if g < NB:
                    act.dma_start(x0_d[g], cvo[:, 0, :]).then_inc(s_cvst, 16)
                    act.dma_start(u_d[g], cvo[:, 1, :]).then_inc(s_cvst, 16)
                else:
                    act.dma_start(z_d[Z_A, g - NB], cvo[:, 0, :]).then_inc(s_cvst, 16)
            act.wait_ge(s_kst, 16 * KT)
            for t in range(N_QKV):
                if t >= 6:
                    act.wait_ge(s_qst[t % 6], 16)
                strip_out(S_QKV + t, st[:, t % 6, 0:T])
                if t >= NB:
                    u = (t - NB) % 4
                    act.wait_ge(s_cacc, t - NB + 1)
                    if t >= 2 * NB:
                        act.wait_ge(s_cst[u], 16)
                    copy(cst[:, u, :], bank(4 + t % 2, width=C)).then_inc(s_cev, 1)
                if 1 <= t <= 2 * NB:
                    act.wait_ge(s_qfree, t)
                    if t >= 2:
                        act.wait_ge(s_qn, t - 1)
                    r1 = log_rsqrt(q_r[:, 0:T], bank(6, 2), HD)
                    if t - 1 >= NB:
                        r1 = log_rsqrt(q_r[:, T:TC], bank(4 + (t - 1) % 2)[:, C:2 * C], HD)
                    r1.then_inc(s_qr, 1)
                for o in ([t - 2] if 0 <= t - 2 < 2 * NB else []) + ([t] if t >= 2 * NB else []):
                    if o < 2 * NB:
                        act.wait_ge(s_qn, o + 1)
                    else:
                        act.wait_ge(s_ev, KT + S_QKV + o + 1)
                        act.wait_ge(s_cev, o - NB + 1)
                    act.dma_start(qkv_d[o], st[:, o % 6, 0:T]).then_inc(s_qst[o % 6], 16)
                    if o >= NB:
                        act.dma_start(kvc_d[o - NB], cst[:, (o - NB) % 4, :]).then_inc(s_cst[(o - NB) % 4], 16)
            for j in range(4):
                act.wait_ge(s_qst[j], 32)

            def gates(i, first=False):
                for j in range(4):
                    m = 4 * i + j
                    if not first:
                        act.wait_ge(s_gst[j], 16 * i)
                    act.wait_ge(s_used, CK_IN + S_G + m + 1)
                    func(st[:, j, 0:T], bank(2 * (j % 2), 2), ACT.Sigmoid).then_inc(s_ev, 1)
                    act.wait_ge(s_ev, KT + S_G + m + 1)
                    act.dma_start(gate_d[m], st[:, j, 0:T]).then_inc(s_gst[j], 16)

            gates(0, first=True)
            with act.Fori(1, N_G // 4) as i:
                gates(i)

            for c in range(NB):
                act.wait_ge(s_lx, c + 1)
                if c >= 2:
                    act.wait_ge(s_l2, c - 1)
                func(sqt[:, c % 2, :], cfo[:, c, :], ACT.Square).then_inc(s_lsq, 1)
            act.wait_ge(s_lf, 1)
            log_rsqrt(l_r[:, :], bank(6, 2), DB).then_inc(s_lr, 1)
            for c in range(NB):
                act.wait_ge(s_ly, c + 1)
                func(cfo[:, c, :], cfo[:, c, :], ACT.Silu, scale=vcol("lng", c),
                     bias=vcol("lnb", c)).then_inc(s_lz, 1)
                act.wait_ge(s_lz, c + 1)
                act.dma_start(z_d[Z_CF, c], cfo[:, c, :]).then_inc(s_zst, 16)
            for j in range(4):
                act.wait_ge(s_gst[j], 16 * N_G // 4)
            for t in range(KT):
                act.wait_ge(s_ut, t + 1)
                copy(u_hi[:, t, :], bank(t % 4)).then_inc(s_uhi, 1)

            def exps(g):
                act.wait_ge(s_anm, g + 1)
                if g >= 2:
                    act.wait_ge(s_at, g - 1)
                func(a_p[:, g % 2, :], a_s[:, g % 2, :], ACT.Exp, bias=st_nm[:, g % 2:g % 2 + 1],
                     accum_out=st_l[:, g % 2:g % 2 + 1]).then_inc(s_aexp, 1)

            def evacuate(g):
                act.wait_ge(s_at, g + 1)
                if g >= 2:
                    act.wait_ge(s_apv, g - 1)
                copy(a_pt[:, g % 2, 0:HALF], bank(4)).then_inc(s_aeva, 1)

            for hp in range(NB):
                act.wait_ge(s_avt, hp + 1)
                copy(a_vt[:, :, :], bank(4, width=10 * P)).then_inc(s_avev, 1)
                for it in range(16):
                    exps(16 * hp + it)
                    if it:
                        evacuate(16 * hp + it - 1)
                evacuate(16 * hp + 15)
                act.wait_ge(s_azt, hp + 1)
                if hp:
                    act.wait_ge(s_azst, 16 * hp)
                copy(a_z[:, :], bank(4, 2)).then_inc(s_azev, 1)
                act.wait_ge(s_azev, hp + 1)
                act.dma_start(z_d[Z_NA, hp], a_z[:, :]).then_inc(s_azst, 16)

            def k_load(q):
                act.dma_start(k_sb[:, q % 2, :, :], kspec[q]).then_inc(s_k[q % 2], 16)

            act.wait_ge(s_azst, 16 * NB)
            act.wait_ge(s_zst, 16 * NB)
            act.wait_ge(s_ly, NB)
            k_load(0)
            k_load(1)
            act.dma_start(x0_f[:, :, :], x0_d.rearrange("c p t -> p c t")).then_inc(s_x0, 16)
            for q in range(KT):
                act.wait_ge(s_pr, q + 1)
                copy(pr_hi[:, q, :], pw[:, q % 2, 0, :])
                copy(ps_hi[:, q, :], pw[:, q % 2, 2, :]).then_inc(s_prhi, 1)
                if q + 2 < KT:
                    act.wait_ge(s_udev, q + 1)
                    k_load(q + 2)

            def z_load(b):
                act.dma_start(zraw[:, :, :], z_d[b].rearrange("c p t -> p c t")).then_inc(s_zld, 16)

            def z_high(b):
                act.wait_ge(s_zld, 16 * (b + 1))
                copy(z_hi[b % 2][:, :, :], zraw[:, :, :]).then_inc(s_zhi, 1)

            def g_load(n):
                b, d = divmod(n, KT)
                act.dma_start(gt[:, n % 4, :], gate_d[GATE_OF[b] * KT + d]).then_inc(s_gld[n % 4], 16)

            act.wait_ge(s_prlo, KT)
            z_load(0)
            for n in range(4):
                g_load(n)
            for t in range(KT):
                act.wait_ge(s_used, CK_IDFT + 2 * t + 2)
                if t >= 2:
                    act.wait_ge(s_idt, t - 1)
                copy(y_t[:, t % 2, :], bank(t % 2)).then_inc(s_idev, 1)
                if t == 1:
                    z_high(0)
                if t >= 2:
                    act.wait_ge(s_idz, t - 1)
                    act.dma_start(z_d[Z_HY].rearrange("c p t -> p c t")[:, :, (t - 2) * P:(t - 1) * P],
                                  y_w[:, t % 2, :, :]).then_inc(s_idst[t % 2], 16)
            for t in (KT - 2, KT - 1):
                act.wait_ge(s_idz, t + 1)
                act.dma_start(z_d[Z_HY].rearrange("c p t -> p c t")[:, :, t * P:(t + 1) * P],
                              y_w[:, t % 2, :, :]).then_inc(s_idst[t % 2], 16)

            for n in range(NBR * KT):
                b, d = divmod(n, KT)
                if d == 0 and b + 1 < NBR:
                    act.wait_ge(s_zlo, b + 1)
                    if b + 1 == Z_HY:
                        act.wait_ge(s_idst[0], 16 * KT // 2)
                        act.wait_ge(s_idst[1], 16 * KT // 2)
                    z_load(b + 1)
                    act.wait_ge(s_used, CK_Y + NB * b)
                    z_high(b + 1)
                act.wait_ge(s_yev, n + 1)
                if n + 4 < NBR * KT:
                    g_load(n + 4)
                if b == NBR - 1:
                    act.wait_ge(s_mg, d + 1)
                    copy(m_hi[:, d, :], mrg[:, d, :]).then_inc(s_mhi, 1)

            act.wait_ge(s_used, CK_WO)
            act.dma_start(x1[:, :, :], xc.rearrange("k p t -> p k t")[:, :, 0:T]).then_inc(s_x1, 16)
            for d in range(KT):
                act.wait_ge(s_woev, d + 1)
                if d >= 2:
                    act.wait_ge(s_one2, d - 1)
                func(sq2[:, d % 2, :], x1[:, d, :], ACT.Square).then_inc(s_sq2, 1)
            act.wait_ge(s_v2, 1)
            log_rsqrt(r2[:, :], bank(4, 2), D).then_inc(s_r2, 1)
            for k in range(KT):
                act.wait_ge(s_t2, k + 1)
                own.done(func(ht[:, k % 2, :], ht[:, k % 2, :], ACT.Identity, bias=mod[:, 3 * KT + k, 0:1]))
                copy(h2_hi[:, k, :], ht[:, k % 2, :]).then_inc(s_h2h, 1)

            m, base = 0, CK_FFN
            for g, gn in enumerate(FGROUPS):
                for i in range(gn):
                    act.wait_ge(s_used, base + 2 * i + 1)
                    if m:
                        act.wait_ge(s_up, m)
                    func(sg[:, :], bank(0, 2), ACT.Silu).then_inc(s_sil, 1)
                    act.wait_ge(s_up, m + 1)
                    copy(g_hi[:, i, :], gm[:, :]).then_inc(s_ghi, 1)
                    m += 1
                base += 2 * gn + KT

        @block.vector
        def _(dve):
            own = Steps(dve, s_dve)
            tt, ts, stt = nc.vector.tensor_tensor, nc.vector.tensor_scalar, nc.vector.scalar_tensor_tensor

            def low(o, x, hi):
                return tt(o, x, hi.bitcast(F32), ALU.subtract)

            def refine(r, v, t):
                own.done(stt(out=t, in0=r, scalar=-0.5, in1=r, op0=ALU.mult, op1=ALU.mult))
                own.done(tt(t, t, v, ALU.mult))
                own.done(stt(out=r, in0=t, scalar=1.5, in1=r, op0=ALU.add, op1=ALU.mult))

            def mean_eps(v, sums, n):
                return ts(v, sums, 1.0 / n, EPS, ALU.mult, ALU.add)

            dve.wait_ge(s_filt, 16)
            w4 = f_sb[:, T:2 * T]
            own.done(tt(f_w4[:, 0, :], w4[:, 0:DB], w4[:, DB:2 * DB], ALU.add))
            tt(f_w4[:, 1, :], w4[:, 0:DB], w4[:, DB:2 * DB], ALU.subtract).then_inc(s_w4, 1)
            dve.wait_ge(s_const, 32)
            nc.vector.tensor_copy(altr[:, :], m_sb[:, M_ALT, :]).then_inc(s_alt, 1)
            own.done(ts(qg8[:, :], vcol("qg"), HD ** -0.5, None, ALU.mult))
            dve.wait_ge(s_csg, 1)
            tt(cs[:, :], csg[:, :], vcol("c", 0, 2 * KT), ALU.mult).then_inc(s_cs, 1)

            magic = float(1.5 * 2 ** 23)
            p1 = 6.28125
            p2 = float(np.float32(np.round((2 * np.pi - p1) * 2 ** 21) / 2 ** 21))
            p3 = float(np.float32(2 * np.pi - p1 - p2))
            for n in range(3):
                dve.wait_ge(s_fmm, n + 1)
                own.done(ts(f_a[:, :], bank(4, 2)[0:64, :], vcol("fb", n)[0:64, :], vcol("freq")[0:64, :],
                            ALU.add, ALU.mult))
                own.done(ts(f_k[:, :], f_a[:, :], float(1 / (2 * np.pi)), magic, ALU.mult, ALU.add))
                own.done(ts(f_k[:, :], f_k[:, :], magic, None, ALU.subtract))
                for part in (p1, p2, p3):
                    own.done(stt(out=f_a[:, :], in0=f_k[:, :], scalar=-part, in1=f_a[:, :], op0=ALU.mult, op1=ALU.add))
                ts(f_a[:, :], f_a[:, :], 3.1415925, -3.1415925, ALU.min, ALU.max).then_inc(s_fred, 1)

            def mod_out(a, b):
                for s in range(2):
                    ins = tt(mod[:, a:b, s], ps[:, 6 * HALF + 2 * a + s:6 * HALF + 2 * b:2], vcol("bmod", a, b - a), ALU.add)
                return ins

            dve.wait_ge(s_mused, 2 * KT)
            mod_out(0, 2 * KT).then_inc(s_mod1, 1)
            dve.wait_ge(s_mod1, 1)
            for s in range(2):
                own.done(stt(out=aff[:, :, s], in0=mod[:, KT:2 * KT, s], scalar=1.0, in1=vcol("g1", 0, KT),
                             op0=ALU.add, op1=ALU.mult))
            dve.wait_ge(s_ss, KT)
            mean_eps(nv[:, :], bank(0, width=TC), D).then_inc(s_nv, 1)
            dve.wait_ge(s_win, 16)

            def eo_low(t):
                dve.wait_ge(s_eohi, t + 1)
                low(e_lo[:, t, :], eo[:, t % 2, 0, :], e_hi[:, t, :])
                low(o_lo[:, t, :], eo[:, t % 2, 1, :], o_hi[:, t, :]).then_inc(s_eolo, 1)
                dve.wait_ge(s_eolo, t + 1)

            for t in range(KT):
                for part in range(2):
                    dve.wait_ge(s_eomm, 2 * t + part + 1)
                    tt(eo[:, t % 2, part, :], bank(4 + part), win_sb[:, t, :], ALU.mult).then_inc(s_eoev, 1)
                dve.wait_ge(s_eoev, 2 * t + 2)
                if t == 0:
                    e0, o0 = eo[0:1, 0, 0, :], eo[0:1, 0, 1, :]
                    own.done(tt(e0, e0, o0, ALU.add))
                    own.done(ts(e0, e0, 0.5, None, ALU.mult))
                nc.vector.tensor_copy(st_m[:, 0:1], vcol("eps")).then_inc(s_eo, 1)
                dve.wait_ge(s_eo, t + 1)
                if t:
                    eo_low(t - 1)
            eo_low(KT - 1)

            dve.wait_ge(s_nv, 1)
            dve.wait_ge(s_r0, 1)
            refine(rstd[:, :], nv[:, :], nt[:, :])

            def h_low(k):
                dve.wait_ge(s_hh, k + 1)
                low(h_lo[:, k, :], xs[:, k % 2, 0:T], h_hi[:, k, :])
                low(c_lo[:, k, :], xs[:, k % 2, T:TC], c_hi[:, k, :]).then_inc(s_hlo, 1)
                dve.wait_ge(s_hlo, k + 1)

            for k in range(KT):
                dve.wait_ge(s_xs[k % 2], 16 * (KT // 2 + k // 2 + 1))
                for s, t in ((0, slice(0, T)), (1, slice(T, TC))):
                    ins = stt(out=xs[:, k % 2, t], in0=xs[:, k % 2, t], scalar=aff[:, k, s:s + 1], in1=rstd[:, t],
                              op0=ALU.mult, op1=ALU.mult)
                ins.then_inc(s_ht, 1)
                if k:
                    h_low(k - 1)
            h_low(KT - 1)

            dve.wait_ge(s_used, CK_IN)
            edge = CFK // 2
            nc.vector.memset(cfm[:, :, 0:edge], 0.0)
            nc.vector.memset(cfm[:, :, T + edge:T + 2 * edge], 0.0)
            nc.vector.memset(st[:, :, 0:1], 0.0)
            own.done(nc.vector.memset(st[:, :, T + 1:T + 2], 0.0))
            for c in range(NB):
                dve.wait_ge(s_ev, KT + 2 * c + 2)
                tt(cfm[:, c, edge:edge + T], st[:, 2 * c % 4, 1:T + 1], st[:, (2 * c + 1) % 4, 1:T + 1],
                   ALU.mult).then_inc(s_cfm, 1)

            def conv3(o, slot, name, n, first, ready):
                dve.wait_ge(s_ev, ready)
                own.done(ts(o, st[:, slot, 0:T], vcol(name, first), None, ALU.mult))
                own.done(stt(out=o, in0=st[:, slot, 1:T + 1], scalar=vcol(name, n + first), in1=o, op0=ALU.mult, op1=ALU.add))
                own.done(stt(out=o, in0=st[:, slot, 2:T + 2], scalar=vcol(name, 2 * n + first), in1=o, op0=ALU.mult, op1=ALU.add))

            for g in range(2 * NB):
                s0 = 3 * (g % 2)
                ready = KT + S_HY + 3 * g + 1
                if g:
                    dve.wait_ge(s_cvst, 16 * (2 * g if g <= NB else NB + g))
                if g < NB:
                    for j in range(3):
                        conv3(cvo[:, j, :], s0 + j, "chy", 3 * NB, j * NB + g, ready + j)
                    tt(cvo[:, 1, :], cvo[:, 1, :], cvo[:, 2, :], ALU.mult).then_inc(s_grpout, 1)
                else:
                    dve.wait_ge(s_ev, ready + 2)
                    own.done(tt(st[:, s0 + 2, 1:T + 1], st[:, s0 + 2, 1:T + 1], st[:, s0, 1:T + 1], ALU.mult))
                    conv3(cvo[:, 0, :], s0 + 2, "ca", NB, g - NB, ready + 2)
                    tt(cvo[:, 0, :], cvo[:, 0, :], st[:, s0 + 1, 1:T + 1], ALU.mult).then_inc(s_grpout, 1)
            dve.wait_ge(s_mused, 6 * KT)
            mod_out(2 * KT, 6 * KT).then_inc(s_modev, 1)

            for t in range(2 * NB):
                x = st[:, t % 6, 0:T]
                kc = cst[:, (t - NB) % 4, :]
                gain = qg8[:, :] if t < NB else vcol("kg")
                n = T if t < NB else TC
                dve.wait_ge(s_ev, KT + S_QKV + t + 1)
                ins = tt(q_t[:, 0:T], x, x, ALU.mult)
                if t >= NB:
                    dve.wait_ge(s_cev, t - NB + 1)
                    ins = tt(q_t[:, T:TC], kc, kc, ALU.mult)
                ins.then_inc(s_qsq, 1)
                dve.wait_ge(s_qones, t + 1)
                ins = mean_eps(q_v[:, 0:T], bank(6, 2), HD)
                if t >= NB:
                    ins = mean_eps(q_v[:, T:TC], bank(4 + t % 2)[:, C:2 * C], HD)
                ins.then_inc(s_qfree, 1)
                dve.wait_ge(s_qfree, t + 1)
                dve.wait_ge(s_qr, t + 1)
                refine(q_r[:, 0:n], q_v[:, 0:n], q_t[:, 0:n])
                ins = stt(out=x, in0=x, scalar=gain, in1=q_r[:, 0:T], op0=ALU.mult, op1=ALU.mult)
                if t >= NB:
                    ins = stt(out=kc, in0=kc, scalar=gain, in1=q_r[:, T:TC], op0=ALU.mult, op1=ALU.mult)
                ins.then_inc(s_qn, 1)
                dve.wait_ge(s_qn, t + 1)

            for c in range(NB):
                o = cfo[:, c, :]
                own.done(ts(o, cfm[:, c, 0:T], vcol("cd", c), vcol("cdb", c), ALU.mult, ALU.add))
                for j in range(1, CFK):
                    ins = stt(out=o, in0=cfm[:, c, j:j + T], scalar=vcol("cd", NB * j + c), in1=o, op0=ALU.mult, op1=ALU.add)
                    if j < CFK - 1:
                        own.done(ins)
                ins.then_inc(s_conv, 1)
            dve.wait_ge(s_conv, NB)
            dve.wait_ge(s_l1, 1)
            for c in range(NB):
                stt(out=cfo[:, c, :], in0=bank(4, 2), scalar=-1.0 / DB, in1=cfo[:, c, :], op0=ALU.mult,
                    op1=ALU.add).then_inc(s_lx, 1)
            dve.wait_ge(s_l2, NB)
            mean_eps(l_v[:, :], bank(6, 2), DB).then_inc(s_lf, 1)
            dve.wait_ge(s_lf, 1)
            dve.wait_ge(s_lr, 1)
            dve.wait_ge(s_lx, NB)
            refine(l_r[:, :], l_v[:, :], l_t[:, :])
            for c in range(NB):
                tt(cfo[:, c, :], cfo[:, c, :], l_r[:, :], ALU.mult).then_inc(s_ly, 1)
            for t in range(KT):
                dve.wait_ge(s_uhi, t + 1)
                low(u_lo[:, t, :], bank(t % 4), u_hi[:, t, :]).then_inc(s_ulo, 1)

            own.done(nc.vector.memset(a_b[:, LOC:KEYS], 0.0))
            dve.wait_ge(s_mask, 16)

            def softmax_in(g):
                hp, it = divmod(g, 16)
                e, rp = divmod(it, 8)
                if it == 0:
                    dve.wait_ge(s_ald, 96 * (hp + 1))
                if rp in MASKS:
                    x = (window_start(rp) - 2 * rp + WIN_H) * GRID
                    own.done(tt(a_b[:, 0:LOC], a_g[:, e, x:x + LOC], a_m[:, MASKS.index(rp), :], ALU.add))
                dve.wait_ge(s_as, g + 1)
                if g >= 2:
                    dve.wait_ge(s_aexp, g - 1)
                s = g % 2
                nc.vector.tensor_tensor_reduce(a_s[:, s, :], bank(2 * s, width=KEYS), a_b[:, :], 1.0, NEG, ALU.add,
                                               ALU.max, st_m[:, s:s + 1]).then_inc(s_attr, 1)
                dve.wait_ge(s_attr, g + 1)
                ts(st_nm[:, s:s + 1], st_m[:, s:s + 1], -1.0, None, ALU.mult).then_inc(s_anm, 1)

            def weights_out(g):
                s = g % 2
                dve.wait_ge(s_at, g + 1)
                if g >= 2:
                    dve.wait_ge(s_apv, g - 1)
                nc.vector.tensor_copy(a_pt[:, s, HALF:KEYS], bank(5, width=KEYS - HALF)).then_inc(s_aevd, 1)
                dve.wait_ge(s_aexp, g + 1)
                own.done(nc.vector.reciprocal(st_r[:, s:s + 1], st_l[:, s:s + 1]))

            def heads_out(g):
                hp, it = divmod(g, 16)
                e, rp = divmod(it, 8)
                s = g % 2
                dve.wait_ge(s_apv, g + 1)
                if it == 0 and hp:
                    dve.wait_ge(s_azt, hp)
                ts(a_o[:, rp, e * HD:(e + 1) * HD], bank(6 + s)[:, 0:HD], st_r[:, s:s + 1], None,
                   ALU.mult).then_inc(s_ao, 1)

            for hp in range(NB):
                g0 = 16 * hp
                for it in range(16):
                    softmax_in(g0 + it)
                    if it >= 2:
                        heads_out(g0 + it - 2)
                    if it:
                        weights_out(g0 + it - 1)
                heads_out(g0 + 14)
                weights_out(g0 + 15)
                heads_out(g0 + 15)

            def pr_low(q):
                dve.wait_ge(s_prhi, q + 1)
                low(pr_lo[:, q, :], pw[:, q % 2, 0, :], pr_hi[:, q, :])
                low(ps_lo[:, q, :], pw[:, q % 2, 2, :], ps_hi[:, q, :]).then_inc(s_prlo, 1)
                dve.wait_ge(s_prlo, q + 1)

            dve.wait_ge(s_zst, 16 * NB)
            dve.wait_ge(s_ao, 16 * NB)
            for q in range(KT):
                s = q % 2
                uc, us = bank(2 * s), bank(2 * s + 1)
                dve.wait_ge(s_k[s], 16 * (q // 2 + 1))
                kc, ks = k_sb[:, s, 0, :], k_sb[:, s, 1, :]
                dve.wait_ge(s_used, CK_UDFT + 2 * q + 1)
                own.done(tt(pw[:, s, 0, :], uc, kc, ALU.mult))
                own.done(tt(pw[:, s, 2, :], uc, ks, ALU.mult))
                dve.wait_ge(s_used, CK_UDFT + 2 * q + 2)
                own.done(tt(pw[:, s, 1, :], us, ks, ALU.mult))
                own.done(tt(pw[:, s, 3, :], us, kc, ALU.mult))
                own.done(tt(pw[:, s, 0, :], pw[:, s, 0, :], pw[:, s, 1, :], ALU.subtract))
                own.done(tt(pw[:, s, 2, :], pw[:, s, 2, :], pw[:, s, 3, :], ALU.add))
                if q == 0:
                    own.done(tt(pw[0:1, s, 0, :], uc[0:1, :], kc[0:1, :], ALU.mult))
                    own.done(tt(pw[0:1, s, 2, :], us[0:1, :], ks[0:1, :], ALU.mult))
                nc.vector.tensor_copy(st_m[:, 0:1], vcol("eps")).then_inc(s_udev, 1)
                nc.vector.tensor_copy(st_m[:, 1:2], vcol("eps")).then_inc(s_pr, 1)
                dve.wait_ge(s_pr, q + 1)
                if q:
                    pr_low(q - 1)
            pr_low(KT - 1)

            def z_low(b):
                dve.wait_ge(s_zhi, b + 1)
                low(z_lo[b % 2][:, :, :], zraw[:, :, :], z_hi[b % 2][:, :, :]).then_inc(s_zlo, 1)

            dve.wait_ge(s_x0, 16)
            for t in range(KT):
                s = t % 2
                dve.wait_ge(s_idt, t + 1)
                if t >= 2:
                    dve.wait_ge(s_idst[s], 16 * (t // 2))
                tsl = slice(t * P, (t + 1) * P)
                for c in range(NB):
                    ins = stt(out=y_w[:, s, c, :], in0=u_f[:, c, tsl], scalar=vcol("skip", c),
                              in1=bank(4 + s)[:, c * P:(c + 1) * P], op0=ALU.mult, op1=ALU.add)
                own.done(ins)
                tt(y_w[:, s, :, :], y_w[:, s, :, :], x0_f[:, :, tsl], ALU.mult).then_inc(s_idz, 1)
                if t == 2:
                    z_low(0)

            for n in range(NBR * KT):
                b, d = divmod(n, KT)
                b0 = 2 * (d % 2)
                dve.wait_ge(s_gld[n % 4], 16 * (n // 4 + 1))
                if d % 2 == 0:
                    dve.wait_ge(s_y, n // 2 + 1)
                else:
                    dve.wait_ge(s_used, CK_Y + n // 2 + 1)
                if b == 0:
                    tt(mrg[:, d, :], bank(b0, 2), gt[:, n % 4, :], ALU.mult).then_inc(s_yev, 1)
                    dve.wait_ge(s_yev, n + 1)
                else:
                    tt(yt[:, :], bank(b0, 2), gt[:, n % 4, :], ALU.mult).then_inc(s_yev, 1)
                    dve.wait_ge(s_yev, n + 1)
                    own.done(tt(mrg[:, d, :], mrg[:, d, :], yt[:, :], ALU.add))
                if b == NBR - 1:
                    nc.vector.tensor_copy(st_m[:, 0:1], vcol("eps")).then_inc(s_mg, 1)
                    if d:
                        dve.wait_ge(s_mhi, d)
                        low(m_lo[:, d - 1, :], mrg[:, d - 1, :], m_hi[:, d - 1, :]).then_inc(s_mlo, 1)
                if b + 1 < NBR and d == 4:
                    z_low(b + 1)
            dve.wait_ge(s_mhi, KT)
            low(m_lo[:, KT - 1, :], mrg[:, KT - 1, :], m_hi[:, KT - 1, :]).then_inc(s_mlo, 1)

            own.done(stt(out=aff2[:, :], in0=mod[:, 4 * KT:5 * KT, 0], scalar=1.0, in1=vcol("g2", 0, KT),
                         op0=ALU.add, op1=ALU.mult))
            dve.wait_ge(s_x1, 16)
            for d in range(KT):
                dve.wait_ge(s_used, CK_WO + d + 1)
                stt(out=x1[:, d, :], in0=bank(2 * (d % 2), 2), scalar=mod[:, 2 * KT + d, 0:1], in1=x1[:, d, :],
                    op0=ALU.mult, op1=ALU.add).then_inc(s_woev, 1)
            dve.wait_ge(s_one2, KT)
            mean_eps(v2[:, :], bank(4, 2), D).then_inc(s_v2, 1)
            dve.wait_ge(s_v2, 1)
            dve.wait_ge(s_r2, 1)
            refine(r2[:, :], v2[:, :], t2[:, :])

            def h2_low(k):
                dve.wait_ge(s_h2h, k + 1)
                low(h2_lo[:, k, :], ht[:, k % 2, :], h2_hi[:, k, :]).then_inc(s_h2, 1)
                dve.wait_ge(s_h2, k + 1)

            dve.wait_ge(s_woev, KT)
            for k in range(KT):
                stt(out=ht[:, k % 2, :], in0=x1[:, k, :], scalar=aff2[:, k:k + 1], in1=r2[:, :], op0=ALU.mult,
                    op1=ALU.mult).then_inc(s_t2, 1)
                if k:
                    h2_low(k - 1)
            h2_low(KT - 1)

            m, base = 0, CK_FFN
            for g, gn in enumerate(FGROUPS):
                for i in range(gn):
                    dve.wait_ge(s_sil, m + 1)
                    dve.wait_ge(s_used, base + 2 * i + 2)
                    if m:
                        dve.wait_ge(s_ghi, m)
                    tt(gm[:, :], bank(2, 2), sg[:, :], ALU.mult).then_inc(s_up, 1)
                    dve.wait_ge(s_up, m + 1)
                    dve.wait_ge(s_ghi, m + 1)
                    low(g_lo[:, i, :], gm[:, :], g_hi[:, i, :]).then_inc(s_glo, 1)
                    dve.wait_ge(s_glo, m + 1)
                    m += 1
                base += 2 * gn
                for d in range(KT):
                    dve.wait_ge(s_used, base + d + 1)
                    stt(out=x1[:, d, :], in0=bank(4 + 2 * (d % 2), 2), scalar=mod[:, 5 * KT + d, 0:1],
                        in1=x1[:, d, :], op0=ALU.mult, op1=ALU.add).then_inc(s_foev, 1)
                    dve.wait_ge(s_foev, KT * g + d + 1)
                base += KT


def _tiles(v):
    return np.ascontiguousarray(v.reshape(-1, P).T)


def _chunk(wt):
    k = wt.shape[0] // P
    o = np.zeros((P, 8, P), np.float32)
    o[:, :k] = wt.reshape(k, P, P).transpose(1, 0, 2)
    return o.reshape(P, CH)


def _tables():
    n = np.arange(T)
    th = 2 * np.pi * ((n[:, None] * n[None, :]) % (2 * T)) / (2 * T)
    alt = np.where(n % 2 == 0, 1.0, -1.0)
    cf, sf = np.cos(th), np.sin(th)
    sf[:, 0] = alt
    ci, si = np.cos(th) / T, np.sin(th) / T
    ci[0] /= 2
    si[0] = alt / (2 * T)
    return [a.astype(np.float32) for a in (cf, sf, ci, si)]


def _chunks(w_in, w_a, w_cf, w_na, w_hy, w_o, w_fi, w_fo):
    cf, sf, ci, si = _tables()
    cols = lambda a, j: a[:, j * P:(j + 1) * P]
    spectrum = [_chunk(cols(a, j)) for j in range(KT) for a in (cf, sf)]
    off_a, off_q = 0, 3 * DB
    off_hy = off_q + 3 * DB
    off_cf = off_hy + 3 * DB
    off_g = off_cf + 2 * DB
    starts = [off_cf + DB * h + c * P for c in range(NB) for h in range(2)]
    starts += [off_hy + DB * h + c * P for c in range(NB) for h in range(3)]
    starts += [off_a + DB * h + c * P for c in range(NB) for h in range(3)]
    starts += [off_q + c * P for c in range(3 * NB)]
    starts += [off_g + c * P for c in range(N_G)]
    strips = [_chunk(w_in[:, s:s + P]) for s in starts]
    inverse = [_chunk(cols(a, j)) for j in range(KT) for a in (ci, si)]
    branch = [_chunk(np.concatenate([cols(b, 2 * m), cols(b, 2 * m + 1)], 0))
              for b in (w_a, w_cf, w_na, w_hy) for m in range(NB)]
    proj = [_chunk(cols(w_o, d)) for d in range(KT)]
    ffn, m = [], 0
    for gn in FGROUPS:
        for i in range(m, m + gn):
            ffn += [_chunk(cols(w_fi, i)), _chunk(cols(w_fi, FFT + i))]
        ffn += [_chunk(w_fo[m * P:(m + gn) * P, d * P:(d + 1) * P]) for d in range(KT)]
        m += gn
    return np.stack(spectrum + strips + spectrum + inverse + branch + proj + ffn)


def _filter_inputs(w1, w2, w3, w4):
    bands = 16
    t = np.linspace(0.0, 1.0, T, dtype=np.float32)[:, None]
    wv = (2.0 * np.pi * np.arange(T, dtype=np.float32)[:, None] / T).astype(np.float32)
    f = np.linspace(1e-4, bands - 1, bands, dtype=np.float32)[None, :]
    z = np.concatenate([t, np.cos(f * wv), -np.sin(f * wv)], -1).astype(np.float32)
    o = np.zeros((64, 2 * T + 192), np.float32)
    o[0:33, 0:T] = z.T
    o[:, T:2 * T] = w4
    o[0:33, 2 * T:2 * T + 64] = w1
    o[:, 2 * T + 64:2 * T + 128] = w2
    o[:, 2 * T + 128:] = w3
    deltas = np.abs(np.linspace(np.log(1e-2) / 1.5, np.log(1e-2) / 0.3, DB, dtype=np.float32))
    win = (np.exp(-t * deltas[None, :]) + np.float32(0.05)).astype(np.float32)
    return o, np.ascontiguousarray(win.reshape(KT, P, DB).transpose(1, 0, 2))


def _bias_tables(rpb):
    q = np.arange(P)
    half, col = q // GRID, q % GRID
    padded = np.pad(rpb, ((0, 0), (2, 2), (GRID - WIN_W, GRID - WIN_W)))
    x = np.arange(XR)
    dr = x[None, :] + 1 - half[:, None]
    dc = np.arange(GRID)[None, :] - col[:, None] + GRID - 1
    table = padded[:, dr[:, :, None], dc[:, None, :]]
    mask = np.full((P, len(MASKS), NROW, GRID), NEG, np.float32)
    for n, rp in enumerate(MASKS):
        for p in range(P):
            r = 2 * rp + half[p]
            r0 = min(max(r - WIN_H // 2, 0), ROWS - WIN_H) - window_start(rp)
            c0 = min(max(col[p] - WIN_W // 2, 0), GRID - WIN_W)
            mask[p, n, r0:r0 + WIN_H, c0:c0 + WIN_W] = 0.0
    return (np.ascontiguousarray(table.reshape(HEADS, P, XR * GRID)),
            np.ascontiguousarray(mask.reshape(P, len(MASKS), LOC)))


def kernel(x, c, ctx, c_ctx, w_mod, b_mod, g_norm1, g_norm2, w_in, conv_a, w_a_out, q_gain, k_gain, rpb,
           w_na_out, conv_h, filt_w1, filt_b1, filt_w2, filt_b2, filt_w3, filt_b3, filt_w4, filt_freq,
           hy_skip, w_h_out, conv_d, conv_d_b, ln_g, ln_b, w_d_out, w_o, w_ffn_in, w_ffn_out):
    import concourse.bacc as _bacc
    from concourse.bass_utils import run_bass_kernel_spmd as _run

    a = lambda v: np.asarray(v)
    tall = lambda v: np.concatenate([a(v)[0], np.zeros(P - 64, np.float32)])[:, None]
    vec = np.concatenate([
        _tiles(a(g_norm1)[0]), _tiles(a(g_norm2)[0]), np.tile(a(q_gain)[0], 2)[:, None],
        np.tile(a(k_gain)[0], 2)[:, None], _tiles(a(conv_a)[0]), _tiles(a(conv_h)[0]), _tiles(a(hy_skip)[0]),
        _tiles(a(conv_d)[0]), _tiles(a(conv_d_b)[0]), _tiles(a(ln_g)[0]), _tiles(a(ln_b)[0]),
        _tiles(a(b_mod)[0]), np.stack([_tiles(a(c)[0]), _tiles(a(c_ctx))], -1).reshape(P, 2 * KT),
        tall(filt_b1), tall(filt_b2), tall(filt_b3), tall(filt_freq), np.full((P, 1), EPS, np.float32)], 1)
    assert vec.shape[1] == NVEC
    mats = np.zeros((P, 4, P), np.float32)
    mats[:, M_ID] = np.eye(P)
    mats[:, M_ONE] = 1.0
    mats[0:HD, M_HEAD, 0:HD] = 1.0
    mats[HD:, M_HEAD, HD:] = 1.0
    mats[:, M_ALT] = np.where(np.arange(P) % 2 == 0, 1.0, -1.0)[:, None]
    filt, win = _filter_inputs(a(filt_w1)[0], a(filt_w2)[0], a(filt_w3)[0], a(filt_w4)[0])
    gat, masks = _bias_tables(a(rpb)[0])
    arrays = {
        "w": _chunks(a(w_in)[0], a(w_a_out)[0], a(w_d_out)[0], a(w_na_out)[0], a(w_h_out)[0], a(w_o)[0],
                     a(w_ffn_in)[0], a(w_ffn_out)[0]),
        "wmod": np.stack([_chunk(a(w_mod)[0][:, j * P:(j + 1) * P]) for j in range(6 * KT)]),
        "xc": np.ascontiguousarray(np.concatenate([a(x)[0], a(ctx)[0]], 0).T.reshape(KT, P, TC)),
        "vec": np.ascontiguousarray(vec), "mats": mats, "filt": filt, "win": win, "gat": gat, "masks": masks,
    }
    nc = _bacc.Bacc("TRN2", target_bir_lowering=False, num_devices=1)
    args = {n: nc.dram_tensor(f"in_{n}", v.shape, mybir.dt.from_np(v.dtype), kind="ExternalInput").ap()
            for n, v in arrays.items()}
    out = nc.dram_tensor("out", (KT, P, T), F32, kind="ExternalOutput").ap()
    layer_program(nc, **args, out=out)
    r = _run(nc, [{f"in_{n}": v for n, v in arrays.items()}], core_ids=[0])
    return np.ascontiguousarray(r.results[0]["out"].reshape(D, T).T)[None]
```

```python
from contextlib import ExitStack, contextmanager

import numpy as np
import concourse.bass as bass
from concourse import mybir

F32 = mybir.dt.float32
F32R = mybir.dt.float32r
ALU = mybir.AluOpType
ACT = mybir.ActivationFunctionType

P = 128
T = 1024
C = 256
TC = T + C
D = 1024
KT = D // P
DB = 512
NB = DB // P
HALF = 512
HD = 64
HEADS = 8
GRID = 64
ROWS = T // GRID
WIN_H, WIN_W = 8, 16
NROW = 10
LOC = NROW * GRID
KEYS = LOC + C
XR = 18
EPS = 1e-6
NEG = -1e30
FF = 2816
FFT = FF // P
FGROUPS = (8, 7, 7)
CFK = 31
NBR = 4
CH = 8 * P

CK_KDFT = 0
CK_IN = CK_KDFT + 2 * KT
N_CF, N_HY, N_A, N_QKV, N_G = 2 * NB, 3 * NB, 3 * NB, 3 * NB, NBR * KT
S_HY = N_CF
S_A = S_HY + N_HY
S_QKV = S_A + N_A
S_G = S_QKV + N_QKV
N_STRIP = S_G + N_G
CK_UDFT = CK_IN + N_STRIP
CK_IDFT = CK_UDFT + 2 * KT
CK_Y = CK_IDFT + 2 * KT
CK_WO = CK_Y + NBR * NB
CK_FFN = CK_WO + KT
N_CHUNK = CK_FFN + 2 * FFT + KT * len(FGROUPS)
assert N_CHUNK % 4 == 0 and CK_IN % 4 == 0

GATE_OF = (0, 3, 1, 2)
Z_A, Z_CF, Z_NA, Z_HY = range(4)

VEC = {}
_at = 0
for _name, _n in (("g1", KT), ("g2", KT), ("qg", 1), ("kg", 1), ("ca", 3 * NB), ("chy", 9 * NB),
                  ("skip", NB), ("cd", CFK * NB), ("cdb", NB), ("lng", NB), ("lnb", NB),
                  ("bmod", 6 * KT), ("c", 2 * KT), ("fb", 3), ("freq", 1), ("eps", 1)):
    VEC[_name] = _at
    _at += _n
NVEC = _at

M_ID, M_ONE, M_HEAD, M_ALT = range(4)


def window_start(rp):
    return min(max(2 * rp - WIN_H // 2, 0), ROWS - NROW)


MASKS = (0, 2, ROWS // 2 - 1)
MASK_OF = {0: 0, 1: 0, 2: 1, ROWS // 2 - 2: 2, ROWS // 2 - 1: 2}


class Steps:

    def __init__(self, eng, sem):
        self.eng, self.sem, self.base, self.n = eng, sem, 0, 0

    def mark(self, ins):
        self.n += 1
        ins.then_inc(self.sem, 1)

    def wait(self):
        self.eng.wait_ge(self.sem, self.base + self.n)

    def done(self, ins):
        self.mark(ins)
        self.wait()

    @contextmanager
    def loop(self, count, per):
        start = self.base + self.n
        with self.eng.Fori(0, count) as i:
            self.base, self.n = start + i * per, 0
            yield i
            assert self.n == per, self.n
        self.base, self.n = start + count * per, 0


def layer_program(nc, w, wmod, xc, vec, mats, filt, win, gat, masks, out):
    kspec = nc.dram_tensor("kspec", (KT, P, 2, DB), F32, kind="Internal").ap()
    x0_d = nc.dram_tensor("x0_d", (NB, P, T), F32, kind="Internal").ap()
    u_d = nc.dram_tensor("u_d", (NB, P, T), F32, kind="Internal").ap()
    q_d = [nc.dram_tensor(f"q_{n}_d", (NB, P, T), F32, kind="Internal").ap() for n in ("hi", "lo")]
    k_d = [nc.dram_tensor(f"k_{n}_d", (NB, P, TC), F32, kind="Internal").ap() for n in ("hi", "lo")]
    v_d = nc.dram_tensor("v_d", (NB, P, T), F32, kind="Internal").ap()
    vc_d = nc.dram_tensor("vc_d", (NB, P, C), F32, kind="Internal").ap()
    gate_d = nc.dram_tensor("gate_d", (NBR * KT, P, T), F32, kind="Internal").ap()
    z_d = nc.dram_tensor("z_d", (NBR, NB, P, T), F32, kind="Internal").ap()

    with ExitStack() as ctx:
        def sb(name, shape, dt=F32):
            return ctx.enter_context(nc.sbuf_tensor(name, shape, dt))

        def sem(name):
            return ctx.enter_context(nc.semaphore(name))

        v_sb = sb("v_sb", [P, NVEC])
        m_sb = sb("m_sb", [P, 4, P])
        altr = sb("altr", [P, P], F32R)
        cs = sb("cs", [P, 2 * KT])
        csg = sb("csg", [P, 2 * KT])
        mod = sb("mod", [P, 6 * KT, 2])
        aff = sb("aff", [P, KT, 2])
        aff2 = sb("aff2", [P, KT])
        qg8 = sb("qg8", [P, 1])
        gate0 = sb("gate0", [P, 2])
        st_nm = sb("st_nm", [P, 2])
        st_m = sb("st_m", [P, 2])
        st_l = sb("st_l", [P, 2])
        st_r = sb("st_r", [P, 2])
        ident = m_sb[:, M_ID, :]
        ones = m_sb[:, M_ONE, :]
        heads = m_sb[:, M_HEAD, :]

        floor = (nc.sbuf_base + 63) // 64 * 64
        room = nc.sbuf_usable_end - floor
        KB = 1024

        def at(name, kb, shape, dt=F32):
            size = int(np.prod(shape[1:])) * 4
            off = int(kb * KB)
            assert off + size <= room, (name, off + size, room)
            return nc.alloc_sbuf_tensor_at(name, shape, dt, offset=floor + off)

        raw = at("raw", 0, [P, 4, CH])
        whi = at("whi", 16, [P, 2, CH], F32R)
        wlo = at("wlo", 24, [P, 2, CH], F32R)
        h_hi = at("h_hi", 32, [P, KT, T], F32R)
        h_lo = at("h_lo", 64, [P, KT, T], F32R)
        c_hi = at("c_hi", 96, [P, KT, C], F32R)
        c_lo = at("c_lo", 104, [P, KT, C], F32R)
        mraw = at("mraw", 112, [P, 2, CH])
        mprod = at("mprod", 199, [P, CH])
        macc = at("macc", 152, [P, 2, P])
        e_hi = at("e_hi", 120, [P, KT, DB], F32R)
        e_lo = at("e_lo", 136, [P, KT, DB], F32R)
        o_hi = at("o_hi", 152, [P, KT, DB], F32R)
        o_lo = at("o_lo", 168, [P, KT, DB], F32R)
        xs = at("xs", 184, [P, 2, TC])
        hx = [xs[:, 0, :], xs[:, 1, :], at("hx2", 112, [P, TC])[:, :]]
        rstd = at("rstd", 194, [P, TC])
        ksp = at("ksp", 199, [P, 2, DB])
        f_sb = at("f_sb", 32, [64, 2 * T + 3 * 64])
        f_w4 = at("f_w4", 41, [64, 2, DB])
        f_a = at("f_a", 45, [64, T])
        f_k = at("f_k", 49, [64, T])
        f_h = at("f_h", 53, [64, T])
        eo = at("eo", 57, [P, 2, 2, DB])
        win_sb = at("win_sb", 65, [P, KT, DB])
        nv = at("nv", 82, [P, TC])
        nt = at("nt", 88, [P, TC])
        cfm = at("cfm", 120, [P, NB, T + CFK - 1])
        cfo = at("cfo", 136.5, [P, NB, T])
        st = at("st", 153, [P, 6, T + 8])
        cvo = at("cvo", 178, [P, 3, T])
        n_hi = at("n_hi", 178, [P, 2, TC], F32R)
        n_lo = at("n_lo", 188, [P, 2, TC], F32R)
        cst = at("cst", 198, [P, 4, C])
        q_t = at("q_t", 137, [P, TC])
        q_r = at("q_r", 142, [P, TC])
        q_v = at("q_v", 147, [P, TC])
        lsq = at("lsq", 96, [P, NB, T])
        l_r = at("l_r", 120, [P, T])
        l_v = at("l_v", 124, [P, T])
        l_t = at("l_t", 128, [P, T])
        u_f = at("u_f", 185, [P, NB, T])
        u_hi = at("u_hi", 153, [P, KT, DB], F32R)
        u_lo = at("u_lo", 169, [P, KT, DB], F32R)
        a_m = at("a_m", 96, [P, len(MASKS), LOC])
        a_vt = at("a_vt", 103.5, [P, 10, P])
        a_o = at("a_o", 115.5, [P, ROWS // 2, P])
        a_pt = at("a_pt", 108.5, [P, 2, KEYS])
        gst = at("gst", 152.5, [P, 2, T])
        a_q = [at(f"a_q{e}", 160.5 + 4 * e, [P, T], F32R) for e in range(2)]
        a_k = [at(f"a_k{e}", 168.5 + 5 * e, [P, TC], F32R) for e in range(2)]
        a_kl = at("a_kl", 178.5, [P, TC], F32R)
        a_v = at("a_v", 164.5, [P, T])
        a_vc = at("a_vc", 173.5, [P, C])
        a_g = [at(f"a_g{e}", 183.5 + 4.5 * e, [P, XR * GRID]) for e in range(2)]
        a_s = at("a_s", 192.5, [P, 2, KEYS])
        a_b = at("a_b", 199.5, [P, KEYS])
        pr_hi = at("pr_hi", 32, [P, KT, DB], F32R)
        pr_lo = at("pr_lo", 48, [P, KT, DB], F32R)
        ps_hi = at("ps_hi", 64, [P, KT, DB], F32R)
        ps_lo = at("ps_lo", 80, [P, KT, DB], F32R)
        k_sb = at("k_sb", 96, [P, 2, 2, DB])
        pw = at("pw", 136, [P, 2, 4, DB])
        x0_f = at("x0_f", 120, [P, NB, T])
        y_t = at("y_t", 112, [P, 2, DB])
        y_w = at("y_w", 116, [P, 2, NB, P])
        z_hi = [at("z_hi0", 153, [P, NB, T], F32R), at("z_hi1", 32, [P, NB, T], F32R)]
        z_lo = [at("z_lo0", 169, [P, NB, T], F32R), at("z_lo1", 48, [P, NB, T], F32R)]
        mrg = at("mrg", 64, [P, KT, T])
        gt = at("gt", 96, [P, 4, T])
        zraw = at("zraw", 136, [P, NB, T])
        yt = at("yt", 185, [P, T])
        m_hi = at("m_hi", 120, [P, KT, T], F32R)
        m_lo = at("m_lo", 152, [P, KT, T], F32R)
        x1 = at("x1", 32, [P, KT, T])
        sq2 = at("sq2", 96, [P, 2, T])
        r2 = at("r2", 185, [P, T])
        v2 = at("v2", 189, [P, T])
        t2 = at("t2", 193, [P, T])
        h2_hi = at("h2_hi", 64, [P, KT, T], F32R)
        h2_lo = at("h2_lo", 96, [P, KT, T], F32R)
        ht = at("ht", 160, [P, 4, HALF])
        g_hi = at("g_hi", 128, [P, 8, T], F32R)
        g_lo = at("g_lo", 160, [P, 8, T], F32R)
        sg = at("sg", 192, [P, T])
        gm = at("gm", 196, [P, T])

        ps = ctx.enter_context(nc.psum_tensor("ps", [P, 8 * HALF], F32))

        def bank(b, n=1, width=None):
            return ps[:, b * HALF:b * HALF + (width or n * HALF)]

        s_const = sem("s_const")
        s_filt = sem("s_filt")
        s_win = sem("s_win")
        s_raw = [sem(f"s_raw{i}") for i in range(4)]
        s_hi = sem("s_hi")
        s_split = sem("s_split")
        s_used = sem("s_used")
        s_gate = sem("s_gate")
        s_mraw = [sem(f"s_mraw{i}") for i in range(2)]
        s_mused = sem("s_mused")
        s_csg = sem("s_csg")
        s_cs = sem("s_cs")
        s_xs = [sem(f"s_xs{i}") for i in range(2)]
        s_hx = [sem(f"s_hx{i}") for i in range(3)]
        s_sq = sem("s_sq")
        s_ss = sem("s_ss")
        s_fmm = sem("s_fmm")
        s_fred = sem("s_fred")
        s_fsin = sem("s_fsin")
        s_w4 = sem("s_w4")
        s_eomm = sem("s_eomm")
        s_eoev = sem("s_eoev")
        s_eo = sem("s_eo")
        s_eohi = sem("s_eohi")
        s_eolo = sem("s_eolo")
        s_alt = sem("s_alt")
        s_ny = sem("s_ny")
        s_r0 = sem("s_r0")
        s_nv = sem("s_nv")
        s_ht = sem("s_ht")
        s_hh = sem("s_hh")
        s_hlo = sem("s_hlo")
        s_ev = sem("s_ev")
        s_kst = sem("s_kst")
        s_pad = sem("s_pad")
        s_cfm = sem("s_cfm")
        s_grpout = sem("s_grpout")
        s_cvst = sem("s_cvst")
        s_cacc = sem("s_cacc")
        s_cev = sem("s_cev")
        s_qsq = sem("s_qsq")
        s_qones = sem("s_qones")
        s_qr = sem("s_qr")
        s_qfree = sem("s_qfree")
        s_qn = sem("s_qn")
        s_nh = sem("s_nh")
        s_nl = sem("s_nl")
        s_nst = [sem(f"s_nst{i}") for i in range(2)]
        s_vst = sem("s_vst")
        s_gst = [sem(f"s_gst{i}") for i in range(2)]
        s_gh = sem("s_gh")
        s_macc = sem("s_macc")
        s_mfree = sem("s_mfree")
        s_modev = sem("s_modev")
        s_conv = sem("s_conv")
        s_l1 = sem("s_l1")
        s_lx = sem("s_lx")
        s_lsq = sem("s_lsq")
        s_l2 = sem("s_l2")
        s_lr = sem("s_lr")
        s_lf = sem("s_lf")
        s_ly = sem("s_ly")
        s_lz = sem("s_lz")
        s_zst = sem("s_zst")
        s_uld = sem("s_uld")
        s_ut = sem("s_ut")
        s_uhi = sem("s_uhi")
        s_ulo = sem("s_ulo")
        s_hld = [sem(f"s_hld{i}") for i in range(2)]
        s_vld = sem("s_vld")
        s_avt = sem("s_avt")
        s_avev = sem("s_avev")
        s_as = sem("s_as")
        s_attr = sem("s_attr")
        s_anm = sem("s_anm")
        s_aexp = sem("s_aexp")
        s_at = sem("s_at")
        s_aeva = sem("s_aeva")
        s_aevd = sem("s_aevd")
        s_apv = sem("s_apv")
        s_ao = sem("s_ao")
        s_azt = sem("s_azt")
        s_azev = sem("s_azev")
        s_azst = sem("s_azst")
        s_k = [sem(f"s_k{i}") for i in range(2)]
        s_ud = sem("s_ud")
        s_udev = sem("s_udev")
        s_pr = sem("s_pr")
        s_prhi = sem("s_prhi")
        s_prlo = sem("s_prlo")
        s_x0 = sem("s_x0")
        s_id = sem("s_id")
        s_idev = sem("s_idev")
        s_idt = sem("s_idt")
        s_idz = sem("s_idz")
        s_idst = [sem(f"s_idst{i}") for i in range(2)]
        s_zld = sem("s_zld")
        s_zhi = sem("s_zhi")
        s_zlo = sem("s_zlo")
        s_gld = [sem(f"s_gld{i}") for i in range(4)]
        s_y = sem("s_y")
        s_yev = sem("s_yev")
        s_mg = sem("s_mg")
        s_mhi = sem("s_mhi")
        s_mlo = sem("s_mlo")
        s_x1 = sem("s_x1")
        s_wo = sem("s_wo")
        s_woev = sem("s_woev")
        s_sq2 = sem("s_sq2")
        s_one2 = sem("s_one2")
        s_r2 = sem("s_r2")
        s_v2 = sem("s_v2")
        s_mod1 = sem("s_mod1")
        s_t2 = sem("s_t2")
        s_h2h = sem("s_h2h")
        s_h2 = sem("s_h2")
        s_fin = sem("s_fin")
        s_sil = sem("s_sil")
        s_up = sem("s_up")
        s_ghi = sem("s_ghi")
        s_glo = sem("s_glo")
        s_fo = sem("s_fo")
        s_foev = sem("s_foev")
        s_out = sem("s_out")
        s_dve = sem("s_dve")
        s_act = sem("s_act")

        def row(t, i):
            return t[bass.ds(i, 1)].rearrange("o p t -> (o p) t")

        def vcol(name, i=0, n=1):
            return v_sb[:, VEC[name] + i:VEC[name] + i + n]

        block = ctx.enter_context(nc.Block())

        @block.sync
        def _(sp):
            def mod_chunk(n, slot):
                sp.dma_start(mraw[:, slot, :], wmod[n]).then_inc(s_mraw[slot], 16)

            sp.dma_start(f_sb[:, :], filt).then_inc(s_filt, 16)
            for k in range(KT):
                if k >= 2:
                    sp.wait_ge(s_ss, k - 1)
                sp.dma_start(xs[:, k % 2, :], xc[k]).then_inc(s_xs[k % 2], 16)
                for j in range(2):
                    if k >= 1:
                        sp.wait_ge(s_mused, 2 * k + j - 1)
                    mod_chunk(2 * k + j, j)
                if k == 4:
                    sp.dma_start(win_sb[:, :, :], win).then_inc(s_win, 16)

            def main_chunks(i, first=False):
                for j in range(4):
                    if not first:
                        sp.wait_ge(s_split, 4 * i + j - 3)
                    sp.dma_start(raw[:, j, :], w[4 * i + j]).then_inc(s_raw[j], 16)

            main_chunks(0, first=True)
            n_k = CK_IN // 4
            n_m = 32 // 4
            with sp.Fori(1, n_k) as i:
                main_chunks(i)
            main_chunks(n_k)
            sp.wait_ge(s_hlo, KT)
            for m in range(4):
                if m < 2:
                    sp.wait_ge(s_mused, 2 * KT)
                else:
                    sp.wait_ge(s_mfree, m - 1)
                mod_chunk(2 * KT + m, m % 2)
            with sp.Fori(n_k + 1, n_k + n_m) as i:
                main_chunks(i)
                for j in range(4):
                    m = 4 * (i - n_k) + j
                    sp.wait_ge(s_mfree, m - 1)
                    mod_chunk(2 * KT + m, j % 2)
            n_g = (CK_IN + S_G) // 4
            with sp.Fori(n_k + n_m, n_g + 1) as i:
                main_chunks(i)
            for i in range(2):
                sp.wait_ge(s_nst[i], 32 * NB)
            sp.wait_ge(s_vst, 32 * NB)
            sp.wait_ge(s_cvst, 16 * 3 * NB)
            sp.dma_start(a_m[:, :, :], masks).then_inc(s_azst, 16)

            def rows64(dram, i, e):
                return row(dram, i)[e * HD:(e + 1) * HD, :]

            def head_in(hp, e):
                own, other = slice(e * HD, (e + 1) * HD), slice((1 - e) * HD, (2 - e) * HD)
                sp.dma_start(a_q[e][own, :].bitcast(F32), rows64(q_d[0], hp, e)).then_inc(s_hld[e], 16)
                sp.dma_start(a_q[e][other, :].bitcast(F32), rows64(q_d[1], hp, e)).then_inc(s_hld[e], 16)
                sp.dma_start(a_k[e][own, :].bitcast(F32), rows64(k_d[0], hp, e)).then_inc(s_hld[e], 16)
                sp.dma_start(a_k[e][other, :].bitcast(F32), rows64(k_d[0], hp, e)).then_inc(s_hld[e], 16)
                sp.dma_start(a_kl[own, :].bitcast(F32), rows64(k_d[1], hp, e)).then_inc(s_hld[e], 16)
                sp.dma_start(a_g[e][:, :], row(gat, 2 * hp + e)).then_inc(s_hld[e], 16)

            def values_load(hp):
                sp.dma_start(a_v[:, :], row(v_d, hp)).then_inc(s_vld, 16)
                sp.dma_start(a_vc[:, :], row(vc_d, hp)).then_inc(s_vld, 16)

            head_in(0, 0)
            values_load(0)
            sp.wait_ge(s_avt, 1)
            head_in(0, 1)
            main_chunks(n_g + 1)
            with sp.Fori(1, NB) as hp:
                sp.wait_ge(s_as, 16 * hp - 8)
                sp.wait_ge(s_attr, 16 * hp - 8)
                head_in(hp, 0)
                main_chunks(n_g + 2 * hp)
                sp.wait_ge(s_as, 16 * hp)
                sp.wait_ge(s_attr, 16 * hp)
                values_load(hp)
                sp.wait_ge(s_avt, hp + 1)
                head_in(hp, 1)
                main_chunks(n_g + 2 * hp + 1)
            main_chunks(CK_UDFT // 4)

            sp.wait_ge(s_azst, 16 * (NB + 1))
            sp.wait_ge(s_apv, 16 * NB)
            sp.dma_start(u_f[:, :, :], u_d.rearrange("c p t -> p c t")).then_inc(s_uld, 16)
            with sp.Fori(CK_UDFT // 4 + 1, N_CHUNK // 4) as i:
                main_chunks(i)
            for d in range(KT):
                sp.wait_ge(s_foev, 2 * KT + d + 1)
                sp.dma_start(out[d], x1[:, d, :]).then_inc(s_out, 16)
            sp.wait_ge(s_out, 16 * KT)

        @block.gpsimd
        def _(pool):
            def split(i, first=False):
                for j in range(4):
                    n = 4 * i + j
                    pool.wait_ge(s_raw[j], 16 * (i + 1))
                    if not (first and j < 2):
                        pool.wait_ge(s_used, n - 1)
                    nc.gpsimd.tensor_tensor(gate0[:, 1:2], gate0[:, 0:1], gate0[:, 0:1], ALU.add)
                    nc.gpsimd.tensor_scalar(whi[:, j % 2, :], raw[:, j, :], 1.0, 0.0, ALU.mult,
                                            ALU.add).then_inc(s_hi, 1)
                    pool.wait_ge(s_hi, n + 1)
                    nc.gpsimd.tensor_tensor(wlo[:, j % 2, :], raw[:, j, :], whi[:, j % 2, :].bitcast(F32),
                                            ALU.subtract).then_inc(s_split, 1)

            nc.gpsimd.memset(gate0[:, :], 0.0).then_inc(s_gate, 1)
            pool.wait_ge(s_gate, 1)
            split(0, first=True)
            with pool.Fori(1, N_CHUNK // 4) as i:
                split(i)

        @block.tensor
        def _(pe):
            def chunk_in(n):
                pe.wait_ge(s_split, n + 1)

            def mm3(o, slot, k, hi, lo, start, stop):
                a, b = whi[:, slot, k * P:(k + 1) * P], wlo[:, slot, k * P:(k + 1) * P]
                nc.tensor.matmul(o, a, hi, start=start, stop=False)
                nc.tensor.matmul(o, a, lo, start=False, stop=False)
                return nc.tensor.matmul(o, b, hi, start=False, stop=stop)

            def strip(slot, b0, hi, lo, ks=KT, k0=0, sk=0, last=None):
                for half in range(2):
                    for k in range(ks):
                        t = slice(half * HALF, (half + 1) * HALF)
                        mm = mm3(bank(b0 + half), slot, sk + k, hi[:, k0 + k, t], lo[:, k0 + k, t],
                                 k == 0, k == ks - 1)
                return mm

            def filter_layer(n, lhsT, rhs):
                for half in range(2):
                    t = slice(half * HALF, (half + 1) * HALF)
                    mm = nc.tensor.matmul(bank(4 + half)[0:64, :], lhsT, rhs[:, t], start=True, stop=True)
                mm.then_inc(s_fmm, 1)

            def mod_tile(n, slot):
                for k in range(KT):
                    mm = nc.tensor.matmul(ps[:, 6 * HALF + 2 * n:6 * HALF + 2 * n + 2], mraw[:, slot, k * P:(k + 1) * P],
                                          cs[:, 2 * k:2 * k + 2], start=k == 0, stop=k == KT - 1)
                mm.then_inc(s_mused, 1)

            pe.wait_ge(s_filt, 16)
            filter_layer(0, f_sb[0:33, 2 * T:2 * T + 64], f_sb[0:33, 0:T])
            pe.wait_ge(s_const, 32)
            for k in range(KT):
                pe.wait_ge(s_sq, k + 1)
                for b, n in ((0, HALF), (1, HALF), (2, C)):
                    mm = nc.tensor.matmul(bank(b, width=n), ones, xs[:, k % 2, b * HALF:b * HALF + n],
                                          start=k == 0, stop=k == KT - 1)
                mm.then_inc(s_ss, 1)
                if k == 0:
                    pe.wait_ge(s_cs, 1)
                for j in range(2):
                    pe.wait_ge(s_mraw[j], 16 * (k + 1))
                    mod_tile(2 * k + j, j)
                if k == 2:
                    pe.wait_ge(s_fsin, 1)
                    filter_layer(1, f_sb[:, 2 * T + 64:2 * T + 128], f_h)
                if k == 4:
                    pe.wait_ge(s_fsin, 2)
                    filter_layer(2, f_sb[:, 2 * T + 128:2 * T + 192], f_h)
            pe.wait_ge(s_fsin, 3)
            pe.wait_ge(s_w4, 1)
            for t in range(KT):
                for part in range(2):
                    n = 2 * t + part
                    if n >= 2:
                        pe.wait_ge(s_eoev, n - 1)
                    nc.tensor.matmul(bank(4 + n % 2), f_h[:, t * P:(t + 1) * P], f_w4[:, part, :],
                                     start=True, stop=True).then_inc(s_eomm, 1)
            pe.wait_ge(s_eolo, KT)
            pe.wait_ge(s_alt, 1)
            pe.wait_ge(s_eoev, 2 * KT)
            for t in range(KT):
                nc.tensor.matmul(bank(4), altr[:, :], e_hi[:, t, :], start=t == 0, stop=False)
                mm = nc.tensor.matmul(bank(4), altr[:, :], e_lo[:, t, :], start=False, stop=t == KT - 1)
            mm.then_inc(s_ny, 1)
            pe.wait_ge(s_nv, 1)
            pe.wait_ge(s_r0, 1)

            def kdft(i, first=False):
                for j in range(2):
                    q = 2 * i + j
                    if not first:
                        pe.wait_ge(s_ev, q - 1)
                    for part, (hi, lo) in enumerate(((e_hi, e_lo), (o_hi, o_lo))):
                        chunk_in(CK_KDFT + 2 * q + part)
                        for k in range(KT):
                            mm = mm3(bank(2 * j + part), part, k, hi[:, k, :], lo[:, k, :], k == 0, k == KT - 1)
                        mm.then_inc(s_used, 1)

            kdft(0, first=True)
            with pe.Fori(1, KT // 2) as i:
                kdft(i)

            pe.wait_ge(s_hlo, KT)
            pe.wait_ge(s_mod1, 1)

            def in_strip(n, j):
                chunk_in(CK_IN + n)
                pe.wait_ge(s_ev, n + KT - 1)
                strip(j, 2 * j, h_hi, h_lo).then_inc(s_used, 1)

            with pe.Fori(0, S_QKV // 2) as i:
                for j in range(2):
                    in_strip(2 * i + j, j)
                    pe.wait_ge(s_macc, 2 * i + j + 1)
                    nc.tensor.matmul(ps[:, bass.ds(6 * HALF + 4 * KT + 4 * i + 2 * j, 2)], macc[:, j, :], ones[:, 0:2],
                                     start=True, stop=True).then_inc(s_mused, 1)

            def q_ones(t):
                pe.wait_ge(s_qsq, t + 1)
                if t >= NB:
                    pe.wait_ge(s_cev, t - NB + 1)
                if t:
                    pe.wait_ge(s_qfree, t)
                    pe.wait_ge(s_qr, t)
                for half in range(2):
                    mm = nc.tensor.matmul(bank(6 + half), heads, q_t[:, half * HALF:(half + 1) * HALF],
                                          start=True, stop=True)
                if t >= NB:
                    mm = nc.tensor.matmul(bank(4 + t % 2)[:, C:2 * C], heads, q_t[:, T:TC], start=True, stop=True)
                mm.then_inc(s_qones, 1)

            for t in range(N_QKV):
                n, j = S_QKV + t, t % 2
                if t == 0:
                    pe.wait_ge(s_modev, 1)
                if t >= NB:
                    chunk_in(CK_IN + n)
                    if t >= NB + 2:
                        pe.wait_ge(s_cev, t - NB - 1)
                        if t - 2 < 2 * NB:
                            pe.wait_ge(s_qfree, t - 1)
                            pe.wait_ge(s_qr, t - 1)
                    for k in range(KT):
                        mm = mm3(bank(4 + j, width=C), j, k, c_hi[:, k, :], c_lo[:, k, :], k == 0, k == KT - 1)
                    mm.then_inc(s_cacc, 1)
                in_strip(n, j)
                if 1 <= t <= 2 * NB:
                    q_ones(t - 1)
            pe.wait_ge(s_qfree, 2 * NB)
            pe.wait_ge(s_qr, 2 * NB)
            pe.wait_ge(s_cev, 2 * NB)
            pe.wait_ge(s_ev, KT + S_G)

            def gate_half(hp, it):
                m, half = 8 * hp + it // 2, it % 2
                t = slice(half * HALF, (half + 1) * HALF)
                if half == 0:
                    chunk_in(CK_IN + S_G + m)
                pe.wait_ge(s_ev, KT + S_G + 16 * hp + it - 1)
                for k in range(KT):
                    mm = mm3(bank(half), it // 2 % 2, k, h_hi[:, k, t], h_lo[:, k, t], k == 0, k == KT - 1)
                mm.then_inc(s_used if half else s_gh, 1)

            def values_in(hp):
                pe.wait_ge(s_ev, KT + S_G + 16 * hp + 1)
                pe.wait_ge(s_vld, 32 * (hp + 1))
                for t in range(8):
                    nc.tensor.transpose(ps[:, 4 * HALF + t * P:4 * HALF + (t + 1) * P],
                                        a_v[:, t * P:(t + 1) * P], ident)
                for t in range(2):
                    mm = nc.tensor.transpose(ps[:, 6 * HALF + t * P:6 * HALF + (t + 1) * P],
                                             a_vc[:, t * P:(t + 1) * P], ident)
                mm.then_inc(s_avt, 1)

            def scores(hp, it):
                e, rp = divmod(it, 8)
                if rp == 0:
                    pe.wait_ge(s_hld[e], 96 * (hp + 1))
                if it:
                    pe.wait_ge(s_attr, 16 * hp + it)
                hs = slice(e * HD, (e + 1) * HD)
                q = slice(rp * P, (rp + 1) * P)
                k0 = window_start(rp) * GRID
                for o, keys in ((bank(2)[:, 0:C], slice(T, TC)), (bank(2)[:, C:HALF], slice(k0, k0 + HALF - C)),
                                (bank(3)[:, 0:KEYS - HALF], slice(k0 + HALF - C, k0 + LOC))):
                    nc.tensor.matmul(o, a_q[e][:, q], a_k[e][:, keys], start=True, stop=False)
                    mm = nc.tensor.matmul(o, a_q[e][hs, q], a_kl[hs, keys], start=False, stop=True)
                mm.then_inc(s_as, 1)

            def turn(hp, it):
                if it == 0:
                    pe.wait_ge(s_avev, hp + 1)
                else:
                    pe.wait_ge(s_aeva, 16 * hp + it)
                    pe.wait_ge(s_aevd, 16 * hp + it)
                pe.wait_ge(s_aexp, 16 * hp + it + 1)
                for b in range(7):
                    mm = nc.tensor.transpose(ps[:, 4 * HALF + b * P:4 * HALF + (b + 1) * P],
                                             a_s[:, it % 2, b * P:(b + 1) * P], ident)
                mm.then_inc(s_at, 1)

            def values(hp, it):
                e, rp = divmod(it, 8)
                pe.wait_ge(s_aeva, 16 * hp + it + 1)
                pe.wait_ge(s_aevd, 16 * hp + it + 1)
                if it >= 2:
                    pe.wait_ge(s_ao, 16 * hp + it - 1)
                v0 = window_start(rp) // 2
                for b in range(7):
                    tile = 8 + b if b < 2 else v0 + b - 2
                    mm = nc.tensor.matmul(bank(6 + it % 2)[:, 0:HD], a_pt[:, it % 2, b * P:(b + 1) * P],
                                          a_vt[:, tile, e * HD:(e + 1) * HD], start=b == 0, stop=b == 6)
                mm.then_inc(s_apv, 1)

            with pe.Fori(0, NB) as hp:
                for it in range(16):
                    if it < 15:
                        gate_half(hp, it)
                    if it == 1:
                        values_in(hp)
                    scores(hp, it)
                    if it:
                        turn(hp, it - 1)
                    if it >= 2:
                        values(hp, it - 2)
                gate_half(hp, 15)
                turn(hp, 15)
                values(hp, 14)
                values(hp, 15)
                pe.wait_ge(s_ao, 16 * hp + 16)
                for rp in range(8):
                    mm = nc.tensor.transpose(ps[:, 4 * HALF + rp * P:4 * HALF + (rp + 1) * P], a_o[:, rp, :], ident)
                mm.then_inc(s_azt, 1)

            pe.wait_ge(s_conv, NB)
            pe.wait_ge(s_azev, NB)
            for half in range(2):
                for c in range(NB):
                    mm = nc.tensor.matmul(bank(4 + half), ones, cfo[:, c, half * HALF:(half + 1) * HALF],
                                          start=c == 0, stop=c == NB - 1)
            mm.then_inc(s_l1, 1)
            pe.wait_ge(s_uld, 16)
            pe.wait_ge(s_ev, KT + S_G + 2 * N_G)
            for t in range(KT):
                if t >= 4:
                    pe.wait_ge(s_ulo, t - 3)
                for c in range(NB):
                    mm = nc.tensor.transpose(bank(t % 4)[:, c * P:(c + 1) * P], u_f[:, c, t * P:(t + 1) * P], ident)
                mm.then_inc(s_ut, 1)
            for c in range(NB):
                pe.wait_ge(s_lsq, c + 1)
                for half in range(2):
                    mm = nc.tensor.matmul(bank(6 + half), ones, lsq[:, c, half * HALF:(half + 1) * HALF],
                                          start=c == 0, stop=c == NB - 1)
                mm.then_inc(s_l2, 1)
            pe.wait_ge(s_ulo, KT)

            def udft(i, first=False):
                for j in range(2):
                    q = 2 * i + j
                    if not first:
                        pe.wait_ge(s_udev, q - 1)
                    for part in range(2):
                        chunk_in(CK_UDFT + 2 * q + part)
                        for k in range(KT):
                            mm = mm3(bank(2 * j + part), part, k, u_hi[:, k, :], u_lo[:, k, :], k == 0, k == KT - 1)
                        mm.then_inc(s_used, 1)

            udft(0, first=True)
            with pe.Fori(1, KT // 2) as i:
                udft(i)
            pe.wait_ge(s_prlo, KT)
            pe.wait_ge(s_udev, KT)

            def inverse(t, slot, first=False):
                if not first:
                    pe.wait_ge(s_idev, t - 1)
                for part, (hi, lo) in enumerate(((pr_hi, pr_lo), (ps_hi, ps_lo))):
                    chunk_in(CK_IDFT + 2 * t + part)
                    for k in range(KT):
                        mm = mm3(bank(slot), part, k, hi[:, k, :], lo[:, k, :],
                                 part == 0 and k == 0, part == 1 and k == KT - 1)
                    mm.then_inc(s_used, 1)

            def back(t, slot, first=False):
                pe.wait_ge(s_idev, t + 1)
                if not first:
                    pe.wait_ge(s_idz, t - 1)
                for c in range(NB):
                    mm = nc.tensor.transpose(bank(4 + slot)[:, c * P:(c + 1) * P], y_t[:, slot, c * P:(c + 1) * P], ident)
                mm.then_inc(s_idt, 1)

            pe.wait_ge(s_lf, 1)
            pe.wait_ge(s_lr, 1)
            inverse(0, 0, first=True)
            inverse(1, 1, first=True)
            back(0, 0, first=True)
            inverse(2, 0)
            back(1, 1, first=True)
            with pe.Fori(1, 3) as i:
                inverse(2 * i + 1, 1)
                back(2 * i, 0)
                inverse(2 * i + 2, 0)
                back(2 * i + 1, 1)
            inverse(7, 1)
            back(6, 0)
            back(7, 1)

            pe.wait_ge(s_idev, KT)
            for b in range(NBR):
                pe.wait_ge(s_zlo, b + 1)

                def y_pair(i, slot, first=False):
                    chunk_in(CK_Y + NB * b + 2 * i + slot)
                    for dd in range(2):
                        if not first:
                            pe.wait_ge(s_yev, 8 * b + 4 * i + 2 * slot + dd - 1)
                        mm = strip(slot, 2 * dd, z_hi[b % 2], z_lo[b % 2], ks=NB, sk=NB * dd)
                        if dd == 0:
                            mm.then_inc(s_y, 1)
                    mm.then_inc(s_used, 1)

                if b == 0:
                    y_pair(0, 0, first=True)
                    y_pair(0, 1)
                    with pe.Fori(1, 2) as i:
                        for slot in range(2):
                            y_pair(i, slot)
                else:
                    with pe.Fori(0, 2) as i:
                        for slot in range(2):
                            y_pair(i, slot)

            pe.wait_ge(s_mlo, KT)

            def wo(d, slot):
                chunk_in(CK_WO + d)
                strip(slot, 2 * slot, m_hi, m_lo).then_inc(s_used, 1)

            def wo_ones(d, slot, start=False, stop=False):
                pe.wait_ge(s_sq2, d + 1)
                for half in range(2):
                    mm = nc.tensor.matmul(bank(4 + half), ones, sq2[:, slot, half * HALF:(half + 1) * HALF],
                                          start=start, stop=stop)
                mm.then_inc(s_one2, 1)

            pe.wait_ge(s_yev, NBR * KT)
            wo(0, 0)
            wo(1, 1)
            wo_ones(0, 0, start=True)
            with pe.Fori(0, 3) as i:
                pe.wait_ge(s_woev, 2 * i + 1)
                wo(2 * i + 2, 0)
                wo_ones(2 * i + 1, 1)
                pe.wait_ge(s_woev, 2 * i + 2)
                wo(2 * i + 3, 1)
                wo_ones(2 * i + 2, 0)
            wo_ones(7, 1, stop=True)

            base, done = CK_FFN, 0
            for g, gn in enumerate(FGROUPS):

                def hidden(i, first=False):
                    chunk_in(base + 2 * i)
                    if not first:
                        pe.wait_ge(s_sil, done + i)
                    if first:
                        for half in range(2):
                            pe.wait_ge(s_h2, KT * (half + 1))
                            t = slice(half * HALF, (half + 1) * HALF)
                            for k in range(KT):
                                mm = mm3(bank(half), 0, k, h2_hi[:, k, t], h2_lo[:, k, t], k == 0, k == KT - 1)
                        mm.then_inc(s_used, 1)
                    else:
                        strip(0, 0, h2_hi, h2_lo).then_inc(s_used, 1)
                    chunk_in(base + 2 * i + 1)
                    if not first:
                        pe.wait_ge(s_up, done + i)
                    strip(1, 2, h2_hi, h2_lo).then_inc(s_used, 1)

                if g == 0:
                    hidden(0, first=True)
                with pe.Fori(int(g == 0), gn) as i:
                    hidden(i)
                done += gn
                base += 2 * gn
                pe.wait_ge(s_glo, done)

                def ffn_out(i, first=False):
                    for j in range(2):
                        chunk_in(base + 2 * i + j)
                        if not first:
                            pe.wait_ge(s_foev, KT * g + 2 * i + j - 1)
                        strip(j, 4 + 2 * j, g_hi, g_lo, ks=gn).then_inc(s_used, 1)

                if g == 0:
                    ffn_out(0, first=True)
                    with pe.Fori(1, KT // 2) as i:
                        ffn_out(i)
                else:
                    with pe.Fori(0, KT // 2) as i:
                        ffn_out(i)
                base += KT

        @block.scalar
        def _(act):
            own = Steps(act, s_act)

            def func(o, i, f, **kw):
                return nc.scalar.activation(o, i, f, **kw)

            def copy(o, i):
                return func(o, i, ACT.Identity)

            def rsqrt(r, sums, n):
                return func(r, sums, ACT.Abs_reciprocal_sqrt, scale=1.0 / n, bias=vcol("eps"))

            act.dma_start(v_sb[:, :], vec).then_inc(s_const, 16)
            act.dma_start(m_sb[:, :, :], mats).then_inc(s_const, 16)
            act.wait_ge(s_const, 32)
            func(csg[:, :], vcol("c", 0, 2 * KT), ACT.Sigmoid).then_inc(s_csg, 1)

            def sin(n):
                act.wait_ge(s_fred, n + 1)
                func(f_h[:, :], f_a[:, :], ACT.Sin).then_inc(s_fsin, 1)

            for k in range(KT):
                act.wait_ge(s_xs[k % 2], 16 * (k // 2 + 1))
                func(xs[:, k % 2, :], xs[:, k % 2, :], ACT.Square).then_inc(s_sq, 1)
                if k == 2:
                    sin(0)
                if k == 4:
                    sin(1)
                if k == 6:
                    sin(2)
            act.wait_ge(s_nv, 1)
            rsqrt(rstd[:, :], bank(0, width=TC), D).then_inc(s_r0, 1)

            def x_load(k):
                act.dma_start(hx[k % 3], xc[k]).then_inc(s_hx[k % 3], 16)

            act.wait_ge(s_ss, KT)
            act.wait_ge(s_mused, 2 * KT)
            for k in range(3):
                x_load(k)
            for t in range(KT):
                act.wait_ge(s_eo, t + 1)
                copy(e_hi[:, t, :], eo[:, t % 2, 0, :])
                copy(o_hi[:, t, :], eo[:, t % 2, 1, :]).then_inc(s_eohi, 1)
            for k in range(KT):
                act.wait_ge(s_ht, k + 1)
                func(h_hi[:, k, :], hx[k % 3][:, 0:T], ACT.Identity, bias=mod[:, k, 0:1])
                func(c_hi[:, k, :], hx[k % 3][:, T:TC], ACT.Identity, bias=mod[:, k, 1:2]).then_inc(s_hh, 1)
                if 1 <= k < KT - 2:
                    act.wait_ge(s_hlo, k)
                    x_load(k + 2)
            for q in range(KT):
                act.wait_ge(s_used, 2 * q + 2)
                if q:
                    act.wait_ge(s_kst, 16 * q)
                copy(ksp[:, :, :], bank(2 * (q % 2), 2)).then_inc(s_ev, 1)
                act.wait_ge(s_ev, q + 1)
                if q == 0:
                    act.wait_ge(s_ny, 1)
                    own.done(copy(ksp[0:1, 1, :], bank(4)[0:1, :]))
                act.dma_start(kspec[q], ksp[:, :, :]).then_inc(s_kst, 16)

            def strip_out(n, dst, f=ACT.Identity):
                act.wait_ge(s_used, CK_IN + n + 1)
                func(dst, bank(2 * (n % 2), 2), f).then_inc(s_ev, 1)

            for c in range(NB):
                if c >= 2:
                    act.wait_ge(s_cfm, c - 1)
                strip_out(2 * c, st[:, 2 * c % 4, 1:T + 1])
                strip_out(2 * c + 1, st[:, (2 * c + 1) % 4, 1:T + 1], ACT.Sigmoid)
            for g in range(2 * NB):
                if g == 0:
                    act.wait_ge(s_cfm, NB)
                if g >= 2:
                    act.wait_ge(s_grpout, g - 1)
                for j in range(3):
                    strip_out(S_HY + 3 * g + j, st[:, 3 * (g % 2) + j, 1:T + 1])
                act.wait_ge(s_grpout, g + 1)
                if g < NB:
                    act.dma_start(x0_d[g], cvo[:, 0, :]).then_inc(s_cvst, 16)
                    act.dma_start(u_d[g], cvo[:, 1, :]).then_inc(s_cvst, 16)
                else:
                    act.dma_start(z_d[Z_A, g - NB], cvo[:, 0, :]).then_inc(s_cvst, 16)
            act.wait_ge(s_kst, 16 * KT)
            act.wait_ge(s_cvst, 16 * 3 * NB)
            for t in range(N_QKV):
                if t >= 6:
                    act.wait_ge(s_nl, t - 5)
                strip_out(S_QKV + t, st[:, t % 6, 0:T])
                if t >= NB:
                    u = (t - NB) % 4
                    act.wait_ge(s_cacc, t - NB + 1)
                    if t >= 2 * NB:
                        act.wait_ge(s_nl, t - NB + 1)
                    copy(cst[:, u, :], bank(4 + t % 2, width=C)).then_inc(s_cev, 1)
                if 1 <= t <= 2 * NB:
                    act.wait_ge(s_qfree, t)
                    if t >= 2:
                        act.wait_ge(s_qn, t - 1)
                    r1 = rsqrt(q_r[:, 0:T], bank(6, 2), HD)
                    if t - 1 >= NB:
                        r1 = rsqrt(q_r[:, T:TC], bank(4 + (t - 1) % 2)[:, C:2 * C], HD)
                    r1.then_inc(s_qr, 1)
                o = t - 2
                if 0 <= o < 2 * NB:
                    act.wait_ge(s_qn, o + 1)
                    if o >= 2:
                        act.wait_ge(s_nst[o % 2], 32 * (o // 2))
                    ins = copy(n_hi[:, o % 2, 0:T], st[:, o % 6, 0:T])
                    if o >= NB:
                        ins = copy(n_hi[:, o % 2, T:TC], cst[:, (o - NB) % 4, :])
                    ins.then_inc(s_nh, 1)
                o = t - 3
                if 0 <= o < 2 * NB:
                    act.wait_ge(s_nl, o + 1)
                    for part, n_p in enumerate((n_hi, n_lo)):
                        if o < NB:
                            act.dma_start(q_d[part][o], n_p[:, o % 2, 0:T].bitcast(F32)).then_inc(s_nst[o % 2], 16)
                        else:
                            act.dma_start(k_d[part][o - NB], n_p[:, o % 2, :].bitcast(F32)).then_inc(s_nst[o % 2], 16)
                if t >= 2 * NB:
                    act.wait_ge(s_ev, KT + S_QKV + t + 1)
                    act.wait_ge(s_cev, t - NB + 1)
                    act.dma_start(v_d[t - 2 * NB], st[:, t % 6, 0:T]).then_inc(s_vst, 16)
                    act.dma_start(vc_d[t - 2 * NB], cst[:, (t - NB) % 4, :]).then_inc(s_vst, 16)
            def gate_out(hp, it):
                m, half = 8 * hp + it // 2, it % 2
                slot = it // 2 % 2
                if half:
                    act.wait_ge(s_used, CK_IN + S_G + m + 1)
                else:
                    act.wait_ge(s_gh, m + 1)
                    if it >= 4:
                        act.wait_ge(s_gst[slot], 64 * hp + 16 * (it // 4))
                func(gst[:, slot, half * HALF:(half + 1) * HALF], bank(half), ACT.Sigmoid).then_inc(s_ev, 1)
                if half:
                    act.wait_ge(s_ev, KT + S_G + 16 * hp + it + 1)
                    act.dma_start(row(gate_d, m), gst[:, slot, :]).then_inc(s_gst[slot], 16)

            def exps(hp, it):
                act.wait_ge(s_anm, 16 * hp + it + 1)
                s = it % 2
                func(a_s[:, s, :], a_s[:, s, :], ACT.Exp, bias=st_nm[:, s:s + 1],
                     accum_out=st_l[:, s:s + 1]).then_inc(s_aexp, 1)

            def evacuate(hp, it):
                act.wait_ge(s_at, 16 * hp + it + 1)
                if it >= 2:
                    act.wait_ge(s_apv, 16 * hp + it - 1)
                copy(a_pt[:, it % 2, 0:HALF], bank(4)).then_inc(s_aeva, 1)

            with act.Fori(0, NB) as hp:
                for it in range(16):
                    if it < 15:
                        gate_out(hp, it)
                    if it == 1:
                        act.wait_ge(s_avt, hp + 1)
                        copy(a_vt[:, :, :], bank(4, width=10 * P)).then_inc(s_avev, 1)
                    exps(hp, it)
                    if it:
                        evacuate(hp, it - 1)
                gate_out(hp, 15)
                evacuate(hp, 15)
                act.wait_ge(s_azt, hp + 1)
                copy(a_o[:, :, :], bank(4, 2)).then_inc(s_azev, 1)
                act.wait_ge(s_azev, hp + 1)
                act.dma_start(row(z_d[Z_NA], hp), a_o.rearrange("p r c -> p (r c)")).then_inc(s_azst, 16)
                for j in range(2):
                    act.wait_ge(s_gst[j], 64 * hp + 64)

            for c in range(NB):
                act.wait_ge(s_lx, c + 1)
                func(lsq[:, c, :], cfo[:, c, :], ACT.Square).then_inc(s_lsq, 1)
            for t in range(KT):
                act.wait_ge(s_ut, t + 1)
                copy(u_hi[:, t, :], bank(t % 4)).then_inc(s_uhi, 1)
            act.wait_ge(s_lf, 1)
            rsqrt(l_r[:, :], bank(6, 2), DB).then_inc(s_lr, 1)
            for c in range(NB):
                act.wait_ge(s_ly, c + 1)
                func(cfo[:, c, :], cfo[:, c, :], ACT.Silu, scale=vcol("lng", c),
                     bias=vcol("lnb", c)).then_inc(s_lz, 1)
                act.wait_ge(s_lz, c + 1)
                act.dma_start(z_d[Z_CF, c], cfo[:, c, :]).then_inc(s_zst, 16)

            def k_load(q):
                act.dma_start(k_sb[:, q % 2, :, :], kspec[q]).then_inc(s_k[q % 2], 16)

            act.wait_ge(s_l2, NB)
            k_load(0)
            k_load(1)
            act.dma_start(x0_f[:, :, :], x0_d.rearrange("c p t -> p c t")).then_inc(s_x0, 16)
            for q in range(KT):
                act.wait_ge(s_pr, q + 1)
                copy(pr_hi[:, q, :], pw[:, q % 2, 0, :])
                copy(ps_hi[:, q, :], pw[:, q % 2, 2, :]).then_inc(s_prhi, 1)
                if q + 2 < KT:
                    act.wait_ge(s_udev, q + 1)
                    k_load(q + 2)

            def z_load(b):
                act.dma_start(zraw[:, :, :], z_d[b].rearrange("c p t -> p c t")).then_inc(s_zld, 16)

            def z_high(b):
                act.wait_ge(s_zld, 16 * (b + 1))
                copy(z_hi[b % 2][:, :, :], zraw[:, :, :]).then_inc(s_zhi, 1)

            def g_load(n):
                b, d = divmod(n, KT)
                act.dma_start(gt[:, n % 4, :], gate_d[GATE_OF[b] * KT + d]).then_inc(s_gld[n % 4], 16)

            act.wait_ge(s_prlo, KT)
            z_load(0)
            for n in range(4):
                g_load(n)
            for t in range(KT):
                act.wait_ge(s_used, CK_IDFT + 2 * t + 2)
                if t >= 2:
                    act.wait_ge(s_idt, t - 1)
                copy(y_t[:, t % 2, :], bank(t % 2)).then_inc(s_idev, 1)
                if t == 1:
                    z_high(0)
                if t >= 2:
                    act.wait_ge(s_idz, t - 1)
                    act.dma_start(z_d[Z_HY].rearrange("c p t -> p c t")[:, :, (t - 2) * P:(t - 1) * P],
                                  y_w[:, t % 2, :, :]).then_inc(s_idst[t % 2], 16)
            for t in (KT - 2, KT - 1):
                act.wait_ge(s_idz, t + 1)
                act.dma_start(z_d[Z_HY].rearrange("c p t -> p c t")[:, :, t * P:(t + 1) * P],
                              y_w[:, t % 2, :, :]).then_inc(s_idst[t % 2], 16)

            for n in range(NBR * KT):
                b, d = divmod(n, KT)
                if d == 0 and b + 1 < NBR:
                    act.wait_ge(s_zlo, b + 1)
                    if b + 1 == Z_HY:
                        act.wait_ge(s_idst[0], 16 * KT // 2)
                        act.wait_ge(s_idst[1], 16 * KT // 2)
                    z_load(b + 1)
                    act.wait_ge(s_used, CK_Y + NB * b)
                    z_high(b + 1)
                act.wait_ge(s_yev, n + 1)
                if n + 4 < NBR * KT:
                    g_load(n + 4)
                if b == NBR - 1:
                    act.wait_ge(s_mg, d + 1)
                    copy(m_hi[:, d, :], mrg[:, d, :]).then_inc(s_mhi, 1)

            act.wait_ge(s_used, CK_WO)
            act.dma_start(x1[:, :, :], xc.rearrange("k p t -> p k t")[:, :, 0:T]).then_inc(s_x1, 16)
            for d in range(KT):
                act.wait_ge(s_woev, d + 1)
                if d >= 2:
                    act.wait_ge(s_one2, d - 1)
                func(sq2[:, d % 2, :], x1[:, d, :], ACT.Square).then_inc(s_sq2, 1)
            for half in range(2):
                t = slice(half * HALF, (half + 1) * HALF)
                act.wait_ge(s_v2, half + 1)
                rsqrt(r2[:, t], bank(4 + half), D).then_inc(s_r2, 1)
            for n in range(2 * KT):
                half, k = divmod(n, KT)
                t = slice(half * HALF, (half + 1) * HALF)
                act.wait_ge(s_t2, n + 1)
                func(h2_hi[:, k, t], ht[:, n % 4, :], ACT.Identity, bias=mod[:, 3 * KT + k, 0:1]).then_inc(s_h2h, 1)

            m, base = 0, CK_FFN
            for g, gn in enumerate(FGROUPS):
                for i in range(gn):
                    act.wait_ge(s_used, base + 2 * i + 1)
                    if m:
                        act.wait_ge(s_up, m)
                    func(sg[:, :], bank(0, 2), ACT.Silu).then_inc(s_sil, 1)
                    act.wait_ge(s_up, m + 1)
                    copy(g_hi[:, i, :], gm[:, :]).then_inc(s_ghi, 1)
                    m += 1
                base += 2 * gn + KT

        @block.vector
        def _(dve):
            own = Steps(dve, s_dve)
            tt, ts, stt = nc.vector.tensor_tensor, nc.vector.tensor_scalar, nc.vector.scalar_tensor_tensor

            def low(o, x, hi):
                return tt(o, x, hi.bitcast(F32), ALU.subtract)

            def low_shift(o, x, shift, hi):
                return stt(out=o, in0=x, scalar=shift, in1=hi.bitcast(F32), op0=ALU.add, op1=ALU.subtract)

            def refine(r, v, t):
                own.done(stt(out=t, in0=r, scalar=-0.5, in1=r, op0=ALU.mult, op1=ALU.mult))
                own.done(tt(t, t, v, ALU.mult))
                own.done(stt(out=r, in0=t, scalar=1.5, in1=r, op0=ALU.add, op1=ALU.mult))

            def mean_eps(v, sums, n):
                return ts(v, sums, 1.0 / n, EPS, ALU.mult, ALU.add)

            dve.wait_ge(s_filt, 16)
            w4 = f_sb[:, T:2 * T]
            own.done(tt(f_w4[:, 0, :], w4[:, 0:DB], w4[:, DB:2 * DB], ALU.add))
            tt(f_w4[:, 1, :], w4[:, 0:DB], w4[:, DB:2 * DB], ALU.subtract).then_inc(s_w4, 1)
            dve.wait_ge(s_const, 32)
            nc.vector.tensor_copy(altr[:, :], m_sb[:, M_ALT, :]).then_inc(s_alt, 1)
            own.done(ts(qg8[:, :], vcol("qg"), HD ** -0.5, None, ALU.mult))
            dve.wait_ge(s_csg, 1)
            tt(cs[:, :], csg[:, :], vcol("c", 0, 2 * KT), ALU.mult).then_inc(s_cs, 1)

            magic = float(1.5 * 2 ** 23)
            p1 = 6.28125
            p2 = float(np.float32(np.round((2 * np.pi - p1) * 2 ** 21) / 2 ** 21))
            p3 = float(np.float32(2 * np.pi - p1 - p2))
            for n in range(3):
                dve.wait_ge(s_fmm, n + 1)
                own.done(ts(f_a[:, :], bank(4, 2)[0:64, :], vcol("fb", n)[0:64, :], vcol("freq")[0:64, :],
                            ALU.add, ALU.mult))
                own.done(ts(f_k[:, :], f_a[:, :], float(1 / (2 * np.pi)), magic, ALU.mult, ALU.add))
                own.done(ts(f_k[:, :], f_k[:, :], magic, None, ALU.subtract))
                for part in (p1, p2, p3):
                    own.done(stt(out=f_a[:, :], in0=f_k[:, :], scalar=-part, in1=f_a[:, :], op0=ALU.mult, op1=ALU.add))
                ts(f_a[:, :], f_a[:, :], 3.1415925, -3.1415925, ALU.min, ALU.max).then_inc(s_fred, 1)

            def mod_out(a, b):
                for s in range(2):
                    ins = tt(mod[:, a:b, s], ps[:, 6 * HALF + 2 * a + s:6 * HALF + 2 * b:2], vcol("bmod", a, b - a), ALU.add)
                return ins

            dve.wait_ge(s_mused, 2 * KT)
            mod_out(0, 2 * KT).then_inc(s_mod1, 1)
            dve.wait_ge(s_mod1, 1)
            for s in range(2):
                own.done(stt(out=aff[:, :, s], in0=mod[:, KT:2 * KT, s], scalar=1.0, in1=vcol("g1", 0, KT),
                             op0=ALU.add, op1=ALU.mult))
            dve.wait_ge(s_ss, KT)
            mean_eps(nv[:, :], bank(0, width=TC), D).then_inc(s_nv, 1)
            dve.wait_ge(s_nv, 1)
            dve.wait_ge(s_r0, 1)
            refine(rstd[:, :], nv[:, :], nt[:, :])

            dve.wait_ge(s_win, 16)

            def eo_low(t):
                dve.wait_ge(s_eohi, t + 1)
                low(e_lo[:, t, :], eo[:, t % 2, 0, :], e_hi[:, t, :])
                low(o_lo[:, t, :], eo[:, t % 2, 1, :], o_hi[:, t, :]).then_inc(s_eolo, 1)
                dve.wait_ge(s_eolo, t + 1)

            for t in range(KT):
                for part in range(2):
                    dve.wait_ge(s_eomm, 2 * t + part + 1)
                    tt(eo[:, t % 2, part, :], bank(4 + part), win_sb[:, t, :], ALU.mult).then_inc(s_eoev, 1)
                dve.wait_ge(s_eoev, 2 * t + 2)
                if t == 0:
                    e0, o0 = eo[0:1, 0, 0, :], eo[0:1, 0, 1, :]
                    own.done(tt(e0, e0, o0, ALU.add))
                    own.done(ts(e0, e0, 0.5, None, ALU.mult))
                nc.vector.tensor_copy(st_m[:, 0:1], vcol("eps")).then_inc(s_eo, 1)
                dve.wait_ge(s_eo, t + 1)
                if t:
                    eo_low(t - 1)
            eo_low(KT - 1)

            def h_low(k):
                dve.wait_ge(s_hh, k + 1)
                low_shift(h_lo[:, k, :], hx[k % 3][:, 0:T], mod[:, k, 0:1], h_hi[:, k, :])
                low_shift(c_lo[:, k, :], hx[k % 3][:, T:TC], mod[:, k, 1:2], c_hi[:, k, :]).then_inc(s_hlo, 1)
                dve.wait_ge(s_hlo, k + 1)

            for k in range(KT):
                dve.wait_ge(s_hx[k % 3], 16 * (k // 3 + 1))
                for s, t in ((0, slice(0, T)), (1, slice(T, TC))):
                    ins = stt(out=hx[k % 3][:, t], in0=hx[k % 3][:, t], scalar=aff[:, k, s:s + 1], in1=rstd[:, t],
                              op0=ALU.mult, op1=ALU.mult)
                ins.then_inc(s_ht, 1)
                if k:
                    h_low(k - 1)
            h_low(KT - 1)

            dve.wait_ge(s_used, CK_IN)
            edge = CFK // 2
            nc.vector.memset(cfm[:, :, 0:edge], 0.0)
            nc.vector.memset(cfm[:, :, T + edge:T + 2 * edge], 0.0)
            nc.vector.memset(st[:, :, 0:1], 0.0)
            own.done(nc.vector.memset(st[:, :, T + 1:T + 2], 0.0))

            def mod_part(n):
                dve.wait_ge(s_mraw[n % 2], 16 * (KT + n // 2 + 1))
                wv = mraw[:, n % 2, :].rearrange("p (k f) -> p k f", k=KT)
                by_k = cs.rearrange("p (k s) -> p k s", s=2)[:, :, 0:1].broadcast_to([P, KT, P])
                tt(mprod.rearrange("p (k f) -> p k f", k=KT), wv, by_k, ALU.mult).then_inc(s_mfree, 1)
                dve.wait_ge(s_mfree, n + 1)
                if n >= 2:
                    dve.wait_ge(s_mused, 16 + n - 1)
                nc.vector.tensor_reduce(macc[:, n % 2, :], mprod.rearrange("p (k f) -> p f k", k=KT),
                                        mybir.AxisListType.X, ALU.add).then_inc(s_macc, 1)
                dve.wait_ge(s_macc, n + 1)

            dve.wait_ge(s_kst, 16 * KT)
            for c in range(NB):
                mod_part(2 * c)
                mod_part(2 * c + 1)
                dve.wait_ge(s_ev, KT + 2 * c + 2)
                tt(cfm[:, c, edge:edge + T], st[:, 2 * c % 4, 1:T + 1], st[:, (2 * c + 1) % 4, 1:T + 1],
                   ALU.mult).then_inc(s_cfm, 1)

            def conv3(o, slot, name, n, first, ready):
                dve.wait_ge(s_ev, ready)
                own.done(ts(o, st[:, slot, 0:T], vcol(name, first), None, ALU.mult))
                own.done(stt(out=o, in0=st[:, slot, 1:T + 1], scalar=vcol(name, n + first), in1=o, op0=ALU.mult, op1=ALU.add))
                own.done(stt(out=o, in0=st[:, slot, 2:T + 2], scalar=vcol(name, 2 * n + first), in1=o, op0=ALU.mult, op1=ALU.add))

            for g in range(2 * NB):
                for j in range(3):
                    mod_part(N_CF + 3 * g + j)
                s0 = 3 * (g % 2)
                ready = KT + S_HY + 3 * g + 1
                if g:
                    dve.wait_ge(s_cvst, 16 * (2 * g if g <= NB else NB + g))
                if g < NB:
                    for j in range(3):
                        conv3(cvo[:, j, :], s0 + j, "chy", 3 * NB, j * NB + g, ready + j)
                    tt(cvo[:, 1, :], cvo[:, 1, :], cvo[:, 2, :], ALU.mult).then_inc(s_grpout, 1)
                else:
                    dve.wait_ge(s_ev, ready + 2)
                    own.done(tt(st[:, s0 + 2, 1:T + 1], st[:, s0 + 2, 1:T + 1], st[:, s0, 1:T + 1], ALU.mult))
                    conv3(cvo[:, 0, :], s0 + 2, "ca", NB, g - NB, ready + 2)
                    tt(cvo[:, 0, :], cvo[:, 0, :], st[:, s0 + 1, 1:T + 1], ALU.mult).then_inc(s_grpout, 1)
            dve.wait_ge(s_mused, 6 * KT)
            mod_out(2 * KT, 6 * KT).then_inc(s_modev, 1)

            def norm_low(t):
                dve.wait_ge(s_nh, t + 1)
                ins = low(n_lo[:, t % 2, 0:T], st[:, t % 6, 0:T], n_hi[:, t % 2, 0:T])
                if t >= NB:
                    ins = low(n_lo[:, t % 2, T:TC], cst[:, (t - NB) % 4, :], n_hi[:, t % 2, T:TC])
                ins.then_inc(s_nl, 1)

            for t in range(2 * NB):
                x = st[:, t % 6, 0:T]
                kc = cst[:, (t - NB) % 4, :]
                gain = qg8[:, :] if t < NB else vcol("kg")
                n = T if t < NB else TC
                dve.wait_ge(s_ev, KT + S_QKV + t + 1)
                ins = tt(q_t[:, 0:T], x, x, ALU.mult)
                if t >= NB:
                    dve.wait_ge(s_cev, t - NB + 1)
                    ins = tt(q_t[:, T:TC], kc, kc, ALU.mult)
                ins.then_inc(s_qsq, 1)
                if t >= 2:
                    norm_low(t - 2)
                dve.wait_ge(s_qones, t + 1)
                ins = mean_eps(q_v[:, 0:T], bank(6, 2), HD)
                if t >= NB:
                    ins = mean_eps(q_v[:, T:TC], bank(4 + t % 2)[:, C:2 * C], HD)
                ins.then_inc(s_qfree, 1)
                dve.wait_ge(s_qfree, t + 1)
                dve.wait_ge(s_qr, t + 1)
                refine(q_r[:, 0:n], q_v[:, 0:n], q_t[:, 0:n])
                ins = stt(out=x, in0=x, scalar=gain, in1=q_r[:, 0:T], op0=ALU.mult, op1=ALU.mult)
                if t >= NB:
                    ins = stt(out=kc, in0=kc, scalar=gain, in1=q_r[:, T:TC], op0=ALU.mult, op1=ALU.mult)
                ins.then_inc(s_qn, 1)
                dve.wait_ge(s_qn, t + 1)

            norm_low(2 * NB - 2)
            norm_low(2 * NB - 1)

            dve.wait_ge(s_azst, 16)
            own.done(nc.vector.memset(a_b[:, 0:C], 0.0))

            def tap(hp, j):
                o = cfo[:, bass.ds(hp, 1), :]
                x = cfm[:, bass.ds(hp, 1), j:j + T]
                wj = v_sb[:, bass.ds(VEC["cd"] + NB * j + hp, 1)]
                if j == 0:
                    own.mark(ts(o, x, wj, v_sb[:, bass.ds(VEC["cdb"] + hp, 1)], ALU.mult, ALU.add))
                elif j < CFK - 1:
                    own.mark(stt(out=o, in0=x, scalar=wj, in1=o, op0=ALU.mult, op1=ALU.add))
                else:
                    stt(out=o, in0=x, scalar=wj, in1=o, op0=ALU.mult, op1=ALU.add).then_inc(s_conv, 1)

            def heads_out(hp, it):
                e, rp = divmod(it, 8)
                s = it % 2
                dve.wait_ge(s_apv, 16 * hp + it + 1)
                ts(a_o[:, rp, e * HD:(e + 1) * HD], bank(6 + s)[:, 0:HD], st_r[:, s:s + 1], None,
                   ALU.mult).then_inc(s_ao, 1)

            def weights_out(hp, it):
                s = it % 2
                dve.wait_ge(s_at, 16 * hp + it + 1)
                if it >= 2:
                    dve.wait_ge(s_apv, 16 * hp + it - 1)
                nc.vector.tensor_copy(a_pt[:, s, HALF:KEYS], bank(5, width=KEYS - HALF)).then_inc(s_aevd, 1)
                dve.wait_ge(s_aexp, 16 * hp + it + 1)
                own.mark(nc.vector.reciprocal(st_r[:, s:s + 1], st_l[:, s:s + 1]))

            with own.loop(NB, 30 + 16 + 10) as hp:
                for it in range(16):
                    e, rp = divmod(it, 8)
                    s = it % 2
                    if rp == 0:
                        dve.wait_ge(s_hld[e], 96 * (hp + 1))
                    if rp in MASK_OF:
                        x = (window_start(rp) - 2 * rp + WIN_H) * GRID
                        own.mark(tt(a_b[:, C:KEYS], a_g[e][:, x:x + LOC], a_m[:, MASK_OF[rp], :], ALU.add))
                    own.wait()
                    dve.wait_ge(s_as, 16 * hp + it + 1)
                    if it >= 2:
                        dve.wait_ge(s_at, 16 * hp + it - 1)
                    tap(hp, 2 * it)
                    nc.vector.tensor_tensor_reduce(a_s[:, s, :], bank(2, width=KEYS), a_b[:, :], 1.0, NEG, ALU.add,
                                                   ALU.max, st_m[:, s:s + 1]).then_inc(s_attr, 1)
                    dve.wait_ge(s_attr, 16 * hp + it + 1)
                    ts(st_nm[:, s:s + 1], st_m[:, s:s + 1], -1.0, None, ALU.mult).then_inc(s_anm, 1)
                    if it == 2:
                        dve.wait_ge(s_azst, 16 * (hp + 1))
                    if it >= 2:
                        heads_out(hp, it - 2)
                    if it:
                        weights_out(hp, it - 1)
                    own.wait()
                    if 2 * it + 1 < CFK:
                        tap(hp, 2 * it + 1)
                heads_out(hp, 14)
                weights_out(hp, 15)
                own.wait()
                heads_out(hp, 15)

            dve.wait_ge(s_l1, 1)
            for c in range(NB):
                stt(out=cfo[:, c, :], in0=bank(4, 2), scalar=-1.0 / DB, in1=cfo[:, c, :], op0=ALU.mult,
                    op1=ALU.add).then_inc(s_lx, 1)
            for t in range(KT):
                dve.wait_ge(s_uhi, t + 1)
                low(u_lo[:, t, :], bank(t % 4), u_hi[:, t, :]).then_inc(s_ulo, 1)
            dve.wait_ge(s_l2, NB)
            mean_eps(l_v[:, :], bank(6, 2), DB).then_inc(s_lf, 1)
            dve.wait_ge(s_lf, 1)
            dve.wait_ge(s_lr, 1)
            dve.wait_ge(s_lx, NB)
            refine(l_r[:, :], l_v[:, :], l_t[:, :])
            for c in range(NB):
                tt(cfo[:, c, :], cfo[:, c, :], l_r[:, :], ALU.mult).then_inc(s_ly, 1)

            def pr_low(q):
                dve.wait_ge(s_prhi, q + 1)
                low(pr_lo[:, q, :], pw[:, q % 2, 0, :], pr_hi[:, q, :])
                low(ps_lo[:, q, :], pw[:, q % 2, 2, :], ps_hi[:, q, :]).then_inc(s_prlo, 1)
                dve.wait_ge(s_prlo, q + 1)

            dve.wait_ge(s_zst, 16 * NB)
            for q in range(KT):
                s = q % 2
                uc, us = bank(2 * s), bank(2 * s + 1)
                dve.wait_ge(s_k[s], 16 * (q // 2 + 1))
                kc, ks = k_sb[:, s, 0, :], k_sb[:, s, 1, :]
                dve.wait_ge(s_used, CK_UDFT + 2 * q + 1)
                own.done(tt(pw[:, s, 0, :], uc, kc, ALU.mult))
                own.done(tt(pw[:, s, 2, :], uc, ks, ALU.mult))
                dve.wait_ge(s_used, CK_UDFT + 2 * q + 2)
                own.done(tt(pw[:, s, 1, :], us, ks, ALU.mult))
                own.done(tt(pw[:, s, 3, :], us, kc, ALU.mult))
                own.done(tt(pw[:, s, 0, :], pw[:, s, 0, :], pw[:, s, 1, :], ALU.subtract))
                own.done(tt(pw[:, s, 2, :], pw[:, s, 2, :], pw[:, s, 3, :], ALU.add))
                if q == 0:
                    own.done(tt(pw[0:1, s, 0, :], uc[0:1, :], kc[0:1, :], ALU.mult))
                    own.done(tt(pw[0:1, s, 2, :], us[0:1, :], ks[0:1, :], ALU.mult))
                nc.vector.tensor_copy(st_m[:, 0:1], vcol("eps")).then_inc(s_udev, 1)
                nc.vector.tensor_copy(st_m[:, 1:2], vcol("eps")).then_inc(s_pr, 1)
                dve.wait_ge(s_pr, q + 1)
                if q:
                    pr_low(q - 1)
            pr_low(KT - 1)

            def z_low(b):
                dve.wait_ge(s_zhi, b + 1)
                low(z_lo[b % 2][:, :, :], zraw[:, :, :], z_hi[b % 2][:, :, :]).then_inc(s_zlo, 1)

            dve.wait_ge(s_x0, 16)
            for t in range(KT):
                s = t % 2
                dve.wait_ge(s_idt, t + 1)
                if t >= 2:
                    dve.wait_ge(s_idst[s], 16 * (t // 2))
                tsl = slice(t * P, (t + 1) * P)
                for c in range(NB):
                    ins = stt(out=y_w[:, s, c, :], in0=u_f[:, c, tsl], scalar=vcol("skip", c),
                              in1=bank(4 + s)[:, c * P:(c + 1) * P], op0=ALU.mult, op1=ALU.add)
                own.done(ins)
                tt(y_w[:, s, :, :], y_w[:, s, :, :], x0_f[:, :, tsl], ALU.mult).then_inc(s_idz, 1)
                if t == 2:
                    z_low(0)

            for n in range(NBR * KT):
                b, d = divmod(n, KT)
                b0 = 2 * (d % 2)
                dve.wait_ge(s_gld[n % 4], 16 * (n // 4 + 1))
                if d % 2 == 0:
                    dve.wait_ge(s_y, n // 2 + 1)
                else:
                    dve.wait_ge(s_used, CK_Y + n // 2 + 1)
                if b == 0:
                    tt(mrg[:, d, :], bank(b0, 2), gt[:, n % 4, :], ALU.mult).then_inc(s_yev, 1)
                    dve.wait_ge(s_yev, n + 1)
                else:
                    tt(yt[:, :], bank(b0, 2), gt[:, n % 4, :], ALU.mult).then_inc(s_yev, 1)
                    dve.wait_ge(s_yev, n + 1)
                    own.done(tt(mrg[:, d, :], mrg[:, d, :], yt[:, :], ALU.add))
                if b == NBR - 1:
                    nc.vector.tensor_copy(st_m[:, 0:1], vcol("eps")).then_inc(s_mg, 1)
                    if d:
                        dve.wait_ge(s_mhi, d)
                        low(m_lo[:, d - 1, :], mrg[:, d - 1, :], m_hi[:, d - 1, :]).then_inc(s_mlo, 1)
                if b + 1 < NBR and d == 4:
                    z_low(b + 1)
            dve.wait_ge(s_mhi, KT)
            low(m_lo[:, KT - 1, :], mrg[:, KT - 1, :], m_hi[:, KT - 1, :]).then_inc(s_mlo, 1)

            own.done(stt(out=aff2[:, :], in0=mod[:, 4 * KT:5 * KT, 0], scalar=1.0, in1=vcol("g2", 0, KT),
                         op0=ALU.add, op1=ALU.mult))
            dve.wait_ge(s_x1, 16)
            for d in range(KT):
                dve.wait_ge(s_used, CK_WO + d + 1)
                stt(out=x1[:, d, :], in0=bank(2 * (d % 2), 2), scalar=mod[:, 2 * KT + d, 0:1], in1=x1[:, d, :],
                    op0=ALU.mult, op1=ALU.add).then_inc(s_woev, 1)
            dve.wait_ge(s_one2, KT)
            for half in range(2):
                mean_eps(v2[:, half * HALF:(half + 1) * HALF], bank(4 + half), D).then_inc(s_v2, 1)
            dve.wait_ge(s_v2, 2)

            def h2_low(n):
                half, k = divmod(n, KT)
                t = slice(half * HALF, (half + 1) * HALF)
                dve.wait_ge(s_h2h, n + 1)
                low_shift(h2_lo[:, k, t], ht[:, n % 4, :], mod[:, 3 * KT + k, 0:1], h2_hi[:, k, t]).then_inc(s_h2, 1)

            dve.wait_ge(s_woev, KT)
            for half in range(2):
                t = slice(half * HALF, (half + 1) * HALF)
                dve.wait_ge(s_r2, half + 1)
                refine(r2[:, t], v2[:, t], t2[:, t])
                for k in range(KT):
                    n = KT * half + k
                    if n >= 4:
                        dve.wait_ge(s_h2, n - 3)
                    stt(out=ht[:, n % 4, :], in0=x1[:, k, t], scalar=aff2[:, k:k + 1], in1=r2[:, t], op0=ALU.mult,
                        op1=ALU.mult).then_inc(s_t2, 1)
                    if n:
                        h2_low(n - 1)
            h2_low(2 * KT - 1)

            m, base = 0, CK_FFN
            for g, gn in enumerate(FGROUPS):
                for i in range(gn):
                    dve.wait_ge(s_sil, m + 1)
                    dve.wait_ge(s_used, base + 2 * i + 2)
                    if m:
                        dve.wait_ge(s_ghi, m)
                    tt(gm[:, :], bank(2, 2), sg[:, :], ALU.mult).then_inc(s_up, 1)
                    dve.wait_ge(s_up, m + 1)
                    dve.wait_ge(s_ghi, m + 1)
                    low(g_lo[:, i, :], gm[:, :], g_hi[:, i, :]).then_inc(s_glo, 1)
                    dve.wait_ge(s_glo, m + 1)
                    m += 1
                base += 2 * gn
                for d in range(KT):
                    dve.wait_ge(s_used, base + d + 1)
                    stt(out=x1[:, d, :], in0=bank(4 + 2 * (d % 2), 2), scalar=mod[:, 5 * KT + d, 0:1],
                        in1=x1[:, d, :], op0=ALU.mult, op1=ALU.add).then_inc(s_foev, 1)
                    dve.wait_ge(s_foev, KT * g + d + 1)
                base += KT


def _tiles(v):
    return np.ascontiguousarray(v.reshape(-1, P).T)


def _chunk(wt):
    k = wt.shape[0] // P
    o = np.zeros((P, 8, P), np.float32)
    o[:, :k] = wt.reshape(k, P, P).transpose(1, 0, 2)
    return o.reshape(P, CH)


def _tables():
    n = np.arange(T)
    th = 2 * np.pi * ((n[:, None] * n[None, :]) % (2 * T)) / (2 * T)
    alt = np.where(n % 2 == 0, 1.0, -1.0)
    cf, sf = np.cos(th), np.sin(th)
    sf[:, 0] = alt
    ci, si = np.cos(th) / T, np.sin(th) / T
    ci[0] /= 2
    si[0] = alt / (2 * T)
    return [a.astype(np.float32) for a in (cf, sf, ci, si)]


def _chunks(w_in, w_a, w_cf, w_na, w_hy, w_o, w_fi, w_fo):
    cf, sf, ci, si = _tables()
    cols = lambda a, j: a[:, j * P:(j + 1) * P]
    spectrum = [_chunk(cols(a, j)) for j in range(KT) for a in (cf, sf)]
    off_a, off_q = 0, 3 * DB
    off_hy = off_q + 3 * DB
    off_cf = off_hy + 3 * DB
    off_g = off_cf + 2 * DB
    starts = [off_cf + DB * h + c * P for c in range(NB) for h in range(2)]
    starts += [off_hy + DB * h + c * P for c in range(NB) for h in range(3)]
    starts += [off_a + DB * h + c * P for c in range(NB) for h in range(3)]
    starts += [off_q + c * P for c in range(3 * NB)]
    starts += [off_g + c * P for c in range(N_G)]
    strips = [_chunk(w_in[:, s:s + P]) for s in starts]
    inverse = [_chunk(cols(a, j)) for j in range(KT) for a in (ci, si)]
    branch = [_chunk(np.concatenate([cols(b, 2 * m), cols(b, 2 * m + 1)], 0))
              for b in (w_a, w_cf, w_na, w_hy) for m in range(NB)]
    proj = [_chunk(cols(w_o, d)) for d in range(KT)]
    ffn, m = [], 0
    for gn in FGROUPS:
        for i in range(m, m + gn):
            ffn += [_chunk(cols(w_fi, i)), _chunk(cols(w_fi, FFT + i))]
        ffn += [_chunk(w_fo[m * P:(m + gn) * P, d * P:(d + 1) * P]) for d in range(KT)]
        m += gn
    return np.stack(spectrum + strips + spectrum + inverse + branch + proj + ffn)


def _filter_inputs(w1, w2, w3, w4):
    bands = 16
    t = np.linspace(0.0, 1.0, T, dtype=np.float32)[:, None]
    wv = (2.0 * np.pi * np.arange(T, dtype=np.float32)[:, None] / T).astype(np.float32)
    f = np.linspace(1e-4, bands - 1, bands, dtype=np.float32)[None, :]
    z = np.concatenate([t, np.cos(f * wv), -np.sin(f * wv)], -1).astype(np.float32)
    o = np.zeros((64, 2 * T + 192), np.float32)
    o[0:33, 0:T] = z.T
    o[:, T:2 * T] = w4
    o[0:33, 2 * T:2 * T + 64] = w1
    o[:, 2 * T + 64:2 * T + 128] = w2
    o[:, 2 * T + 128:] = w3
    deltas = np.abs(np.linspace(np.log(1e-2) / 1.5, np.log(1e-2) / 0.3, DB, dtype=np.float32))
    win = (np.exp(-t * deltas[None, :]) + np.float32(0.05)).astype(np.float32)
    return o, np.ascontiguousarray(win.reshape(KT, P, DB).transpose(1, 0, 2))


def _bias_tables(rpb):
    q = np.arange(P)
    half, col = q // GRID, q % GRID
    padded = np.pad(rpb, ((0, 0), (2, 2), (GRID - WIN_W, GRID - WIN_W)))
    x = np.arange(XR)
    dr = x[None, :] + 1 - half[:, None]
    dc = np.arange(GRID)[None, :] - col[:, None] + GRID - 1
    table = padded[:, dr[:, :, None], dc[:, None, :]]
    mask = np.full((P, len(MASKS), NROW, GRID), NEG, np.float32)
    for n, rp in enumerate(MASKS):
        for p in range(P):
            r = 2 * rp + half[p]
            r0 = min(max(r - WIN_H // 2, 0), ROWS - WIN_H) - window_start(rp)
            c0 = min(max(col[p] - WIN_W // 2, 0), GRID - WIN_W)
            mask[p, n, r0:r0 + WIN_H, c0:c0 + WIN_W] = 0.0
    return (np.ascontiguousarray(table.reshape(HEADS, P, XR * GRID)),
            np.ascontiguousarray(mask.reshape(P, len(MASKS), LOC)))


def kernel(x, c, ctx, c_ctx, w_mod, b_mod, g_norm1, g_norm2, w_in, conv_a, w_a_out, q_gain, k_gain, rpb,
           w_na_out, conv_h, filt_w1, filt_b1, filt_w2, filt_b2, filt_w3, filt_b3, filt_w4, filt_freq,
           hy_skip, w_h_out, conv_d, conv_d_b, ln_g, ln_b, w_d_out, w_o, w_ffn_in, w_ffn_out):
    import concourse.bacc as _bacc
    from concourse.bass_utils import run_bass_kernel_spmd as _run

    a = lambda v: np.asarray(v)
    tall = lambda v: np.concatenate([a(v)[0], np.zeros(P - 64, np.float32)])[:, None]
    vec = np.concatenate([
        _tiles(a(g_norm1)[0]), _tiles(a(g_norm2)[0]), np.tile(a(q_gain)[0], 2)[:, None],
        np.tile(a(k_gain)[0], 2)[:, None], _tiles(a(conv_a)[0]), _tiles(a(conv_h)[0]), _tiles(a(hy_skip)[0]),
        _tiles(a(conv_d)[0]), _tiles(a(conv_d_b)[0]), _tiles(a(ln_g)[0]), _tiles(a(ln_b)[0]),
        _tiles(a(b_mod)[0]), np.stack([_tiles(a(c)[0]), _tiles(a(c_ctx))], -1).reshape(P, 2 * KT),
        tall(filt_b1), tall(filt_b2), tall(filt_b3), tall(filt_freq), np.full((P, 1), EPS, np.float32)], 1)
    assert vec.shape[1] == NVEC
    mats = np.zeros((P, 4, P), np.float32)
    mats[:, M_ID] = np.eye(P)
    mats[:, M_ONE] = 1.0
    mats[0:HD, M_HEAD, 0:HD] = 1.0
    mats[HD:, M_HEAD, HD:] = 1.0
    mats[:, M_ALT] = np.where(np.arange(P) % 2 == 0, 1.0, -1.0)[:, None]
    filt, win = _filter_inputs(a(filt_w1)[0], a(filt_w2)[0], a(filt_w3)[0], a(filt_w4)[0])
    gat, masks = _bias_tables(a(rpb)[0])
    arrays = {
        "w": _chunks(a(w_in)[0], a(w_a_out)[0], a(w_d_out)[0], a(w_na_out)[0], a(w_h_out)[0], a(w_o)[0],
                     a(w_ffn_in)[0], a(w_ffn_out)[0]),
        "wmod": np.stack([_chunk(a(w_mod)[0][:, j * P:(j + 1) * P]) for j in range(6 * KT)]),
        "xc": np.ascontiguousarray(np.concatenate([a(x)[0], a(ctx)[0]], 0).T.reshape(KT, P, TC)),
        "vec": np.ascontiguousarray(vec), "mats": mats, "filt": filt, "win": win, "gat": gat, "masks": masks,
    }
    nc = _bacc.Bacc("TRN2", target_bir_lowering=False, num_devices=1)
    args = {n: nc.dram_tensor(f"in_{n}", v.shape, mybir.dt.from_np(v.dtype), kind="ExternalInput").ap()
            for n, v in arrays.items()}
    out = nc.dram_tensor("out", (KT, P, T), F32, kind="ExternalOutput").ap()
    layer_program(nc, **args, out=out)
    r = _run(nc, [{f"in_{n}": v for n, v in arrays.items()}], core_ids=[0])
    return np.ascontiguousarray(r.results[0]["out"].reshape(D, T).T)[None]
```

```python
from contextlib import ExitStack, contextmanager

import numpy as np
import concourse.bass as bass
from concourse import mybir

F32 = mybir.dt.float32
F32R = mybir.dt.float32r
ALU = mybir.AluOpType
ACT = mybir.ActivationFunctionType

P = 128
T = 1024
C = 256
TC = T + C
D = 1024
KT = D // P
KH = KT // 2
DB = 512
NB = DB // P
HALF = 512
HD = 64
HEADS = 8
GRID = 64
ROWS = T // GRID
WIN_H, WIN_W = 8, 16
NROW = 10
LOC = NROW * GRID
KEYS = LOC + C
XR = 18
EPS = 1e-6
NEG = -1e30
FF = 2816
FFT = FF // P
FGROUPS = (8, 7, 7)
CFK = 31
NBR = 4
CH = 8 * P

CK_KDFT = 0
CK_IN = CK_KDFT + KT
N_CF, N_HY, N_A, N_QKV, N_G = 2 * NB, 3 * NB, 3 * NB, 3 * NB, NBR * KT
S_HY = N_CF
S_A = S_HY + N_HY
S_QKV = S_A + N_A
S_G = S_QKV + N_QKV
N_STRIP = S_G + N_G
CK_UDFT = CK_IN + N_STRIP
CK_IDFT = CK_UDFT + KT
CK_Y = CK_IDFT + KT
CK_WO = CK_Y + NBR * NB
CK_FFN = CK_WO + KT
N_CHUNK = CK_FFN + 2 * FFT + KT * len(FGROUPS)
assert N_CHUNK % 4 == 0 and CK_IN % 4 == 0

GATE_OF = (0, 3, 1, 2)
Z_A, Z_CF, Z_NA, Z_HY = range(4)

VEC = {}
_at = 0
for _name, _n in (("g1", KT), ("g2", KT), ("qg", 1), ("kg", 1), ("ca", 3 * NB), ("chy", 9 * NB),
                  ("skip", NB), ("cd", CFK * NB), ("cdb", NB), ("lng", NB), ("lnb", NB),
                  ("bmod", 6 * KT), ("c", 2 * KT), ("fb", 3), ("freq", 1), ("eps", 1)):
    VEC[_name] = _at
    _at += _n
NVEC = _at

M_ID, M_ONE, M_HEAD, M_REV = range(4)


def window_start(rp):
    return min(max(2 * rp - WIN_H // 2, 0), ROWS - NROW)


TAP_BANKS = (4, 5, 7, 0)
MASKS = (0, 2, ROWS // 2 - 1)
MASK_OF = {0: 0, 1: 0, 2: 1, ROWS // 2 - 2: 2, ROWS // 2 - 1: 2}


def y_range(n):
    return (n // 2 * P, P) if n % 2 == 0 else ((KT - 1 - n // 2) * P + 1, P - (n == 1))


class Steps:

    def __init__(self, eng, sem):
        self.eng, self.sem, self.base, self.n = eng, sem, 0, 0

    def mark(self, ins):
        self.n += 1
        ins.then_inc(self.sem, 1)

    def wait(self):
        self.eng.wait_ge(self.sem, self.base + self.n)

    def done(self, ins):
        self.mark(ins)
        self.wait()

    @contextmanager
    def loop(self, count, per):
        start = self.base + self.n
        with self.eng.Fori(0, count) as i:
            self.base, self.n = start + i * per, 0
            yield i
            assert self.n == per, self.n
        self.base, self.n = start + count * per, 0


def layer_program(nc, w, wmod, xc, vec, mats, checker, filt, win, gat, masks, out):
    kspec = nc.dram_tensor("kspec", (KT, P, 2, DB), F32, kind="Internal").ap()
    x0_d = nc.dram_tensor("x0_d", (NB, P, T), F32, kind="Internal").ap()
    u_d = nc.dram_tensor("u_d", (NB, P, T), F32, kind="Internal").ap()
    q_d = [nc.dram_tensor(f"q_{n}_d", (NB, P, T), F32, kind="Internal").ap() for n in ("hi", "lo")]
    k_d = [nc.dram_tensor(f"k_{n}_d", (NB, P, TC), F32, kind="Internal").ap() for n in ("hi", "lo")]
    v_d = nc.dram_tensor("v_d", (NB, P, T), F32, kind="Internal").ap()
    vc_d = nc.dram_tensor("vc_d", (NB, P, C), F32, kind="Internal").ap()
    gate_d = nc.dram_tensor("gate_d", (NBR * KT, P, T), F32, kind="Internal").ap()
    z_d = nc.dram_tensor("z_d", (NBR, NB, P, T), F32, kind="Internal").ap()

    with ExitStack() as ctx:
        def sb(name, shape, dt=F32):
            return ctx.enter_context(nc.sbuf_tensor(name, shape, dt))

        def sem(name):
            return ctx.enter_context(nc.semaphore(name))

        v_sb = sb("v_sb", [P, NVEC])
        m_sb = sb("m_sb", [P, 4, P])
        altr = sb("altr", [P, P], F32R)
        cs = sb("cs", [P, 2 * KT])
        csg = sb("csg", [P, 2 * KT])
        mod = sb("mod", [P, 6 * KT, 2])
        aff = sb("aff", [P, KT, 2])
        aff2 = sb("aff2", [P, KT])
        qg8 = sb("qg8", [P, 1])
        gate0 = sb("gate0", [P, 2])
        st_nm = sb("st_nm", [P, 2])
        st_m = sb("st_m", [P, 2])
        st_l = sb("st_l", [P, 2])
        st_r = sb("st_r", [P, 2])
        ident = m_sb[:, M_ID, :]
        ones = m_sb[:, M_ONE, :]
        heads = m_sb[:, M_HEAD, :]
        rev = m_sb[:, M_REV, :]

        floor = (nc.sbuf_base + 63) // 64 * 64
        room = nc.sbuf_usable_end - floor
        KB = 1024

        def at(name, kb, shape, dt=F32):
            size = int(np.prod(shape[1:])) * 4
            off = int(kb * KB)
            assert off + size <= room, (name, off + size, room)
            return nc.alloc_sbuf_tensor_at(name, shape, dt, offset=floor + off)

        raw = at("raw", 0, [P, 4, CH])
        whi = at("whi", 16, [P, 2, CH], F32R)
        wlo = at("wlo", 24, [P, 2, CH], F32R)
        h_hi = at("h_hi", 32, [P, KT, T], F32R)
        h_lo = at("h_lo", 64, [P, KT, T], F32R)
        c_hi = at("c_hi", 96, [P, KT, C], F32R)
        c_lo = at("c_lo", 104, [P, KT, C], F32R)
        mraw = at("mraw", 112, [P, 2, CH])
        mprod = at("mprod", 199, [P, CH])
        macc = at("macc", 152, [P, 2, P])
        alt_f = at("alt_f", 96, [P, P])
        mrow = at("mrow", 199, [2, 2, HALF])
        ab = at("ab", 96, [P, 2, 2, 2, DB])
        xk_hi = at("xk_hi", 117, [P, DB], F32R)
        xk_lo = at("xk_lo", 93.5, [P, DB], F32R)
        e_hi = at("e_hi", 120, [P, KT, DB], F32R)
        e_lo = at("e_lo", 136, [P, KT, DB], F32R)
        o_hi = at("o_hi", 152, [P, KT, DB], F32R)
        o_lo = at("o_lo", 168, [P, KT, DB], F32R)
        xs = at("xs", 184, [P, 2, TC])
        hx = [xs[:, 0, :], xs[:, 1, :], at("hx2", 112, [P, TC])[:, :]]
        rstd = at("rstd", 194, [P, TC])
        ksp = at("ksp", 199, [P, 2, DB])
        f_sb = at("f_sb", 32, [64, 2 * T + 3 * 64])
        f_w4 = at("f_w4", 41, [64, 2, DB])
        f_a = at("f_a", 45, [64, T])
        f_k = at("f_k", 49, [64, T])
        f_h = at("f_h", 53, [64, T])
        eo = at("eo", 57, [P, 2, 2, DB])
        win_sb = at("win_sb", 65, [P, KT + 1, DB])
        nv = at("nv", 83, [P, TC])
        nt = at("nt", 88, [P, TC])
        sqs = at("sqs", 194, [P, TC])
        cfm = at("cfm", 120, [P, NB, T + CFK - 1])
        cfo = at("cfo", 136.5, [P, NB, T])
        st = at("st", 153, [P, 6, T + 8])
        cvo = at("cvo", 178, [P, 3, T])
        n_hi = at("n_hi", 178, [P, 2, TC], F32R)
        n_lo = at("n_lo", 188, [P, 2, TC], F32R)
        v_late = at("v_late", 144, [P, 2, T])
        cst = at("cst", 198, [P, 4, C])
        q_t = at("q_t", 137, [P, TC])
        q_r = at("q_r", 142, [P, TC])
        q_v = at("q_v", 147, [P, TC])
        lsq = at("lsq", 96, [P, NB, T])
        l_r = at("l_r", 116, [P, T])
        l_v = at("l_v", 124, [P, T])
        l_t = at("l_t", 128, [P, T])
        u_f = at("u_f", 185, [P, NB, T])
        ub = at("ub", 32, [P, NB, T])
        xu_hi = at("xu_hi", 112, [P, DB], F32R)
        xu_lo = at("xu_lo", 114, [P, DB], F32R)
        u_hi = at("u_hi", 153, [P, KT, DB], F32R)
        u_lo = at("u_lo", 169, [P, KT, DB], F32R)
        a_m = at("a_m", 96, [P, len(MASKS), LOC])
        a_vt = at("a_vt", 103.5, [P, 10, P])
        a_o = at("a_o", 115.5, [P, ROWS // 2, P])
        a_pt = at("a_pt", 108.5, [P, 2, KEYS])
        gst = at("gst", 152.5, [P, 2, T])
        a_q = [at(f"a_q{e}", 160.5 + 4 * e, [P, T], F32R) for e in range(2)]
        a_k = [at(f"a_k{e}", 168.5 + 5 * e, [P, TC], F32R) for e in range(2)]
        a_kl = at("a_kl", 178.5, [P, TC], F32R)
        a_v = at("a_v", 164.5, [P, T])
        a_vc = at("a_vc", 173.5, [P, C])
        a_g = [at(f"a_g{e}", 183.5 + 4.5 * e, [P, XR * GRID]) for e in range(2)]
        a_s = at("a_s", 192.5, [P, 2, KEYS])
        a_b = at("a_b", 199.5, [P, KEYS])
        pr_hi = at("pr_hi", 32, [P, KT, DB], F32R)
        pr_lo = at("pr_lo", 48, [P, KT, DB], F32R)
        ps_hi = at("ps_hi", 64, [P, KT, DB], F32R)
        ps_lo = at("ps_lo", 80, [P, KT, DB], F32R)
        k_sb = at("k_sb", 96, [P, 2, 2, DB])
        pw = at("pw", 120, [P, 2, 4, DB])
        x0_f = at("x0_f", 120, [P, NB, T])
        xn_hi = at("xn_hi", 108, [P, DB], F32R)
        xn_lo = at("xn_lo", 110, [P, DB], F32R)
        y_b = at("y_b", 201, [P, DB])
        y5w = at("y5w", 203, [P, NB])
        y_t = at("y_t", 112, [P, 2, DB])
        y_w = at("y_w", 116, [P, 2, NB, P])
        z_hi = [at("z_hi0", 153, [P, NB, T], F32R), at("z_hi1", 32, [P, NB, T], F32R)]
        z_lo = [at("z_lo0", 169, [P, NB, T], F32R), at("z_lo1", 48, [P, NB, T], F32R)]
        mrg = at("mrg", 64, [P, KT, T])
        gt = at("gt", 96, [P, 3, T])
        zraw = at("zraw", 136, [P, NB, T])
        yt = at("yt", 185, [P, T])
        m_hi = at("m_hi", 120, [P, KT, T], F32R)
        m_lo = at("m_lo", 152, [P, KT, T], F32R)
        x1 = at("x1", 32, [P, KT, T])
        sq2 = at("sq2", 96, [P, 2, T])
        r2 = at("r2", 185, [P, T])
        v2 = at("v2", 189, [P, T])
        t2 = at("t2", 193, [P, T])
        h2_hi = at("h2_hi", 64, [P, KT, T], F32R)
        h2_lo = at("h2_lo", 96, [P, KT, T], F32R)
        ht = at("ht", 160, [P, 4, HALF])
        g_hi = at("g_hi", 128, [P, 8, T], F32R)
        g_lo = at("g_lo", 160, [P, 8, T], F32R)
        sg = at("sg", 192, [P, T])
        gm = at("gm", 196, [P, T])

        ps = ctx.enter_context(nc.psum_tensor("ps", [P, 8 * HALF], F32))

        def bank(b, n=1, width=None):
            return ps[:, b * HALF:b * HALF + (width or n * HALF)]

        s_const = sem("s_const")
        s_filt = sem("s_filt")
        s_win = sem("s_win")
        s_raw = [sem(f"s_raw{i}") for i in range(4)]
        s_hi = sem("s_hi")
        s_split = sem("s_split")
        s_used = sem("s_used")
        s_gate = sem("s_gate")
        s_mraw = [sem(f"s_mraw{i}") for i in range(2)]
        s_mused = sem("s_mused")
        s_csg = sem("s_csg")
        s_cs = sem("s_cs")
        s_xs = [sem(f"s_xs{i}") for i in range(2)]
        s_hx = [sem(f"s_hx{i}") for i in range(3)]
        s_sq = sem("s_sq")
        s_ss = sem("s_ss")
        s_sum = sem("s_sum")
        s_mrow = sem("s_mrow")
        s_mrowc = sem("s_mrowc")
        s_mcol = sem("s_mcol")
        s_fmm = sem("s_fmm")
        s_fred = sem("s_fred")
        s_fsin = sem("s_fsin")
        s_w4 = sem("s_w4")
        s_eomm = sem("s_eomm")
        s_eoev = sem("s_eoev")
        s_eo = sem("s_eo")
        s_eohi = sem("s_eohi")
        s_eolo = sem("s_eolo")
        s_alt = sem("s_alt")
        s_ny = sem("s_ny")
        s_r0 = sem("s_r0")
        s_nv = sem("s_nv")
        s_ht = sem("s_ht")
        s_hh = sem("s_hh")
        s_hlo = sem("s_hlo")
        s_ev = sem("s_ev")
        s_kst = sem("s_kst")
        s_cfm = sem("s_cfm")
        s_grpout = sem("s_grpout")
        s_cvst = sem("s_cvst")
        s_cacc = sem("s_cacc")
        s_cev = sem("s_cev")
        s_qsq = sem("s_qsq")
        s_qones = sem("s_qones")
        s_qr = sem("s_qr")
        s_qfree = sem("s_qfree")
        s_qn = sem("s_qn")
        s_nh = sem("s_nh")
        s_nl = sem("s_nl")
        s_nst = [sem(f"s_nst{i}") for i in range(2)]
        s_vst = sem("s_vst")
        s_vlate = sem("s_vlate")
        s_gst = [sem(f"s_gst{i}") for i in range(2)]
        s_gh = sem("s_gh")
        s_macc = sem("s_macc")
        s_mfree = sem("s_mfree")
        s_modev = sem("s_modev")
        s_conv = sem("s_conv")
        s_l1 = sem("s_l1")
        s_lx = sem("s_lx")
        s_lsq = sem("s_lsq")
        s_l2 = sem("s_l2")
        s_lr = sem("s_lr")
        s_lf = sem("s_lf")
        s_ly = sem("s_ly")
        s_lz = sem("s_lz")
        s_zst = sem("s_zst")
        s_uld = [sem(f"s_uld{c}") for c in range(NB)]
        s_fold = sem("s_fold")
        s_un = sem("s_un")
        s_ut = sem("s_ut")
        s_uhi = sem("s_uhi")
        s_ulo = sem("s_ulo")
        s_hld = [sem(f"s_hld{i}") for i in range(2)]
        s_vld = sem("s_vld")
        s_avt = sem("s_avt")
        s_avev = sem("s_avev")
        s_as = sem("s_as")
        s_attr = sem("s_attr")
        s_anm = sem("s_anm")
        s_aexp = sem("s_aexp")
        s_at = sem("s_at")
        s_aeva = sem("s_aeva")
        s_aevd = sem("s_aevd")
        s_apv = sem("s_apv")
        s_ao = sem("s_ao")
        s_azt = sem("s_azt")
        s_azev = sem("s_azev")
        s_azst = sem("s_azst")
        s_k = [sem(f"s_k{i}") for i in range(2)]
        s_udev = sem("s_udev")
        s_pr = sem("s_pr")
        s_prhi = sem("s_prhi")
        s_prlo = sem("s_prlo")
        s_x0 = sem("s_x0")
        s_xn = sem("s_xn")
        s_y5 = sem("s_y5")
        s_y5c = sem("s_y5c")
        s_y5t = sem("s_y5t")
        s_y5z = sem("s_y5z")
        s_idb = sem("s_idb")
        s_yt = sem("s_yt")
        s_idt = sem("s_idt")
        s_idz = sem("s_idz")
        s_idst = [sem(f"s_idst{i}") for i in range(2)]
        s_zld = sem("s_zld")
        s_zhi = sem("s_zhi")
        s_zlo = sem("s_zlo")
        s_gld = [sem(f"s_gld{i}") for i in range(3)]
        s_y = sem("s_y")
        s_yev = sem("s_yev")
        s_mg = sem("s_mg")
        s_mhi = sem("s_mhi")
        s_mlo = sem("s_mlo")
        s_x1 = sem("s_x1")
        s_woev = sem("s_woev")
        s_sq2 = sem("s_sq2")
        s_one2 = sem("s_one2")
        s_r2 = sem("s_r2")
        s_v2 = sem("s_v2")
        s_mod1 = sem("s_mod1")
        s_t2 = sem("s_t2")
        s_h2h = sem("s_h2h")
        s_h2 = sem("s_h2")
        s_sil = sem("s_sil")
        s_up = sem("s_up")
        s_ghi = sem("s_ghi")
        s_glo = sem("s_glo")
        s_foev = sem("s_foev")
        s_out = sem("s_out")
        s_dve = sem("s_dve")
        s_act = sem("s_act")

        def row(t, i):
            return t[bass.ds(i, 1)].rearrange("o p t -> (o p) t")

        def both(v, t):
            return v.rearrange("p (s k) f -> p s k f", s=2)[:, :, t, :]

        def vcol(name, i=0, n=1):
            return v_sb[:, VEC[name] + i:VEC[name] + i + n]

        block = ctx.enter_context(nc.Block())

        @block.sync
        def _(sp):
            def mod_chunk(n, slot):
                sp.dma_start(mraw[:, slot, :], wmod[n]).then_inc(s_mraw[slot], 16)

            sp.dma_start(f_sb[:, :], filt).then_inc(s_filt, 16)
            for k in range(KT):
                if k >= 2:
                    sp.wait_ge(s_ss, k - 1)
                sp.dma_start(xs[:, k % 2, :], xc[k]).then_inc(s_xs[k % 2], 16)
                for j in range(2):
                    if k >= 1:
                        sp.wait_ge(s_mused, 2 * k + j - 1)
                    mod_chunk(2 * k + j, j)
                if k == 1:
                    sp.dma_start(win_sb[:, :, :], win).then_inc(s_win, 16)

            def main_chunks(i, first=False):
                for j in range(4):
                    if not first:
                        sp.wait_ge(s_split, 4 * i + j - 3)
                    sp.dma_start(raw[:, j, :], w[4 * i + j]).then_inc(s_raw[j], 16)

            main_chunks(0, first=True)
            n_k = CK_IN // 4
            n_m = 32 // 4
            with sp.Fori(1, n_k) as i:
                main_chunks(i)
            main_chunks(n_k)
            sp.wait_ge(s_hlo, KT)
            for m in range(4):
                if m < 2:
                    sp.wait_ge(s_mused, 2 * KT)
                else:
                    sp.wait_ge(s_mfree, m - 1)
                mod_chunk(2 * KT + m, m % 2)
            with sp.Fori(n_k + 1, n_k + n_m) as i:
                main_chunks(i)
                for j in range(4):
                    m = 4 * (i - n_k) + j
                    sp.wait_ge(s_mfree, m - 1)
                    mod_chunk(2 * KT + m, j % 2)
            n_g = (CK_IN + S_G) // 4
            with sp.Fori(n_k + n_m, n_g + 1) as i:
                main_chunks(i)
            for i in range(2):
                sp.wait_ge(s_nst[i], 32 * NB)
            sp.wait_ge(s_vst, 32 * (NB - 2))
            sp.wait_ge(s_cvst, 16 * 3 * NB)
            def rows64(dram, i, e):
                return row(dram, i)[e * HD:(e + 1) * HD, :]

            def head_in(hp, e):
                own, other = slice(e * HD, (e + 1) * HD), slice((1 - e) * HD, (2 - e) * HD)
                sp.dma_start(a_q[e][own, :].bitcast(F32), rows64(q_d[0], hp, e)).then_inc(s_hld[e], 16)
                sp.dma_start(a_q[e][other, :].bitcast(F32), rows64(q_d[1], hp, e)).then_inc(s_hld[e], 16)
                sp.dma_start(a_k[e][own, :].bitcast(F32), rows64(k_d[0], hp, e)).then_inc(s_hld[e], 16)
                sp.dma_start(a_k[e][other, :].bitcast(F32), rows64(k_d[0], hp, e)).then_inc(s_hld[e], 16)
                sp.dma_start(a_kl[own, :].bitcast(F32), rows64(k_d[1], hp, e)).then_inc(s_hld[e], 16)
                sp.dma_start(a_g[e][:, :], row(gat, 2 * hp + e)).then_inc(s_hld[e], 16)

            def values_load(hp):
                sp.dma_start(a_v[:, :], row(v_d, hp)).then_inc(s_vld, 16)
                sp.dma_start(a_vc[:, :], row(vc_d, hp)).then_inc(s_vld, 16)

            head_in(0, 0)
            sp.wait_ge(s_cacc, 2 * NB)
            sp.dma_start(a_m[:, :, :], masks).then_inc(s_azst, 16)
            sp.wait_ge(s_vlate, 64)
            values_load(0)
            sp.wait_ge(s_avt, 1)
            head_in(0, 1)
            main_chunks(n_g + 1)
            with sp.Fori(1, NB) as hp:
                sp.wait_ge(s_as, 16 * hp - 8)
                sp.wait_ge(s_attr, 16 * hp - 8)
                head_in(hp, 0)
                main_chunks(n_g + 2 * hp)
                sp.wait_ge(s_as, 16 * hp)
                sp.wait_ge(s_attr, 16 * hp)
                values_load(hp)
                sp.wait_ge(s_avt, hp + 1)
                head_in(hp, 1)
                main_chunks(n_g + 2 * hp + 1)
            main_chunks(CK_UDFT // 4)

            sp.wait_ge(s_attr, 16 * NB)
            for c in range(NB):
                if c == 1:
                    sp.wait_ge(s_at, 16 * NB)
                sp.dma_start(u_f[:, c, :], u_d[c]).then_inc(s_uld[c], 16)
            with sp.Fori(CK_UDFT // 4 + 1, N_CHUNK // 4) as i:
                main_chunks(i)
            for d in range(KT):
                sp.wait_ge(s_foev, 2 * KT + d + 1)
                sp.dma_start(out[d], x1[:, d, :]).then_inc(s_out, 16)
            sp.wait_ge(s_out, 16 * KT)

        @block.gpsimd
        def _(pool):
            def split(i, first=False):
                for j in range(4):
                    n = 4 * i + j
                    pool.wait_ge(s_raw[j], 16 * (i + 1))
                    if not (first and j < 2):
                        pool.wait_ge(s_used, n - 1)
                    nc.gpsimd.tensor_tensor(gate0[:, 1:2], gate0[:, 0:1], gate0[:, 0:1], ALU.add)
                    nc.gpsimd.tensor_scalar(whi[:, j % 2, :], raw[:, j, :], 1.0, 0.0, ALU.mult,
                                            ALU.add).then_inc(s_hi, 1)
                    pool.wait_ge(s_hi, n + 1)
                    nc.gpsimd.tensor_tensor(wlo[:, j % 2, :], raw[:, j, :], whi[:, j % 2, :].bitcast(F32),
                                            ALU.subtract).then_inc(s_split, 1)

            nc.gpsimd.memset(gate0[:, :], 0.0).then_inc(s_gate, 1)
            pool.wait_ge(s_gate, 1)
            for k in range(KT):
                pool.wait_ge(s_sq, k + 1)
                if k == 0:
                    nc.gpsimd.tensor_scalar(sqs[:, :], xs[:, 0, :], 1.0, 0.0, ALU.mult, ALU.add).then_inc(s_ss, 1)
                else:
                    nc.gpsimd.tensor_tensor(sqs[:, :], sqs[:, :], xs[:, k % 2, :], ALU.add).then_inc(s_ss, 1)
                pool.wait_ge(s_ss, k + 1)
            split(0, first=True)
            with pool.Fori(1, N_CHUNK // 4) as i:
                split(i)

        @block.tensor
        def _(pe):
            def chunk_in(n):
                pe.wait_ge(s_split, n + 1)

            def mm3(o, slot, k, hi, lo, start, stop):
                a, b = whi[:, slot, k * P:(k + 1) * P], wlo[:, slot, k * P:(k + 1) * P]
                nc.tensor.matmul(o, a, hi, start=start, stop=False)
                nc.tensor.matmul(o, a, lo, start=False, stop=False)
                return nc.tensor.matmul(o, b, hi, start=False, stop=stop)

            def strip(slot, b0, hi, lo, ks=KT, sk=0, halves=(0, 1)):
                for half in halves:
                    for k in range(ks):
                        t = slice(half * HALF, (half + 1) * HALF)
                        mm = mm3(bank(b0 + half), slot, sk + k, hi[:, k, t], lo[:, k, t], k == 0, k == ks - 1)
                return mm

            def strip_parts(slot, b0, hi, lo, ks, early, sem_rest, count):
                for k0, k1 in ((0, early), (early, ks)):
                    if k0:
                        pe.wait_ge(sem_rest, count)
                    for half in range(2):
                        t = slice(half * HALF, (half + 1) * HALF)
                        for k in range(k0, k1):
                            mm = mm3(bank(b0 + half), slot, k, hi[:, k, t], lo[:, k, t], k == 0, k == ks - 1)
                return mm

            def filter_layer(n, lhsT, rhs):
                for half in range(2):
                    t = slice(half * HALF, (half + 1) * HALF)
                    mm = nc.tensor.matmul(bank(4 + half)[0:64, :], lhsT, rhs[:, t], start=True, stop=True)
                mm.then_inc(s_fmm, 1)

            def mod_rows(n):
                g, kk = divmod(n, KT // 2)
                pe.wait_ge(s_mraw[n % 2], 16 * (n // 2 + 1))
                for i in range(2):
                    k = 2 * kk + i
                    mm = nc.tensor.matmul(bank(2 + g % 2)[0:2, :], cs[:, 2 * k:2 * k + 2],
                                          mraw[:, n % 2, i * HALF:(i + 1) * HALF], start=k == 0, stop=k == KT - 1)
                mm.then_inc(s_mused, 1)
                if kk == KT // 2 - 1:
                    nc.tensor.matmul(bank(6)[0:2, HALF - 2:HALF], ident[0:2, 0:2], ident[0:2, 0:2],
                                     start=True, stop=True).then_inc(s_mrow, 1)

            def mod_columns(g):
                pe.wait_ge(s_mrowc, g + 1)
                for i in range(4):
                    o = 6 * HALF + 2 * (4 * g + i)
                    mm = nc.tensor.matmul(ps[:, o:o + 2], mrow[:, g % 2, i * P:(i + 1) * P], ident[0:2, 0:2],
                                          start=True, stop=True)
                mm.then_inc(s_mcol, 1)

            pe.wait_ge(s_filt, 16)
            filter_layer(0, f_sb[0:33, 2 * T:2 * T + 64], f_sb[0:33, 0:T])
            pe.wait_ge(s_const, 48)
            pe.wait_ge(s_cs, 1)

            def taps(i):
                for j in range(2 if i < KH else 1):
                    for part in range(2):
                        n = 4 * i + 2 * j + part
                        if n >= 4:
                            pe.wait_ge(s_eoev, n - 3)
                        c0 = (i + KH * j) * P if i < KH else HALF - 64 * part
                        nc.tensor.matmul(bank(TAP_BANKS[n % 4]), f_h[:, c0:c0 + P], f_w4[:, part, :],
                                         start=True, stop=True).then_inc(s_eomm, 1)

            for k in range(KT):
                for j in range(2):
                    mod_rows(2 * k + j)
                if k in (2, 4, 6):
                    mod_columns(k // 2 - 1)
                if k == 1:
                    pe.wait_ge(s_fsin, 1)
                    filter_layer(1, f_sb[:, 2 * T + 64:2 * T + 128], f_h)
                if k == 3:
                    pe.wait_ge(s_fsin, 2)
                    filter_layer(2, f_sb[:, 2 * T + 128:2 * T + 192], f_h)
                if k >= 5:
                    if k == 5:
                        pe.wait_ge(s_fsin, 3)
                        pe.wait_ge(s_w4, 1)
                    taps(k - 5)
            pe.wait_ge(s_ss, KT)
            pe.wait_ge(s_mrowc, KT // 2)
            for b, n in ((0, HALF), (1, HALF), (2, C)):
                mm = nc.tensor.matmul(bank(1 + b, width=n), ones, sqs[:, b * HALF:b * HALF + n], start=True, stop=True)
            mm.then_inc(s_sum, 1)
            mod_columns(KT // 2 - 1)
            taps(KH - 1)
            taps(KH)
            pe.wait_ge(s_eolo, KH + 1)
            pe.wait_ge(s_alt, 1)
            pe.wait_ge(s_eoev, 2 * KT + 2)

            def nyquist(hi, lo, x_hi, x_lo):
                for t in range(KH):
                    nc.tensor.matmul(bank(4), altr[:, :], hi[:, t, :], start=t == 0, stop=False)
                    nc.tensor.matmul(bank(4), altr[:, :], lo[:, t, :], start=False, stop=False)
                nc.tensor.matmul(bank(4), altr[0:1, :], x_hi[0:1, :], start=False, stop=False)
                return nc.tensor.matmul(bank(4), altr[0:1, :], x_lo[0:1, :], start=False, stop=True)

            def folded(o, slot, part, hi, lo, side, x=None, start=True, stop=True):
                if x:
                    for i, v in enumerate(x):
                        nc.tensor.matmul(o, altr[v[1]:v[1] + 1, :], v[0][v[1]:v[1] + 1, :], start=start and i == 0,
                                         stop=False)
                for k in range(KH):
                    mm = mm3(o, slot, KH * part + k, hi[:, KH * side + k, :], lo[:, KH * side + k, :],
                             start and k == 0 and not x, stop and k == KH - 1)
                return mm

            def spectrum(q, slot, c, s, odd, xc_, xs_):
                folded(bank(2 * slot), slot, 0, *c, side=int(odd), x=None if odd else xc_)
                return folded(bank(2 * slot + 1), slot, 1, *s, side=int(not odd), x=xs_ if odd else None)

            nyquist(e_hi, e_lo, xk_hi, xk_lo).then_inc(s_ny, 1)
            pe.wait_ge(s_nv, 1)
            pe.wait_ge(s_r0, 1)

            def kdft(i, odd, first=False):
                for j in range(2):
                    q = 2 * i + j
                    if not first:
                        pe.wait_ge(s_ev, q - 1)
                    chunk_in(CK_KDFT + q)
                    spectrum(q, j, (e_hi, e_lo), (o_hi, o_lo), odd, ((xk_hi, 0), (xk_lo, 0)),
                             ((xk_hi, 64), (xk_lo, 64))).then_inc(s_used, 1)

            kdft(0, False, first=True)
            kdft(1, False)
            with pe.Fori(KH // 2, KH) as i:
                kdft(i, True)

            pe.wait_ge(s_hlo, KT)

            def in_strip(n, j):
                chunk_in(CK_IN + n)
                pe.wait_ge(s_ev, n + KT - 1)
                strip(j, 2 * j, h_hi, h_lo).then_inc(s_used, 1)

            with pe.Fori(0, S_QKV // 2) as i:
                for j in range(2):
                    in_strip(2 * i + j, j)
                    pe.wait_ge(s_macc, 2 * i + j + 1)
                    nc.tensor.matmul(ps[:, bass.ds(6 * HALF + 4 * KT + 4 * i + 2 * j, 2)], macc[:, j, :], ones[:, 0:2],
                                     start=True, stop=True).then_inc(s_mused, 1)

            def q_ones(t):
                pe.wait_ge(s_qsq, t + 1)
                if t == 0:
                    pe.wait_ge(s_modev, 1)
                if t >= NB:
                    pe.wait_ge(s_cev, t - NB + 1)
                if t:
                    pe.wait_ge(s_qfree, t)
                    pe.wait_ge(s_qr, t)
                for half in range(2):
                    mm = nc.tensor.matmul(bank(6 + half), heads, q_t[:, half * HALF:(half + 1) * HALF],
                                          start=True, stop=True)
                if t >= NB:
                    mm = nc.tensor.matmul(bank(4 + t % 2)[:, C:2 * C], heads, q_t[:, T:TC], start=True, stop=True)
                mm.then_inc(s_qones, 1)

            for t in range(N_QKV):
                n, j = S_QKV + t, t % 2
                if t < NB:
                    in_strip(n, j)
                else:
                    chunk_in(CK_IN + n)
                    pe.wait_ge(s_ev, n + KT - 1)
                    strip(j, 2 * j, h_hi, h_lo, halves=(0,))
                    if t >= NB + 2:
                        pe.wait_ge(s_cev, t - NB - 1)
                        if t - 2 < 2 * NB:
                            pe.wait_ge(s_qfree, t - 1)
                            pe.wait_ge(s_qr, t - 1)
                    for k in range(KT):
                        mm = mm3(bank(4 + j, width=C), j, k, c_hi[:, k, :], c_lo[:, k, :], k == 0, k == KT - 1)
                    mm.then_inc(s_cacc, 1)
                    strip(j, 2 * j, h_hi, h_lo, halves=(1,)).then_inc(s_used, 1)
                if 1 <= t <= 2 * NB:
                    q_ones(t - 1)

            def gate_half(hp, it, k0=0, k1=KT):
                m, half = 8 * hp + it // 2, it % 2
                t = slice(half * HALF, (half + 1) * HALF)
                if half == 0:
                    chunk_in(CK_IN + S_G + m)
                if k0 == 0:
                    pe.wait_ge(s_ev, KT + S_G + 16 * hp + it - 1)
                for k in range(k0, k1):
                    mm = mm3(bank(half), it // 2 % 2, k, h_hi[:, k, t], h_lo[:, k, t], k == 0, k == KT - 1)
                if k1 == KT:
                    mm.then_inc(s_used if half else s_gh, 1)

            def values_in(hp):
                pe.wait_ge(s_ev, KT + S_G + 16 * hp + 1)
                pe.wait_ge(s_vld, 32 * (hp + 1))
                for t in range(8):
                    nc.tensor.transpose(ps[:, 4 * HALF + t * P:4 * HALF + (t + 1) * P],
                                        a_v[:, t * P:(t + 1) * P], ident)
                for t in range(2):
                    mm = nc.tensor.transpose(ps[:, 6 * HALF + t * P:6 * HALF + (t + 1) * P],
                                             a_vc[:, t * P:(t + 1) * P], ident)
                mm.then_inc(s_avt, 1)

            def scores(hp, it):
                e, rp = divmod(it, 8)
                if rp == 0:
                    pe.wait_ge(s_hld[e], 96 * (hp + 1))
                if it == 0:
                    pe.wait_ge(s_ev, KT + S_G + 16 * hp)
                if it:
                    pe.wait_ge(s_attr, 16 * hp + it)
                hs = slice(e * HD, (e + 1) * HD)
                q = slice(rp * P, (rp + 1) * P)
                k0 = window_start(rp) * GRID
                for o, keys in ((bank(2)[:, 0:C], slice(T, TC)), (bank(2)[:, C:HALF], slice(k0, k0 + HALF - C)),
                                (bank(3)[:, 0:KEYS - HALF], slice(k0 + HALF - C, k0 + LOC))):
                    nc.tensor.matmul(o, a_q[e][:, q], a_k[e][:, keys], start=True, stop=False)
                    mm = nc.tensor.matmul(o, a_q[e][hs, q], a_kl[hs, keys], start=False, stop=True)
                mm.then_inc(s_as, 1)

            def turn(hp, it):
                if it == 0:
                    pe.wait_ge(s_avev, hp + 1)
                else:
                    pe.wait_ge(s_aeva, 16 * hp + it)
                    pe.wait_ge(s_aevd, 16 * hp + it)
                pe.wait_ge(s_aexp, 16 * hp + it + 1)
                for b in range(7):
                    mm = nc.tensor.transpose(ps[:, 4 * HALF + b * P:4 * HALF + (b + 1) * P],
                                             a_s[:, it % 2, b * P:(b + 1) * P], ident)
                mm.then_inc(s_at, 1)

            def values(hp, it):
                e, rp = divmod(it, 8)
                pe.wait_ge(s_aeva, 16 * hp + it + 1)
                pe.wait_ge(s_aevd, 16 * hp + it + 1)
                if it >= 2:
                    pe.wait_ge(s_ao, 16 * hp + it - 1)
                v0 = window_start(rp) // 2
                for b in range(7):
                    tile = 8 + b if b < 2 else v0 + b - 2
                    mm = nc.tensor.matmul(bank(6 + it % 2)[:, 0:HD], a_pt[:, it % 2, b * P:(b + 1) * P],
                                          a_vt[:, tile, e * HD:(e + 1) * HD], start=b == 0, stop=b == 6)
                mm.then_inc(s_apv, 1)

            with pe.Fori(0, NB) as hp:
                for it in range(16):
                    if it < 15:
                        gate_half(hp, it)
                    if it == 1:
                        values_in(hp)
                    scores(hp, it)
                    if it:
                        turn(hp, it - 1)
                    if it >= 2:
                        values(hp, it - 2)
                gate_half(hp, 15, 0, KT // 2)
                turn(hp, 15)
                values(hp, 14)
                gate_half(hp, 15, KT // 2, KT)
                values(hp, 15)
                pe.wait_ge(s_ao, 16 * hp + 16)
                for rp in range(8):
                    mm = nc.tensor.transpose(ps[:, 4 * HALF + rp * P:4 * HALF + (rp + 1) * P], a_o[:, rp, :], ident)
                mm.then_inc(s_azt, 1)

            pe.wait_ge(s_conv, NB)
            pe.wait_ge(s_azev, NB)
            for half in range(2):
                for c in range(NB):
                    mm = nc.tensor.matmul(bank(4 + half), ones, cfo[:, c, half * HALF:(half + 1) * HALF],
                                          start=c == 0, stop=c == NB - 1)
            mm.then_inc(s_l1, 1)
            pe.wait_ge(s_fold, NB)
            pe.wait_ge(s_ev, KT + S_G + 2 * N_G)
            for t in range(KT + 1):
                if t >= 4:
                    pe.wait_ge(s_ulo, t - 3)
                for c in range(NB):
                    x = ub[:, c, t * P:(t + 1) * P] if t < KT else u_f[:, c, HALF:HALF + P]
                    mm = nc.tensor.transpose(bank(t % 4)[:, c * P:(c + 1) * P], x, ident)
                mm.then_inc(s_ut, 1)
            for c in range(NB):
                pe.wait_ge(s_lsq, c + 1)
                for half in range(2):
                    mm = nc.tensor.matmul(bank(6 + half), ones, lsq[:, c, half * HALF:(half + 1) * HALF],
                                          start=c == 0, stop=c == NB - 1)
                mm.then_inc(s_l2, 1)
            pe.wait_ge(s_ulo, KT + 1)
            pe.wait_ge(s_lx, NB)

            nyquist(u_hi, u_lo, xu_hi, xu_lo).then_inc(s_un, 1)

            def udft(i, odd, first=False):
                for j in range(2):
                    q = 2 * i + j
                    if not first:
                        pe.wait_ge(s_udev, q - 1)
                    chunk_in(CK_UDFT + q)
                    spectrum(q, j, (u_hi, u_lo), (u_hi, u_lo), odd, ((xu_hi, 0), (xu_lo, 0)),
                             ((xu_hi, 0), (xu_lo, 0))).then_inc(s_used, 1)

            udft(0, False, first=True)
            udft(1, False)
            with pe.Fori(KH // 2, KH) as i:
                udft(i, True)
            pe.wait_ge(s_udev, KT - 1)
            pe.wait_ge(s_prlo, KH)
            pe.wait_ge(s_xn, 1)
            pe.wait_ge(s_lf, 1)
            pe.wait_ge(s_lr, 1)
            def inverse(i):
                b = 2 * (i % 2)
                if i >= 2:
                    pe.wait_ge(s_yt, 2 * i - 2)
                chunk_in(CK_IDFT + 2 * i)
                folded(bank(b), 0, 0, pr_hi, pr_lo, 0, x=((xn_hi, 0), (xn_lo, 0)), stop=False)
                if i == 0:
                    pe.wait_ge(s_prlo, KT)
                folded(bank(b), 0, 1, ps_hi, ps_lo, 1, start=False).then_inc(s_used, 1)
                chunk_in(CK_IDFT + 2 * i + 1)
                folded(bank(b + 1), 1, 0, pr_hi, pr_lo, 1, stop=False)
                folded(bank(b + 1), 1, 1, ps_hi, ps_lo, 0, start=False).then_inc(s_used, 1)

            def back(n):
                slot = n % 2
                pe.wait_ge(s_yt, n + 1)
                if n >= 2:
                    pe.wait_ge(s_idz, n - 1)
                for c in range(NB):
                    o, y = bank(4 + slot)[:, c * P:(c + 1) * P], y_t[:, slot, c * P:(c + 1) * P]
                    if slot == 0:
                        mm = nc.tensor.transpose(o, y, ident)
                    else:
                        mm = nc.tensor.matmul(o, y, rev, start=True, stop=True)
                mm.then_inc(s_idt, 1)

            inverse(0)
            for n, (v, t0) in enumerate(((pr_hi, 0), (pr_lo, 0), (ps_hi, KH), (ps_lo, KH))):
                for k in range(KH):
                    nc.tensor.matmul(bank(6), altr[:, :], v[:, t0 + k, :], start=n == 0 and k == 0, stop=False)
            nc.tensor.matmul(bank(6), altr[0:1, :], xn_hi[0:1, :], start=False, stop=False)
            nc.tensor.matmul(bank(6), altr[0:1, :], xn_lo[0:1, :], start=False, stop=True).then_inc(s_y5, 1)
            for i in range(1, KH):
                inverse(i)
                if i == 1:
                    pe.wait_ge(s_y5c, 1)
                    for c in range(NB):
                        mm = nc.tensor.matmul(bank(7)[:, c:c + 1], y_t[0:1, 1, c * P:(c + 1) * P], ones[0:1, 0:1],
                                              start=True, stop=True)
                    mm.then_inc(s_y5t, 1)
                back(2 * i - 2)
                back(2 * i - 1)

            pe.wait_ge(s_zlo, 1)
            chunk_in(CK_Y)
            strip(0, 0, z_hi[0], z_lo[0], ks=NB).then_inc(s_y, 1)
            back(KT - 2)
            back(KT - 1)
            strip(0, 2, z_hi[0], z_lo[0], ks=NB, sk=NB).then_inc(s_used, 1)
            for b in range(NBR):
                if b:
                    pe.wait_ge(s_zlo, b + 1)

                def y_pair(i, slot):
                    chunk_in(CK_Y + NB * b + 2 * i + slot)
                    for dd in range(2):
                        pe.wait_ge(s_yev, 8 * b + 4 * i + 2 * slot + dd - 1)
                        mm = strip(slot, 2 * dd, z_hi[b % 2], z_lo[b % 2], ks=NB, sk=NB * dd)
                        if dd == 0:
                            mm.then_inc(s_y, 1)
                    mm.then_inc(s_used, 1)

                if b == 0:
                    y_pair(0, 1)
                    with pe.Fori(1, 2) as i:
                        for slot in range(2):
                            y_pair(i, slot)
                else:
                    with pe.Fori(0, 2) as i:
                        for slot in range(2):
                            y_pair(i, slot)

            def wo(d, slot):
                chunk_in(CK_WO + d)
                strip(slot, 2 * slot, m_hi, m_lo).then_inc(s_used, 1)

            def wo_ones(d, slot, start=False, stop=False):
                pe.wait_ge(s_sq2, d + 1)
                for half in range(2):
                    mm = nc.tensor.matmul(bank(4 + half), ones, sq2[:, slot, half * HALF:(half + 1) * HALF],
                                          start=start, stop=stop)
                mm.then_inc(s_one2, 1)

            pe.wait_ge(s_yev, NBR * KT - 1)
            pe.wait_ge(s_mlo, KT - 2)
            chunk_in(CK_WO)
            strip_parts(0, 0, m_hi, m_lo, KT, KT - 2, s_mlo, KT).then_inc(s_used, 1)
            wo(1, 1)
            wo_ones(0, 0, start=True)
            with pe.Fori(0, 3) as i:
                pe.wait_ge(s_woev, 2 * i + 1)
                wo(2 * i + 2, 0)
                wo_ones(2 * i + 1, 1)
                pe.wait_ge(s_woev, 2 * i + 2)
                wo(2 * i + 3, 1)
                wo_ones(2 * i + 2, 0)
            wo_ones(7, 1, stop=True)

            base, done = CK_FFN, 0
            for g, gn in enumerate(FGROUPS):

                def hidden_first():
                    chunk_in(base)
                    chunk_in(base + 1)
                    for half in range(2):
                        t = slice(half * HALF, (half + 1) * HALF)
                        for k in range(KT):
                            pe.wait_ge(s_h2, KT * half + k + 1)
                            for slot in range(2):
                                mm = mm3(bank(2 * slot + half), slot, k, h2_hi[:, k, t], h2_lo[:, k, t],
                                         k == 0, k == KT - 1)
                                if half == 1 and k == KT - 1:
                                    mm.then_inc(s_used, 1)

                def hidden(i):
                    chunk_in(base + 2 * i)
                    pe.wait_ge(s_sil, done + i)
                    strip(0, 0, h2_hi, h2_lo).then_inc(s_used, 1)
                    chunk_in(base + 2 * i + 1)
                    pe.wait_ge(s_up, done + i)
                    strip(1, 2, h2_hi, h2_lo).then_inc(s_used, 1)

                if g == 0:
                    hidden_first()
                with pe.Fori(int(g == 0), gn) as i:
                    hidden(i)
                done += gn
                base += 2 * gn

                def ffn_out(i, first=False):
                    for j in range(2):
                        chunk_in(base + 2 * i + j)
                        if not (first and g == 0):
                            pe.wait_ge(s_foev, KT * g + 2 * i + j - 1)
                        if first and j == 0:
                            pe.wait_ge(s_glo, done - 1)
                            strip_parts(0, 4, g_hi, g_lo, gn, gn - 1, s_glo, done).then_inc(s_used, 1)
                        else:
                            strip(j, 4 + 2 * j, g_hi, g_lo, ks=gn).then_inc(s_used, 1)

                ffn_out(0, first=True)
                with pe.Fori(1, KT // 2) as i:
                    ffn_out(i)
                base += KT

        @block.scalar
        def _(act):
            own = Steps(act, s_act)

            def func(o, i, f, **kw):
                return nc.scalar.activation(o, i, f, **kw)

            def copy(o, i):
                return func(o, i, ACT.Identity)

            def rsqrt(r, sums, n):
                return func(r, sums, ACT.Abs_reciprocal_sqrt, scale=1.0 / n, bias=vcol("eps"))

            act.dma_start(v_sb[:, :], vec).then_inc(s_const, 16)
            act.dma_start(m_sb[:, :, :], mats).then_inc(s_const, 16)
            act.dma_start(alt_f[:, :], checker).then_inc(s_const, 16)
            act.wait_ge(s_const, 48)
            func(csg[:, :], vcol("c", 0, 2 * KT), ACT.Sigmoid).then_inc(s_csg, 1)

            def x_load(k):
                act.dma_start(hx[k % 3], xc[k]).then_inc(s_hx[k % 3], 16)

            def taps_high(t):
                act.wait_ge(s_eo, t + 1)
                copy(both(e_hi, t), ab[:, t % 2, 0, :, :])
                copy(both(o_hi, t), ab[:, t % 2, 1, :, :]).then_inc(s_eohi, 1)

            def row_out(g):
                act.wait_ge(s_mrow, g + 1)
                if g >= 2:
                    act.wait_ge(s_mcol, g - 1)
                copy(mrow[:, g % 2, :], bank(2 + g % 2)[0:2, :]).then_inc(s_mrowc, 1)

            def sin(n):
                act.wait_ge(s_fred, n + 1)
                func(f_h[:, :], f_a[:, :], ACT.Sin).then_inc(s_fsin, 1)

            for k in range(KT):
                act.wait_ge(s_xs[k % 2], 16 * (k // 2 + 1))
                func(xs[:, k % 2, :], xs[:, k % 2, :], ACT.Square).then_inc(s_sq, 1)
                if k in (1, 3, 5):
                    sin(k // 2)
                if k in (2, 4, 6):
                    row_out(k // 2 - 1)
                if k >= 6:
                    taps_high(k - 6)
            row_out(KT // 2 - 1)
            act.wait_ge(s_ss, KT)
            act.wait_ge(s_mused, 2 * KT)
            for k in range(3):
                x_load(k)
            taps_high(2)
            act.wait_ge(s_nv, 1)
            rsqrt(rstd[:, :], bank(1, width=TC), D).then_inc(s_r0, 1)
            taps_high(3)
            act.wait_ge(s_eo, KH + 1)
            copy(xk_hi[0:1, :], eo[0:1, 0, 0, :])
            copy(xk_hi[64:65, :], eo[64:65, 0, 1, :]).then_inc(s_eohi, 1)

            def spectrum_out(q):
                act.wait_ge(s_used, CK_KDFT + q + 1)
                if q:
                    act.wait_ge(s_kst, 16 * q)
                copy(ksp[:, :, :], bank(2 * (q % 2), 2)).then_inc(s_ev, 1)
                act.wait_ge(s_ev, q + 1)
                if q == 0:
                    act.wait_ge(s_ny, 1)
                    own.done(copy(ksp[0:1, 1, :], bank(4)[0:1, :]))
                act.dma_start(kspec[q], ksp[:, :, :]).then_inc(s_kst, 16)

            for k in range(KT):
                act.wait_ge(s_ht, k + 1)
                func(h_hi[:, k, :], hx[k % 3][:, 0:T], ACT.Identity, bias=mod[:, k, 0:1])
                func(c_hi[:, k, :], hx[k % 3][:, T:TC], ACT.Identity, bias=mod[:, k, 1:2]).then_inc(s_hh, 1)
                if 1 <= k < KT - 2:
                    act.wait_ge(s_hlo, k)
                    x_load(k + 2)
                if k in (3, 5):
                    spectrum_out(k // 2 - 1)
            for q in range(2, KT):
                spectrum_out(q)

            def strip_out(n, dst, f=ACT.Identity):
                act.wait_ge(s_used, CK_IN + n + 1)
                func(dst, bank(2 * (n % 2), 2), f).then_inc(s_ev, 1)

            for c in range(NB):
                if c >= 2:
                    act.wait_ge(s_cfm, c - 1)
                strip_out(2 * c, st[:, 2 * c % 4, 1:T + 1])
                strip_out(2 * c + 1, st[:, (2 * c + 1) % 4, 1:T + 1], ACT.Sigmoid)
            for g in range(2 * NB):
                if g == 0:
                    act.wait_ge(s_cfm, NB)
                if g >= 2:
                    act.wait_ge(s_grpout, g - 1)
                for j in range(3):
                    strip_out(S_HY + 3 * g + j, st[:, 3 * (g % 2) + j, 1:T + 1])
                act.wait_ge(s_grpout, g + 1)
                if g < NB:
                    act.dma_start(x0_d[g], cvo[:, 0, :]).then_inc(s_cvst, 16)
                    act.dma_start(u_d[g], cvo[:, 1, :]).then_inc(s_cvst, 16)
                else:
                    act.dma_start(z_d[Z_A, g - NB], cvo[:, 0, :]).then_inc(s_cvst, 16)
            act.wait_ge(s_kst, 16 * KT)
            act.wait_ge(s_cvst, 16 * 3 * NB)
            for t in range(N_QKV):
                late = t >= N_QKV - 2
                if late:
                    act.wait_ge(s_qn, 2 * NB)
                elif t >= 6:
                    act.wait_ge(s_nl, t - 5)
                strip_out(S_QKV + t, v_late[:, t % 2, :] if late else st[:, t % 6, 0:T])
                if t >= NB:
                    u = (t - NB) % 4
                    act.wait_ge(s_cacc, t - NB + 1)
                    if t >= 2 * NB:
                        act.wait_ge(s_nl, t - NB + 1)
                    copy(cst[:, u, :], bank(4 + t % 2, width=C)).then_inc(s_cev, 1)
                if 1 <= t <= 2 * NB:
                    act.wait_ge(s_qfree, t)
                    if t >= 2:
                        act.wait_ge(s_qn, t - 1)
                    r1 = rsqrt(q_r[:, 0:T], bank(6, 2), HD)
                    if t - 1 >= NB:
                        r1 = rsqrt(q_r[:, T:TC], bank(4 + (t - 1) % 2)[:, C:2 * C], HD)
                    r1.then_inc(s_qr, 1)
                o = t - 2
                if 0 <= o < 2 * NB:
                    act.wait_ge(s_qn, o + 1)
                    if o >= 2:
                        act.wait_ge(s_nst[o % 2], 32 * (o // 2))
                    ins = copy(n_hi[:, o % 2, 0:T], st[:, o % 6, 0:T])
                    if o >= NB:
                        ins = copy(n_hi[:, o % 2, T:TC], cst[:, (o - NB) % 4, :])
                    ins.then_inc(s_nh, 1)
                o = t - 3
                if 0 <= o < 2 * NB:
                    act.wait_ge(s_nl, o + 1)
                    for part, n_p in enumerate((n_hi, n_lo)):
                        if o < NB:
                            act.dma_start(q_d[part][o], n_p[:, o % 2, 0:T].bitcast(F32)).then_inc(s_nst[o % 2], 16)
                        else:
                            act.dma_start(k_d[part][o - NB], n_p[:, o % 2, :].bitcast(F32)).then_inc(s_nst[o % 2], 16)
                if t >= 2 * NB:
                    act.wait_ge(s_ev, KT + S_QKV + t + 1)
                    act.wait_ge(s_cev, t - NB + 1)
                    done = s_vlate if late else s_vst
                    act.dma_start(v_d[t - 2 * NB], v_late[:, t % 2, :] if late else st[:, t % 6, 0:T]).then_inc(done, 16)
                    act.dma_start(vc_d[t - 2 * NB], cst[:, (t - NB) % 4, :]).then_inc(done, 16)
            def gate_out(hp, it):
                m, half = 8 * hp + it // 2, it % 2
                slot = it // 2 % 2
                if half:
                    act.wait_ge(s_used, CK_IN + S_G + m + 1)
                else:
                    act.wait_ge(s_gh, m + 1)
                    if it >= 4:
                        act.wait_ge(s_gst[slot], 64 * hp + 16 * (it // 4))
                func(gst[:, slot, half * HALF:(half + 1) * HALF], bank(half), ACT.Sigmoid).then_inc(s_ev, 1)
                if half:
                    act.wait_ge(s_ev, KT + S_G + 16 * hp + it + 1)
                    act.dma_start(row(gate_d, m), gst[:, slot, :]).then_inc(s_gst[slot], 16)

            def exps(hp, it):
                act.wait_ge(s_anm, 16 * hp + it + 1)
                s = it % 2
                func(a_s[:, s, :], a_s[:, s, :], ACT.Exp, bias=st_nm[:, s:s + 1],
                     accum_out=st_l[:, s:s + 1]).then_inc(s_aexp, 1)

            def evacuate(hp, it):
                act.wait_ge(s_at, 16 * hp + it + 1)
                if it >= 2:
                    act.wait_ge(s_apv, 16 * hp + it - 1)
                copy(a_pt[:, it % 2, 0:HALF], bank(4)).then_inc(s_aeva, 1)

            with act.Fori(0, NB) as hp:
                for it in range(16):
                    if it < 15:
                        gate_out(hp, it)
                    if it == 1:
                        act.wait_ge(s_avt, hp + 1)
                        copy(a_vt[:, :, :], bank(4, width=10 * P)).then_inc(s_avev, 1)
                    exps(hp, it)
                    if it:
                        evacuate(hp, it - 1)
                evacuate(hp, 15)
                gate_out(hp, 15)
                act.wait_ge(s_azt, hp + 1)
                copy(a_o[:, :, :], bank(4, 2)).then_inc(s_azev, 1)
                act.wait_ge(s_azev, hp + 1)
                act.dma_start(row(z_d[Z_NA], hp), a_o.rearrange("p r c -> p (r c)")).then_inc(s_azst, 16)
                for j in range(2):
                    act.wait_ge(s_gst[j], 64 * hp + 64)

            for c in range(NB):
                act.wait_ge(s_lx, c + 1)
                func(lsq[:, c, :], cfo[:, c, :], ACT.Square).then_inc(s_lsq, 1)
            for t in range(KT):
                act.wait_ge(s_ut, t + 1)
                copy(u_hi[:, t, :], bank(t % 4)).then_inc(s_uhi, 1)
            act.wait_ge(s_ut, KT + 1)
            act.wait_ge(s_azst, 16 * (NB + 1))
            copy(xu_hi[0:1, :], bank(KT % 4)[0:1, :]).then_inc(s_uhi, 1)
            act.wait_ge(s_lf, 1)
            rsqrt(l_r[:, :], bank(6, 2), DB).then_inc(s_lr, 1)
            def k_load(q):
                act.dma_start(k_sb[:, q % 2, :, :], kspec[q]).then_inc(s_k[q % 2], 16)

            act.wait_ge(s_l2, NB)
            k_load(0)
            k_load(1)
            for q in range(KT):
                act.wait_ge(s_pr, q + 1)
                copy(pr_hi[:, q, :], pw[:, q % 2, 0, :])
                copy(ps_hi[:, q, :], pw[:, q % 2, 2, :]).then_inc(s_prhi, 1)
                if q + 2 < KT:
                    act.wait_ge(s_udev, q + 1)
                    k_load(q + 2)

            def z_load(b):
                z = z_d[b].rearrange("c p t -> p c t")
                if b == Z_HY:
                    for t in (slice(0, HALF), slice(HALF + 1, T)):
                        act.dma_start(zraw[:, :, t], z[:, :, t]).then_inc(s_zld, 16)
                else:
                    act.dma_start(zraw[:, :, :], z).then_inc(s_zld, 16)

            def z_high(b):
                if b == Z_HY:
                    act.wait_ge(s_y5z, 1)
                    own.done(copy(zraw[:, :, HALF:HALF + 1], y5w.rearrange("p (c o) -> p c o", o=1)))
                act.wait_ge(s_zld, 16 * (b + 1 + (b == Z_HY)))
                copy(z_hi[b % 2][:, :, :], zraw[:, :, :]).then_inc(s_zhi, 1)

            def g_load(n):
                b, d = divmod(n, KT)
                act.dma_start(gt[:, n % 3, :], gate_d[GATE_OF[b] * KT + d]).then_inc(s_gld[n % 3], 16)

            act.wait_ge(s_prlo, KT)
            act.dma_start(x0_f[:, :, :], x0_d.rearrange("c p t -> p c t")).then_inc(s_x0, 16)
            for n in range(3):
                g_load(n)
            for c in range(NB):
                act.wait_ge(s_ly, c + 1)
                func(cfo[:, c, :], cfo[:, c, :], ACT.Silu, scale=vcol("lng", c),
                     bias=vcol("lnb", c)).then_inc(s_lz, 1)
                act.wait_ge(s_lz, c + 1)
                act.dma_start(z_d[Z_CF, c], cfo[:, c, :]).then_inc(s_zst, 16)

            def y_store(n):
                act.wait_ge(s_idz, n + 1)
                t0, width = y_range(n)
                act.dma_start(z_d[Z_HY].rearrange("c p t -> p c t")[:, :, t0:t0 + width],
                              y_w[:, n % 2, :, 0:width]).then_inc(s_idst[n % 2], 16)

            for i in range(KH):
                act.wait_ge(s_used, CK_IDFT + 2 * i + 2)
                if i:
                    act.wait_ge(s_yt, 2 * i)
                func(y_b[:, :], bank(2 * (i % 2) + 1), ACT.Identity, scale=1.0 / T).then_inc(s_idb, 1)
                if i == 0:
                    act.wait_ge(s_y5, 1)
                    func(y_t[0:1, 1, :], bank(6)[0:1, :], ACT.Identity, scale=1.0 / T).then_inc(s_y5c, 1)
                    act.wait_ge(s_zst, 16 * NB)
                    z_load(0)
                if i == 1:
                    z_high(0)
                if i:
                    y_store(2 * i - 2)
                    y_store(2 * i - 1)
            y_store(KT - 2)
            y_store(KT - 1)

            for n in range(NBR * KT):
                b, d = divmod(n, KT)
                if d == 0 and b + 1 < NBR:
                    act.wait_ge(s_zlo, b + 1)
                    if b + 1 == Z_HY:
                        act.wait_ge(s_idst[0], 16 * KT // 2)
                        act.wait_ge(s_idst[1], 16 * KT // 2)
                    z_load(b + 1)
                    act.wait_ge(s_used, CK_Y + NB * b)
                    z_high(b + 1)
                act.wait_ge(s_yev, n + 1)
                if n + 3 < NBR * KT:
                    g_load(n + 3)
                if b == NBR - 1:
                    act.wait_ge(s_mg, d + 1)
                    copy(m_hi[:, d, :], mrg[:, d, :]).then_inc(s_mhi, 1)

            act.wait_ge(s_used, CK_WO)
            act.dma_start(x1[:, :, :], xc.rearrange("k p t -> p k t")[:, :, 0:T]).then_inc(s_x1, 16)
            for d in range(KT):
                act.wait_ge(s_woev, d + 1)
                if d >= 2:
                    act.wait_ge(s_one2, d - 1)
                func(sq2[:, d % 2, :], x1[:, d, :], ACT.Square).then_inc(s_sq2, 1)
            for half in range(2):
                t = slice(half * HALF, (half + 1) * HALF)
                act.wait_ge(s_v2, half + 1)
                rsqrt(r2[:, t], bank(4 + half), D).then_inc(s_r2, 1)
            for n in range(2 * KT):
                half, k = divmod(n, KT)
                t = slice(half * HALF, (half + 1) * HALF)
                act.wait_ge(s_t2, n + 1)
                func(h2_hi[:, k, t], ht[:, n % 4, :], ACT.Identity, bias=mod[:, 3 * KT + k, 0:1]).then_inc(s_h2h, 1)

            m, base = 0, CK_FFN
            for g, gn in enumerate(FGROUPS):
                for i in range(gn):
                    act.wait_ge(s_used, base + 2 * i + 1)
                    if m:
                        act.wait_ge(s_up, m)
                    func(sg[:, :], bank(0, 2), ACT.Silu).then_inc(s_sil, 1)
                    act.wait_ge(s_up, m + 1)
                    copy(g_hi[:, i, :], gm[:, :]).then_inc(s_ghi, 1)
                    m += 1
                base += 2 * gn + KT

        @block.vector
        def _(dve):
            own = Steps(dve, s_dve)
            tt, ts, stt = nc.vector.tensor_tensor, nc.vector.tensor_scalar, nc.vector.scalar_tensor_tensor

            def low(o, x, hi):
                return tt(o, x, hi.bitcast(F32), ALU.subtract)

            def low_shift(o, x, shift, hi):
                return stt(out=o, in0=x, scalar=shift, in1=hi.bitcast(F32), op0=ALU.add, op1=ALU.subtract)

            def refine(r, v, t):
                own.done(stt(out=t, in0=r, scalar=-0.5, in1=r, op0=ALU.mult, op1=ALU.mult))
                own.done(tt(t, t, v, ALU.mult))
                own.done(stt(out=r, in0=t, scalar=1.5, in1=r, op0=ALU.add, op1=ALU.mult))

            def mean_eps(v, sums, n):
                return ts(v, sums, 1.0 / n, EPS, ALU.mult, ALU.add)

            dve.wait_ge(s_filt, 16)
            w4 = f_sb[:, T:2 * T]
            own.done(tt(f_w4[:, 0, :], w4[:, 0:DB], w4[:, DB:2 * DB], ALU.add))
            tt(f_w4[:, 1, :], w4[:, 0:DB], w4[:, DB:2 * DB], ALU.subtract).then_inc(s_w4, 1)
            dve.wait_ge(s_const, 48)
            nc.vector.tensor_copy(altr[:, :], alt_f[:, :]).then_inc(s_alt, 1)
            own.done(ts(qg8[:, :], vcol("qg"), HD ** -0.5, None, ALU.mult))
            dve.wait_ge(s_csg, 1)
            tt(cs[:, :], csg[:, :], vcol("c", 0, 2 * KT), ALU.mult).then_inc(s_cs, 1)

            magic = float(1.5 * 2 ** 23)
            p1 = 6.28125
            p2 = float(np.float32(np.round((2 * np.pi - p1) * 2 ** 21) / 2 ** 21))
            p3 = float(np.float32(2 * np.pi - p1 - p2))
            for n in range(3):
                dve.wait_ge(s_fmm, n + 1)
                own.done(ts(f_a[:, :], bank(4, 2)[0:64, :], vcol("fb", n)[0:64, :], vcol("freq")[0:64, :],
                            ALU.add, ALU.mult))
                own.done(ts(f_k[:, :], f_a[:, :], float(1 / (2 * np.pi)), magic, ALU.mult, ALU.add))
                own.done(ts(f_k[:, :], f_k[:, :], magic, None, ALU.subtract))
                for part in (p1, p2, p3):
                    own.done(stt(out=f_a[:, :], in0=f_k[:, :], scalar=-part, in1=f_a[:, :], op0=ALU.mult, op1=ALU.add))
                ts(f_a[:, :], f_a[:, :], 3.1415925, -3.1415925, ALU.min, ALU.max).then_inc(s_fred, 1)

            def mod_out(a, b):
                for s in range(2):
                    ins = tt(mod[:, a:b, s], ps[:, 6 * HALF + 2 * a + s:6 * HALF + 2 * b:2], vcol("bmod", a, b - a), ALU.add)
                return ins

            def norm_sums():
                dve.wait_ge(s_mcol, KT // 2)
                mod_out(0, 2 * KT).then_inc(s_mod1, 1)
                dve.wait_ge(s_mod1, 1)
                for s in range(2):
                    own.done(stt(out=aff[:, :, s], in0=mod[:, KT:2 * KT, s], scalar=1.0, in1=vcol("g1", 0, KT),
                                 op0=ALU.add, op1=ALU.mult))
                dve.wait_ge(s_sum, 1)
                mean_eps(nv[:, :], bank(1, width=TC), D).then_inc(s_nv, 1)
                dve.wait_ge(s_nv, 1)

            dve.wait_ge(s_win, 16)

            def eo_low(t):
                dve.wait_ge(s_eohi, t + 1)
                low(both(e_lo, t), ab[:, t % 2, 0, :, :], both(e_hi, t))
                low(both(o_lo, t), ab[:, t % 2, 1, :, :], both(o_hi, t)).then_inc(s_eolo, 1)
                dve.wait_ge(s_eolo, t + 1)

            for j, t in enumerate((0, 4, 1, 5, 2, 6, 3, 7)):
                if t == 3:
                    norm_sums()
                for part in range(2):
                    dve.wait_ge(s_eomm, 2 * j + part + 1)
                    tt(eo[:, j % 2, part, :], bank(TAP_BANKS[2 * (j % 2) + part]), win_sb[:, t, :], ALU.mult).then_inc(s_eoev, 1)
                dve.wait_ge(s_eoev, 2 * j + 2)
                if t == 0:
                    e0, o0 = eo[0:1, 0, 0, :], eo[0:1, 0, 1, :]
                    own.done(tt(e0, e0, o0, ALU.add))
                    own.done(ts(e0, e0, 0.5, None, ALU.mult))
                if j % 2:
                    tt(ab[:, t % 2, :, 0, :], eo[:, 0, :, :], eo[:, 1, :, :], ALU.add)
                    tt(ab[:, t % 2, :, 1, :], eo[:, 0, :, :], eo[:, 1, :, :], ALU.subtract).then_inc(s_eo, 1)
                    dve.wait_ge(s_eo, j // 2 + 1)
                    if j > 1:
                        eo_low(j // 2 - 1)
            for part in range(2):
                r = slice(64 * part, 64 * part + 1)
                dve.wait_ge(s_eomm, 2 * KT + part + 1)
                ins = tt(eo[r, 0, part, :], bank(4 + part)[r, :], win_sb[r, KT, :], ALU.mult)
                ins.then_inc(s_eoev, 1)
            dve.wait_ge(s_eoev, 2 * KT + 2)
            nc.vector.tensor_copy(st_m[:, 0:1], vcol("eps")).then_inc(s_eo, 1)
            eo_low(KH - 1)
            dve.wait_ge(s_eohi, KH + 1)
            low(xk_lo[0:1, :], eo[0:1, 0, 0, :], xk_hi[0:1, :])
            low(xk_lo[64:65, :], eo[64:65, 0, 1, :], xk_hi[64:65, :]).then_inc(s_eolo, 1)
            dve.wait_ge(s_eolo, KH + 1)

            dve.wait_ge(s_r0, 1)
            refine(rstd[:, :], nv[:, :], nt[:, :])

            def h_low(k):
                dve.wait_ge(s_hh, k + 1)
                if k == KT - 1:
                    dve.wait_ge(s_used, CK_IN)
                low_shift(h_lo[:, k, :], hx[k % 3][:, 0:T], mod[:, k, 0:1], h_hi[:, k, :])
                low_shift(c_lo[:, k, :], hx[k % 3][:, T:TC], mod[:, k, 1:2], c_hi[:, k, :]).then_inc(s_hlo, 1)
                dve.wait_ge(s_hlo, k + 1)

            for k in range(KT):
                dve.wait_ge(s_hx[k % 3], 16 * (k // 3 + 1))
                for s, t in ((0, slice(0, T)), (1, slice(T, TC))):
                    ins = stt(out=hx[k % 3][:, t], in0=hx[k % 3][:, t], scalar=aff[:, k, s:s + 1], in1=rstd[:, t],
                              op0=ALU.mult, op1=ALU.mult)
                ins.then_inc(s_ht, 1)
                if k:
                    h_low(k - 1)
            h_low(KT - 1)

            dve.wait_ge(s_used, CK_IN)
            edge = CFK // 2
            nc.vector.memset(cfm[:, :, 0:edge], 0.0)
            nc.vector.memset(cfm[:, :, T + edge:T + 2 * edge], 0.0)
            nc.vector.memset(st[:, :, 0:1], 0.0)
            own.done(nc.vector.memset(st[:, :, T + 1:T + 2], 0.0))

            def mod_part(n):
                dve.wait_ge(s_mraw[n % 2], 16 * (KT + n // 2 + 1))
                wv = mraw[:, n % 2, :].rearrange("p (k f) -> p k f", k=KT)
                by_k = cs.rearrange("p (k s) -> p k s", s=2)[:, :, 0:1].broadcast_to([P, KT, P])
                tt(mprod.rearrange("p (k f) -> p k f", k=KT), wv, by_k, ALU.mult).then_inc(s_mfree, 1)
                dve.wait_ge(s_mfree, n + 1)
                if n >= 2:
                    dve.wait_ge(s_mused, 16 + n - 1)
                nc.vector.tensor_reduce(macc[:, n % 2, :], mprod.rearrange("p (k f) -> p f k", k=KT),
                                        mybir.AxisListType.X, ALU.add).then_inc(s_macc, 1)
                dve.wait_ge(s_macc, n + 1)

            dve.wait_ge(s_kst, 16 * KT)
            for c in range(NB):
                mod_part(2 * c)
                mod_part(2 * c + 1)
                dve.wait_ge(s_ev, KT + 2 * c + 2)
                tt(cfm[:, c, edge:edge + T], st[:, 2 * c % 4, 1:T + 1], st[:, (2 * c + 1) % 4, 1:T + 1],
                   ALU.mult).then_inc(s_cfm, 1)

            def conv3(o, slot, name, n, first, ready):
                dve.wait_ge(s_ev, ready)
                own.done(ts(o, st[:, slot, 0:T], vcol(name, first), None, ALU.mult))
                own.done(stt(out=o, in0=st[:, slot, 1:T + 1], scalar=vcol(name, n + first), in1=o, op0=ALU.mult, op1=ALU.add))
                own.done(stt(out=o, in0=st[:, slot, 2:T + 2], scalar=vcol(name, 2 * n + first), in1=o, op0=ALU.mult, op1=ALU.add))

            for g in range(2 * NB):
                for j in range(3):
                    mod_part(N_CF + 3 * g + j)
                s0 = 3 * (g % 2)
                ready = KT + S_HY + 3 * g + 1
                if g:
                    dve.wait_ge(s_cvst, 16 * (2 * g if g <= NB else NB + g))
                if g < NB:
                    for j in range(3):
                        conv3(cvo[:, j, :], s0 + j, "chy", 3 * NB, j * NB + g, ready + j)
                    tt(cvo[:, 1, :], cvo[:, 1, :], cvo[:, 2, :], ALU.mult).then_inc(s_grpout, 1)
                else:
                    dve.wait_ge(s_ev, ready + 2)
                    own.done(tt(st[:, s0 + 2, 1:T + 1], st[:, s0 + 2, 1:T + 1], st[:, s0, 1:T + 1], ALU.mult))
                    conv3(cvo[:, 0, :], s0 + 2, "ca", NB, g - NB, ready + 2)
                    tt(cvo[:, 0, :], cvo[:, 0, :], st[:, s0 + 1, 1:T + 1], ALU.mult).then_inc(s_grpout, 1)
            dve.wait_ge(s_mused, 6 * KT)
            mod_out(2 * KT, 6 * KT).then_inc(s_modev, 1)

            def norm_low(t):
                dve.wait_ge(s_nh, t + 1)
                ins = low(n_lo[:, t % 2, 0:T], st[:, t % 6, 0:T], n_hi[:, t % 2, 0:T])
                if t >= NB:
                    ins = low(n_lo[:, t % 2, T:TC], cst[:, (t - NB) % 4, :], n_hi[:, t % 2, T:TC])
                ins.then_inc(s_nl, 1)

            for t in range(2 * NB):
                x = st[:, t % 6, 0:T]
                kc = cst[:, (t - NB) % 4, :]
                gain = qg8[:, :] if t < NB else vcol("kg")
                n = T if t < NB else TC
                dve.wait_ge(s_ev, KT + S_QKV + t + 1)
                ins = tt(q_t[:, 0:T], x, x, ALU.mult)
                if t >= NB:
                    dve.wait_ge(s_cev, t - NB + 1)
                    ins = tt(q_t[:, T:TC], kc, kc, ALU.mult)
                ins.then_inc(s_qsq, 1)
                if t >= 2:
                    norm_low(t - 2)
                dve.wait_ge(s_qones, t + 1)
                ins = mean_eps(q_v[:, 0:T], bank(6, 2), HD)
                if t >= NB:
                    ins = mean_eps(q_v[:, T:TC], bank(4 + t % 2)[:, C:2 * C], HD)
                ins.then_inc(s_qfree, 1)
                dve.wait_ge(s_qfree, t + 1)
                dve.wait_ge(s_qr, t + 1)
                refine(q_r[:, 0:n], q_v[:, 0:n], q_t[:, 0:n])
                ins = stt(out=x, in0=x, scalar=gain, in1=q_r[:, 0:T], op0=ALU.mult, op1=ALU.mult)
                if t >= NB:
                    ins = stt(out=kc, in0=kc, scalar=gain, in1=q_r[:, T:TC], op0=ALU.mult, op1=ALU.mult)
                ins.then_inc(s_qn, 1)
                dve.wait_ge(s_qn, t + 1)

            norm_low(2 * NB - 2)
            norm_low(2 * NB - 1)

            dve.wait_ge(s_azst, 16)
            dve.wait_ge(s_vlate, 64)
            own.done(nc.vector.memset(a_b[:, 0:C], 0.0))

            def tap(hp, j):
                o = cfo[:, bass.ds(hp, 1), :]
                x = cfm[:, bass.ds(hp, 1), j:j + T]
                wj = v_sb[:, bass.ds(VEC["cd"] + NB * j + hp, 1)]
                if j == 0:
                    own.mark(ts(o, x, wj, v_sb[:, bass.ds(VEC["cdb"] + hp, 1)], ALU.mult, ALU.add))
                elif j < CFK - 1:
                    own.mark(stt(out=o, in0=x, scalar=wj, in1=o, op0=ALU.mult, op1=ALU.add))
                else:
                    stt(out=o, in0=x, scalar=wj, in1=o, op0=ALU.mult, op1=ALU.add).then_inc(s_conv, 1)

            def heads_out(hp, it):
                e, rp = divmod(it, 8)
                s = it % 2
                dve.wait_ge(s_apv, 16 * hp + it + 1)
                ts(a_o[:, rp, e * HD:(e + 1) * HD], bank(6 + s)[:, 0:HD], st_r[:, s:s + 1], None,
                   ALU.mult).then_inc(s_ao, 1)

            def weights_out(hp, it):
                s = it % 2
                dve.wait_ge(s_at, 16 * hp + it + 1)
                if it >= 2:
                    dve.wait_ge(s_apv, 16 * hp + it - 1)
                nc.vector.tensor_copy(a_pt[:, s, HALF:KEYS], bank(5, width=KEYS - HALF)).then_inc(s_aevd, 1)
                dve.wait_ge(s_aexp, 16 * hp + it + 1)
                own.mark(nc.vector.reciprocal(st_r[:, s:s + 1], st_l[:, s:s + 1]))

            with own.loop(NB, 30 + 16 + 10) as hp:
                for it in range(16):
                    e, rp = divmod(it, 8)
                    s = it % 2
                    if rp == 0:
                        dve.wait_ge(s_hld[e], 96 * (hp + 1))
                    if rp in MASK_OF:
                        x = (window_start(rp) - 2 * rp + WIN_H) * GRID
                        own.mark(tt(a_b[:, C:KEYS], a_g[e][:, x:x + LOC], a_m[:, MASK_OF[rp], :], ALU.add))
                    own.wait()
                    dve.wait_ge(s_as, 16 * hp + it + 1)
                    if it >= 2:
                        dve.wait_ge(s_at, 16 * hp + it - 1)
                    tap(hp, 2 * it)
                    nc.vector.tensor_tensor_reduce(a_s[:, s, :], bank(2, width=KEYS), a_b[:, :], 1.0, NEG, ALU.add,
                                                   ALU.max, st_m[:, s:s + 1]).then_inc(s_attr, 1)
                    dve.wait_ge(s_attr, 16 * hp + it + 1)
                    ts(st_nm[:, s:s + 1], st_m[:, s:s + 1], -1.0, None, ALU.mult).then_inc(s_anm, 1)
                    if it == 2:
                        dve.wait_ge(s_azst, 16 * (hp + 1))
                    if it >= 2:
                        heads_out(hp, it - 2)
                    if it:
                        weights_out(hp, it - 1)
                    own.wait()
                    if 2 * it + 1 < CFK:
                        tap(hp, 2 * it + 1)
                heads_out(hp, 14)
                weights_out(hp, 15)
                own.wait()
                heads_out(hp, 15)

            dve.wait_ge(s_used, CK_UDFT)
            for c in range(NB):
                dve.wait_ge(s_uld[c], 16)
                back_u = u_f[:, c, T - 1:HALF:-1]
                nc.vector.tensor_copy(ub[:, c, 0:T:HALF], u_f[:, c, 0:1].broadcast_to([P, 2]))
                tt(ub[:, c, 1:HALF], u_f[:, c, 1:HALF], back_u, ALU.add)
                tt(ub[:, c, HALF + 1:T], u_f[:, c, 1:HALF], back_u, ALU.subtract).then_inc(s_fold, 1)

            dve.wait_ge(s_l1, 1)
            for c in range(NB):
                stt(out=cfo[:, c, :], in0=bank(4, 2), scalar=-1.0 / DB, in1=cfo[:, c, :], op0=ALU.mult,
                    op1=ALU.add).then_inc(s_lx, 1)
            for t in range(KT):
                dve.wait_ge(s_uhi, t + 1)
                low(u_lo[:, t, :], bank(t % 4), u_hi[:, t, :]).then_inc(s_ulo, 1)
            dve.wait_ge(s_uhi, KT + 1)
            low(xu_lo[0:1, :], bank(KT % 4)[0:1, :], xu_hi[0:1, :]).then_inc(s_ulo, 1)
            dve.wait_ge(s_l2, NB)
            mean_eps(l_v[:, :], bank(6, 2), DB).then_inc(s_lf, 1)
            dve.wait_ge(s_lf, 1)
            dve.wait_ge(s_lr, 1)
            dve.wait_ge(s_lx, NB)
            refine(l_r[:, :], l_v[:, :], l_t[:, :])
            def pr_low(q):
                dve.wait_ge(s_prhi, q + 1)
                low(pr_lo[:, q, :], pw[:, q % 2, 0, :], pr_hi[:, q, :])
                low(ps_lo[:, q, :], pw[:, q % 2, 2, :], ps_hi[:, q, :]).then_inc(s_prlo, 1)
                dve.wait_ge(s_prlo, q + 1)

            for q in range(KT):
                s = q % 2
                uc, us = bank(2 * s), bank(2 * s + 1)
                dve.wait_ge(s_k[s], 16 * (q // 2 + 1))
                kc, ks = k_sb[:, s, 0, :], k_sb[:, s, 1, :]
                dve.wait_ge(s_used, CK_UDFT + q + 1)
                if q == 0:
                    xn = pw[0:1, s, 1, :]
                    dve.wait_ge(s_un, 1)
                    own.done(tt(xn, bank(4)[0:1, :], ks[0:1, :], ALU.mult))
                    own.done(ts(xn, xn, 0.5, None, ALU.mult))
                    own.done(nc.vector.tensor_copy(xn_hi[0:1, :], xn))
                    low(xn_lo[0:1, :], xn, xn_hi[0:1, :]).then_inc(s_xn, 1)
                    dve.wait_ge(s_xn, 1)
                tt(pw[:, s, 0, :], uc, kc, ALU.mult)
                tt(pw[:, s, 2, :], uc, ks, ALU.mult)
                tt(pw[:, s, 1, :], us, ks, ALU.mult)
                tt(pw[:, s, 3, :], us, kc, ALU.mult).then_inc(s_udev, 1)
                dve.wait_ge(s_udev, q + 1)
                tt(pw[:, s, 0, :], pw[:, s, 0, :], pw[:, s, 1, :], ALU.subtract)
                ins = tt(pw[:, s, 2, :], pw[:, s, 2, :], pw[:, s, 3, :], ALU.add)
                if q == 0:
                    own.done(ins)
                    ins = ts(pw[0:1, s, 0, :], pw[0:1, s, 0, :], 0.5, None, ALU.mult)
                ins.then_inc(s_pr, 1)
                dve.wait_ge(s_pr, q + 1)
                if q:
                    pr_low(q - 1)
            pr_low(KT - 1)

            for c in range(NB):
                tt(cfo[:, c, :], cfo[:, c, :], l_r[:, :], ALU.mult).then_inc(s_ly, 1)

            def z_low(b):
                dve.wait_ge(s_zhi, b + 1)
                low(z_lo[b % 2][:, :, :], zraw[:, :, :], z_hi[b % 2][:, :, :]).then_inc(s_zlo, 1)

            dve.wait_ge(s_x0, 16)
            def y_middle():
                dve.wait_ge(s_y5t, 1)
                mid = slice(HALF, HALF + 1)
                own.done(tt(y5w[:, :], u_f[:, :, mid].rearrange("p c o -> p (c o)"), vcol("skip", 0, NB), ALU.mult))
                own.done(tt(y5w[:, :], y5w[:, :], bank(7, width=NB), ALU.add))
                tt(y5w[:, :], y5w[:, :], x0_f[:, :, mid].rearrange("p c o -> p (c o)"), ALU.mult).then_inc(s_y5z, 1)

            def y_out(n):
                s = n % 2
                t0, width = y_range(n)
                dve.wait_ge(s_idt, n + 1)
                if n >= 2:
                    dve.wait_ge(s_idst[s], 16 * (n // 2))
                for c in range(NB):
                    ins = stt(out=y_w[:, s, c, 0:width], in0=u_f[:, c, t0:t0 + width], scalar=vcol("skip", c),
                              in1=bank(4 + s)[:, c * P:c * P + width], op0=ALU.mult, op1=ALU.add)
                own.done(ins)
                tt(y_w[:, s, :, 0:width], y_w[:, s, :, 0:width], x0_f[:, :, t0:t0 + width],
                   ALU.mult).then_inc(s_idz, 1)

            for i in range(KH):
                first = bank(2 * (i % 2))
                dve.wait_ge(s_idb, i + 1)
                for part, op in enumerate((ALU.add, ALU.subtract)):
                    n = 2 * i + part
                    if i:
                        dve.wait_ge(s_idt, n - 1)
                    elif part:
                        y_middle()
                    stt(out=y_t[:, part, :], in0=first, scalar=1.0 / T, in1=y_b[:, :], op0=ALU.mult,
                        op1=op).then_inc(s_yt, 1)
                if i == 1:
                    z_low(0)
                y_out(2 * i)
                y_out(2 * i + 1)

            for n in range(NBR * KT):
                b, d = divmod(n, KT)
                b0 = 2 * (d % 2)
                dve.wait_ge(s_gld[n % 3], 16 * (n // 3 + 1))
                if d % 2 == 0:
                    dve.wait_ge(s_y, n // 2 + 1)
                else:
                    dve.wait_ge(s_used, CK_Y + n // 2 + 1)
                if b == 0:
                    tt(mrg[:, d, :], bank(b0, 2), gt[:, n % 3, :], ALU.mult).then_inc(s_yev, 1)
                    dve.wait_ge(s_yev, n + 1)
                else:
                    tt(yt[:, :], bank(b0, 2), gt[:, n % 3, :], ALU.mult).then_inc(s_yev, 1)
                    dve.wait_ge(s_yev, n + 1)
                    own.done(tt(mrg[:, d, :], mrg[:, d, :], yt[:, :], ALU.add))
                if b == NBR - 1:
                    nc.vector.tensor_copy(st_m[:, 0:1], vcol("eps")).then_inc(s_mg, 1)
                    if d:
                        dve.wait_ge(s_mhi, d)
                        low(m_lo[:, d - 1, :], mrg[:, d - 1, :], m_hi[:, d - 1, :]).then_inc(s_mlo, 1)
                if b + 1 < NBR and d == 4:
                    z_low(b + 1)
            dve.wait_ge(s_mhi, KT)
            low(m_lo[:, KT - 1, :], mrg[:, KT - 1, :], m_hi[:, KT - 1, :]).then_inc(s_mlo, 1)

            own.done(stt(out=aff2[:, :], in0=mod[:, 4 * KT:5 * KT, 0], scalar=1.0, in1=vcol("g2", 0, KT),
                         op0=ALU.add, op1=ALU.mult))
            dve.wait_ge(s_x1, 16)
            for d in range(KT):
                dve.wait_ge(s_used, CK_WO + d + 1)
                stt(out=x1[:, d, :], in0=bank(2 * (d % 2), 2), scalar=mod[:, 2 * KT + d, 0:1], in1=x1[:, d, :],
                    op0=ALU.mult, op1=ALU.add).then_inc(s_woev, 1)
            dve.wait_ge(s_one2, KT)
            for half in range(2):
                mean_eps(v2[:, half * HALF:(half + 1) * HALF], bank(4 + half), D).then_inc(s_v2, 1)
            dve.wait_ge(s_v2, 2)

            def h2_low(n):
                half, k = divmod(n, KT)
                t = slice(half * HALF, (half + 1) * HALF)
                dve.wait_ge(s_h2h, n + 1)
                low_shift(h2_lo[:, k, t], ht[:, n % 4, :], mod[:, 3 * KT + k, 0:1], h2_hi[:, k, t]).then_inc(s_h2, 1)

            dve.wait_ge(s_woev, KT)
            for half in range(2):
                t = slice(half * HALF, (half + 1) * HALF)
                dve.wait_ge(s_r2, half + 1)
                refine(r2[:, t], v2[:, t], t2[:, t])
                for k in range(KT):
                    n = KT * half + k
                    if n >= 4:
                        dve.wait_ge(s_h2, n - 3)
                    stt(out=ht[:, n % 4, :], in0=x1[:, k, t], scalar=aff2[:, k:k + 1], in1=r2[:, t], op0=ALU.mult,
                        op1=ALU.mult).then_inc(s_t2, 1)
                    if n:
                        h2_low(n - 1)
            h2_low(2 * KT - 1)

            m, base = 0, CK_FFN
            for g, gn in enumerate(FGROUPS):
                for i in range(gn):
                    dve.wait_ge(s_sil, m + 1)
                    dve.wait_ge(s_used, base + 2 * i + 2)
                    if m:
                        dve.wait_ge(s_ghi, m)
                    tt(gm[:, :], bank(2, 2), sg[:, :], ALU.mult).then_inc(s_up, 1)
                    dve.wait_ge(s_up, m + 1)
                    dve.wait_ge(s_ghi, m + 1)
                    low(g_lo[:, i, :], gm[:, :], g_hi[:, i, :]).then_inc(s_glo, 1)
                    dve.wait_ge(s_glo, m + 1)
                    m += 1
                base += 2 * gn
                for d in range(KT):
                    dve.wait_ge(s_used, base + d + 1)
                    stt(out=x1[:, d, :], in0=bank(4 + 2 * (d % 2), 2), scalar=mod[:, 5 * KT + d, 0:1],
                        in1=x1[:, d, :], op0=ALU.mult, op1=ALU.add).then_inc(s_foev, 1)
                    dve.wait_ge(s_foev, KT * g + d + 1)
                base += KT


def _tiles(v):
    return np.ascontiguousarray(v.reshape(-1, P).T)


def _chunk(wt):
    k = wt.shape[0] // P
    o = np.zeros((P, 8, P), np.float32)
    o[:, :k] = wt.reshape(k, P, P).transpose(1, 0, 2)
    return o.reshape(P, CH)


def _tables():
    n = np.arange(T)
    th = 2 * np.pi * ((n[:HALF, None] * n[None, :]) % (2 * T)) / (2 * T)
    cos, sin = np.cos(th).astype(np.float32), np.sin(th).astype(np.float32)
    sin[:, 0] = 0.0
    even, odd = n[0::2], n[1::2]
    order = np.concatenate([even, odd])
    forward = [_chunk(np.concatenate([a[:, order[j * P:(j + 1) * P]] for a in (cos, sin)], 0)) for j in range(KT)]
    inverse = []
    for i in range(KH):
        t = slice(i * P, (i + 1) * P)
        inverse.append(_chunk(np.concatenate([cos[t, even].T, sin[t, odd].T], 0)))
        inverse.append(_chunk(np.concatenate([cos[t, odd].T, sin[t, even].T], 0)))
    return forward, inverse


def _chunks(w_in, w_a, w_cf, w_na, w_hy, w_o, w_fi, w_fo):
    spectrum, inverse = _tables()
    cols = lambda a, j: a[:, j * P:(j + 1) * P]
    off_a, off_q = 0, 3 * DB
    off_hy = off_q + 3 * DB
    off_cf = off_hy + 3 * DB
    off_g = off_cf + 2 * DB
    starts = [off_cf + DB * h + c * P for c in range(NB) for h in range(2)]
    starts += [off_hy + DB * h + c * P for c in range(NB) for h in range(3)]
    starts += [off_a + DB * h + c * P for c in range(NB) for h in range(3)]
    starts += [off_q + c * P for c in range(3 * NB)]
    starts += [off_g + c * P for c in range(N_G)]
    strips = [_chunk(w_in[:, s:s + P]) for s in starts]
    branch = [_chunk(np.concatenate([cols(b, 2 * m), cols(b, 2 * m + 1)], 0))
              for b in (w_a, w_cf, w_na, w_hy) for m in range(NB)]
    proj = [_chunk(cols(w_o, d)) for d in range(KT)]
    ffn, m = [], 0
    for gn in FGROUPS:
        for i in range(m, m + gn):
            ffn += [_chunk(cols(w_fi, i)), _chunk(cols(w_fi, FFT + i))]
        ffn += [_chunk(w_fo[m * P:(m + gn) * P, d * P:(d + 1) * P]) for d in range(KT)]
        m += gn
    return np.stack(spectrum + strips + spectrum + inverse + branch + proj + ffn)


def _modulation(w):
    rows = [w[kk * 2 * P:(kk + 1) * 2 * P, g * HALF:(g + 1) * HALF].reshape(2, P, HALF).transpose(1, 0, 2)
            .reshape(P, CH) for g in range(2 * D // HALF) for kk in range(KT // 2)]
    return np.stack(rows + [_chunk(w[:, j * P:(j + 1) * P]) for j in range(2 * KT, 6 * KT)])


def _filter_inputs(w1, w2, w3, w4):
    bands = 16
    t = np.linspace(0.0, 1.0, T, dtype=np.float32)[:, None]
    wv = (2.0 * np.pi * np.arange(T, dtype=np.float32)[:, None] / T).astype(np.float32)
    f = np.linspace(1e-4, bands - 1, bands, dtype=np.float32)[None, :]
    z = np.concatenate([t, np.cos(f * wv), -np.sin(f * wv)], -1).astype(np.float32)
    o = np.zeros((64, 2 * T + 192), np.float32)
    order = np.concatenate([np.arange(HALF), [HALF], np.arange(T - 1, HALF, -1)])
    o[0:33, 0:T] = z[order].T
    o[:, T:2 * T] = w4
    o[0:33, 2 * T:2 * T + 64] = w1
    o[:, 2 * T + 64:2 * T + 128] = w2
    o[:, 2 * T + 128:] = w3
    deltas = np.abs(np.linspace(np.log(1e-2) / 1.5, np.log(1e-2) / 0.3, DB, dtype=np.float32))
    win = (np.exp(-t * deltas[None, :]) + np.float32(0.05)).astype(np.float32)
    middle = np.repeat(win[HALF:HALF + 1], P, 0)
    win = win[order]
    win[HALF] = 0.0
    return o, np.ascontiguousarray(np.concatenate([win, middle]).reshape(KT + 1, P, DB).transpose(1, 0, 2))


def _bias_tables(rpb):
    q = np.arange(P)
    half, col = q // GRID, q % GRID
    padded = np.pad(rpb, ((0, 0), (2, 2), (GRID - WIN_W, GRID - WIN_W)))
    x = np.arange(XR)
    dr = x[None, :] + 1 - half[:, None]
    dc = np.arange(GRID)[None, :] - col[:, None] + GRID - 1
    table = padded[:, dr[:, :, None], dc[:, None, :]]
    mask = np.full((P, len(MASKS), NROW, GRID), NEG, np.float32)
    for n, rp in enumerate(MASKS):
        for p in range(P):
            r = 2 * rp + half[p]
            r0 = min(max(r - WIN_H // 2, 0), ROWS - WIN_H) - window_start(rp)
            c0 = min(max(col[p] - WIN_W // 2, 0), GRID - WIN_W)
            mask[p, n, r0:r0 + WIN_H, c0:c0 + WIN_W] = 0.0
    return (np.ascontiguousarray(table.reshape(HEADS, P, XR * GRID)),
            np.ascontiguousarray(mask.reshape(P, len(MASKS), LOC)))


def kernel(x, c, ctx, c_ctx, w_mod, b_mod, g_norm1, g_norm2, w_in, conv_a, w_a_out, q_gain, k_gain, rpb,
           w_na_out, conv_h, filt_w1, filt_b1, filt_w2, filt_b2, filt_w3, filt_b3, filt_w4, filt_freq,
           hy_skip, w_h_out, conv_d, conv_d_b, ln_g, ln_b, w_d_out, w_o, w_ffn_in, w_ffn_out):
    import concourse.bacc as _bacc
    from concourse.bass_utils import run_bass_kernel_spmd as _run

    a = lambda v: np.asarray(v)
    tall = lambda v: np.concatenate([a(v)[0], np.zeros(P - 64, np.float32)])[:, None]
    vec = np.concatenate([
        _tiles(a(g_norm1)[0]), _tiles(a(g_norm2)[0]), np.tile(a(q_gain)[0], 2)[:, None],
        np.tile(a(k_gain)[0], 2)[:, None], _tiles(a(conv_a)[0]), _tiles(a(conv_h)[0]), _tiles(a(hy_skip)[0]),
        _tiles(a(conv_d)[0]), _tiles(a(conv_d_b)[0]), _tiles(a(ln_g)[0]), _tiles(a(ln_b)[0]),
        _tiles(a(b_mod)[0]), np.stack([_tiles(a(c)[0]), _tiles(a(c_ctx))], -1).reshape(P, 2 * KT),
        tall(filt_b1), tall(filt_b2), tall(filt_b3), tall(filt_freq), np.full((P, 1), EPS, np.float32)], 1)
    assert vec.shape[1] == NVEC
    mats = np.zeros((P, 4, P), np.float32)
    mats[:, M_ID] = np.eye(P)
    mats[:, M_ONE] = 1.0
    mats[0:HD, M_HEAD, 0:HD] = 1.0
    mats[HD:, M_HEAD, HD:] = 1.0
    mats[:, M_REV] = np.eye(P)[::-1]
    sign = np.where(np.arange(P) % 2 == 0, 1.0, -1.0).astype(np.float32)
    filt, win = _filter_inputs(a(filt_w1)[0], a(filt_w2)[0], a(filt_w3)[0], a(filt_w4)[0])
    gat, masks = _bias_tables(a(rpb)[0])
    arrays = {
        "w": _chunks(a(w_in)[0], a(w_a_out)[0], a(w_d_out)[0], a(w_na_out)[0], a(w_h_out)[0], a(w_o)[0],
                     a(w_ffn_in)[0], a(w_ffn_out)[0]),
        "wmod": _modulation(a(w_mod)[0]),
        "xc": np.ascontiguousarray(np.concatenate([a(x)[0], a(ctx)[0]], 0).T.reshape(KT, P, TC)),
        "vec": np.ascontiguousarray(vec), "mats": mats,
        "checker": np.outer(sign, sign), "filt": filt, "win": win, "gat": gat, "masks": masks,
    }
    nc = _bacc.Bacc("TRN2", target_bir_lowering=False, num_devices=1)
    args = {n: nc.dram_tensor(f"in_{n}", v.shape, mybir.dt.from_np(v.dtype), kind="ExternalInput").ap()
            for n, v in arrays.items()}
    out = nc.dram_tensor("out", (KT, P, T), F32, kind="ExternalOutput").ap()
    layer_program(nc, **args, out=out)
    r = _run(nc, [{f"in_{n}": v for n, v in arrays.items()}], core_ids=[0])
    return np.ascontiguousarray(r.results[0]["out"].reshape(D, T).T)[None]
```
